# Optimizing a Trainium2 kernel written in Bass

```python
import jax, jax.numpy as jnp
from jax import lax
import numpy as np
import math

D_MODEL = 1024
BATCH = 1
SEQ = 512
DEPTH = 1

N_META = 16
GRID_W = 64
CHUNK = 128
Q_BLOCK = 128
EPS = 1e-6
HG_HEADS = 4
HG_K = 128
HG_V = 128
HG_KW = HG_HEADS * HG_K
HG_VW = HG_HEADS * HG_V
AT_HEADS = 8
AT_KV_HEADS = 2
AT_HD = 64
AT_GROUP = AT_HEADS // AT_KV_HEADS
AT_W = AT_HEADS * AT_HD
AT_KVW = AT_KV_HEADS * AT_HD
ROPE_THETA = 10000.0
ROPE_AXIS = AT_HD // 2
D_FF = 2816
IN_SIZES = (HG_KW, HG_VW, HG_KW, HG_KW, HG_VW, AT_W, AT_KVW, AT_KVW, D_MODEL, D_MODEL)
D_IN = sum(IN_SIZES)


def rms_norm(x, w):
    xf = x.astype(jnp.float32)
    y = xf * lax.rsqrt(jnp.mean(xf * xf, axis=-1, keepdims=True) + EPS)
    return (y * w.astype(jnp.float32)).astype(x.dtype)

def swiglu(x, w_gate, w_up, w_down):
    return (jax.nn.silu(x @ w_gate) * (x @ w_up)) @ w_down

def split_cols(z, sizes):
    outs = []
    start = 0
    for s in sizes:
        outs.append(z[..., start:start + s])
        start += s
    return outs

def axial_rope_tables(n_real):
    rows = n_real // GRID_W
    row = jnp.repeat(jnp.arange(rows, dtype=jnp.float32), GRID_W)
    col = jnp.tile(jnp.arange(GRID_W, dtype=jnp.float32), rows)
    zeros = jnp.zeros((N_META,), jnp.float32)
    row = jnp.concatenate([zeros, row])
    col = jnp.concatenate([zeros, col])
    inv = ROPE_THETA ** (-jnp.arange(0, ROPE_AXIS, 2, dtype=jnp.float32) / ROPE_AXIS)
    ang = jnp.concatenate([row[:, None] * inv, col[:, None] * inv], axis=-1)
    return jnp.cos(ang), jnp.sin(ang)

def apply_rope(x, cos, sin):
    xf = x.astype(jnp.float32).reshape(x.shape[:-1] + (AT_HD // 2, 2))
    x1, x2 = xf[..., 0], xf[..., 1]
    c = cos[None, :, None, :]
    s = sin[None, :, None, :]
    out = jnp.stack([x1 * c - x2 * s, x1 * s + x2 * c], axis=-1).reshape(x.shape)
    return out.astype(x.dtype)

def attend(qb, k, v):
    s = jnp.einsum('bkgqd,bksd->bkgqs', qb, k, preferred_element_type=jnp.float32) * (AT_HD ** -0.5)
    p = jax.nn.softmax(s, axis=-1)
    return jnp.einsum('bkgqs,bksd->bkgqd', p.astype(v.dtype), v)

def axial_gqa(zq, zk, zv, q_norm_w, k_norm_w, cos, sin):
    B, L, _ = zq.shape
    q = rms_norm(zq.reshape(B, L, AT_HEADS, AT_HD), q_norm_w)
    k = rms_norm(zk.reshape(B, L, AT_KV_HEADS, AT_HD), k_norm_w)
    v = zv.reshape(B, L, AT_KV_HEADS, AT_HD)
    q = apply_rope(q, cos, sin)
    k = apply_rope(k, cos, sin)
    q = q.transpose(0, 2, 1, 3).reshape(B, AT_KV_HEADS, AT_GROUP, L, AT_HD)
    k = k.transpose(0, 2, 1, 3)
    v = v.transpose(0, 2, 1, 3)
    n_real = L - N_META
    n_blk = n_real // Q_BLOCK
    o_meta = attend(q[:, :, :, :N_META], k, v)
    q_real = jnp.moveaxis(q[:, :, :, N_META:].reshape(B, AT_KV_HEADS, AT_GROUP, n_blk, Q_BLOCK, AT_HD), 3, 0)
    o_real = lax.map(lambda qb: attend(qb, k, v), q_real)
    o_real = jnp.moveaxis(o_real, 0, 3).reshape(B, AT_KV_HEADS, AT_GROUP, n_real, AT_HD)
    o = jnp.concatenate([o_meta, o_real], axis=3)
    return o.transpose(0, 3, 1, 2, 4).reshape(B, L, AT_W)

def gla_chunked(q, k, v, logf):
    B, T, H, K = q.shape
    n = T // CHUNK
    def to_chunks(a):
        return a.reshape(B, n, CHUNK, H, a.shape[-1]).transpose(1, 0, 3, 2, 4)
    mask = jnp.tril(jnp.ones((CHUNK, CHUNK), dtype=bool))

    def step(S, xs):
        qc, kc, vc, lc = xs
        b = jnp.cumsum(lc, axis=2)
        o_inter = jnp.einsum('bhck,bhkv->bhcv', qc * jnp.exp(b), S)
        diff = jnp.where(mask[None, None, :, :, None], b[:, :, :, None, :] - b[:, :, None, :, :], -jnp.inf)
        attn = jnp.einsum('bhtk,bhsk,bhtsk->bhts', qc, kc, jnp.exp(diff))
        o_intra = jnp.einsum('bhts,bhsv->bhtv', attn, vc)
        b_last = b[:, :, -1:, :]
        S_new = jnp.exp(b_last[:, :, 0, :])[..., None] * S + jnp.einsum('bhsk,bhsv->bhkv', kc * jnp.exp(b_last - b), vc)
        return S_new, o_inter + o_intra

    S0 = jnp.zeros((B, H, K, v.shape[-1]), jnp.float32)
    _, o = lax.scan(step, S0, (to_chunks(q), to_chunks(k), to_chunks(v), to_chunks(logf)))
    return o.transpose(1, 0, 3, 2, 4).reshape(B, T, H, v.shape[-1])

def hgrn2_bidir(zq, zi, zf_f, zf_b, zg, lb_f, lb_b, out_norm_w):
    B, L, _ = zq.shape
    q = jax.nn.silu(zq.astype(jnp.float32)).reshape(B, L, HG_HEADS, HG_K)
    v = zi.astype(jnp.float32).reshape(B, L, HG_HEADS, HG_V)

    def gates(zf, lb):
        lb = lb.reshape(HG_HEADS, HG_K)
        kk = (1.0 - lb) * jax.nn.sigmoid(-zf.astype(jnp.float32).reshape(B, L, HG_HEADS, HG_K))
        return kk, jnp.log1p(-kk)

    k_f, lf_f = gates(zf_f, lb_f)
    k_b, lf_b = gates(zf_b, lb_b)
    n_pad = CHUNK - N_META
    pad = lambda a: jnp.pad(a, ((0, 0), (n_pad, 0), (0, 0), (0, 0)))
    flip = lambda a: jnp.flip(a, axis=1)
    q_p, v_p = pad(q), pad(v)
    o_fwd = gla_chunked(q_p, pad(k_f), v_p, pad(lf_f))
    o_bwd = flip(gla_chunked(flip(q_p), flip(pad(k_b)), flip(v_p), flip(pad(lf_b))))
    o = (o_fwd + o_bwd)[:, n_pad:]
    o = o * lax.rsqrt(jnp.mean(o * o, axis=-1, keepdims=True) + EPS) * out_norm_w.astype(jnp.float32).reshape(HG_HEADS, HG_V)
    o = o.reshape(B, L, HG_VW) * jax.nn.silu(zg.astype(jnp.float32))
    return o.astype(zq.dtype)

def first_inputs(seed: int = 0) -> dict:
    key = jax.random.key(seed)
    ks = jax.random.split(key, 24)
    nrm = lambda k, shape, fan_in: jax.random.normal(k, shape, jnp.float32) * (fan_in ** -0.5)
    gain = lambda k, shape: 1.0 + 0.01 * jax.random.normal(k, shape, jnp.float32)
    return {
        'x': jax.random.normal(ks[0], (BATCH, SEQ, D_MODEL), jnp.float32),
        'meta_tokens': jax.random.normal(ks[1], (N_META, D_MODEL), jnp.float32),
        'ffn1_norm': gain(ks[2], (DEPTH, D_MODEL)),
        'ffn1_w_gate': nrm(ks[3], (DEPTH, D_MODEL, D_FF), D_MODEL),
        'ffn1_w_up': nrm(ks[4], (DEPTH, D_MODEL, D_FF), D_MODEL),
        'ffn1_w_down': nrm(ks[5], (DEPTH, D_FF, D_MODEL), D_FF),
        'mix_norm': gain(ks[6], (DEPTH, D_MODEL)),
        'w_in': nrm(ks[7], (DEPTH, D_MODEL, D_IN), D_MODEL),
        'hg_lb_fwd': 0.1 * jax.random.normal(ks[8], (DEPTH + 1, HG_KW), jnp.float32),
        'hg_lb_bwd': 0.1 * jax.random.normal(ks[9], (DEPTH + 1, HG_KW), jnp.float32),
        'hg_out_norm': gain(ks[10], (DEPTH, HG_VW)),
        'q_norm': gain(ks[11], (DEPTH, AT_HD)),
        'k_norm': gain(ks[12], (DEPTH, AT_HD)),
        'w_up_a': nrm(ks[13], (DEPTH, HG_VW, D_MODEL), HG_VW),
        'w_up_b': nrm(ks[14], (DEPTH, AT_W, D_MODEL), AT_W),
        'w_out': nrm(ks[15], (DEPTH, D_MODEL, D_MODEL), D_MODEL),
        'ffn2_norm': gain(ks[16], (DEPTH, D_MODEL)),
        'ffn2_w_gate': nrm(ks[17], (DEPTH, D_MODEL, D_FF), D_MODEL),
        'ffn2_w_up': nrm(ks[18], (DEPTH, D_MODEL, D_FF), D_MODEL),
        'ffn2_w_down': nrm(ks[19], (DEPTH, D_FF, D_MODEL), D_FF),
    }

def first_block(x, meta_tokens, ffn1_norm, ffn1_w_gate, ffn1_w_up, ffn1_w_down, mix_norm, w_in, hg_lb_fwd, hg_lb_bwd, hg_out_norm, q_norm, k_norm, w_up_a, w_up_b, w_out, ffn2_norm, ffn2_w_gate, ffn2_w_up, ffn2_w_down):
    B, n_real, _ = x.shape
    meta = jnp.broadcast_to(meta_tokens.astype(x.dtype)[None], (B, N_META, D_MODEL))
    h = jnp.concatenate([meta, x], axis=1)
    cos, sin = axial_rope_tables(n_real)
    lb_fwd_all = jnp.cumsum(jax.nn.softmax(hg_lb_fwd.astype(jnp.float32), axis=0), axis=0)
    lb_bwd_all = jnp.cumsum(jax.nn.softmax(hg_lb_bwd.astype(jnp.float32), axis=0), axis=0)
    for layer in range(DEPTH):
        h = h + 0.5 * swiglu(rms_norm(h, ffn1_norm[layer]), ffn1_w_gate[layer], ffn1_w_up[layer], ffn1_w_down[layer])
        u = rms_norm(h, mix_norm[layer])
        z = u @ w_in[layer]
        zq_a, zi_a, zf_f, zf_b, zg_a, zq_b, zk_b, zv_b, zgate_a, zgate_b = split_cols(z, IN_SIZES)
        y_a = hgrn2_bidir(zq_a, zi_a, zf_f, zf_b, zg_a, lb_fwd_all[layer], lb_bwd_all[layer], hg_out_norm[layer])
        y_b = axial_gqa(zq_b, zk_b, zv_b, q_norm[layer], k_norm[layer], cos, sin)
        mixed = jax.nn.sigmoid(zgate_a) * (y_a @ w_up_a[layer]) + jax.nn.sigmoid(zgate_b) * (y_b @ w_up_b[layer])
        h = h + mixed @ w_out[layer]
        h = h + 0.5 * swiglu(rms_norm(h, ffn2_norm[layer]), ffn2_w_gate[layer], ffn2_w_up[layer], ffn2_w_down[layer])
    return h[:, N_META:]


_first_inputs = first_inputs


def first_inputs(seed=0):
    import zlib

    import numpy as np

    out = dict(_first_inputs(seed))
    spreads = {}
    factors = {'meta_tokens': 5.446,
     'ffn1_norm': 8.0,
     'mix_norm': 8.0,
     'hg_lb_fwd': 8.0,
     'hg_lb_bwd': 8.0,
     'hg_out_norm': 8.0,
     'q_norm': 8.0,
     'k_norm': 8.0,
     'ffn2_norm': 8.0}
    for name, (base, spread) in spreads.items():
        noise = np.random.default_rng([zlib.crc32(name.encode()), seed]).standard_normal(out[name].shape)
        drawn = base * np.exp(spread * noise) if base else spread * noise
        out[name] = __import__('jax').numpy.asarray(drawn.astype(out[name].dtype))
    for name, factor in factors.items():
        out[name] = (out[name] * factor).astype(out[name].dtype)
    return out


_narrow_inputs = first_inputs


def first_inputs(seed=0):

    out = dict(_narrow_inputs(seed))
    wider = {'hg_out_norm': 6.87, 'q_norm': 5.21, 'k_norm': 5.61, 'ffn2_norm': 8.89}
    for name, times in wider.items():
        mean = out[name].mean()
        out[name] = (mean + times * (out[name] - mean)).astype(out[name].dtype)
    return out


D_MIX = D_MODEL
W_CONF = D_MIX // 4
W_POOL = D_MIX // 4
W_SCONV = D_MIX // 4
W_ATTN = D_MIX - W_CONF - W_POOL - W_SCONV
CONF_WIDTH = 31
POOL_WINDOWS = (2, 4, 8, 16)
POOL_GROUP = W_POOL // len(POOL_WINDOWS)
SCONV_WIDTH = 3
ATTN_HEAD_DIM = 64
ATTN_HEADS = W_ATTN // ATTN_HEAD_DIM
ATTN_BLOCK = 128
SPLIT_SIZES = (W_CONF, W_CONF, W_POOL, W_SCONV, W_SCONV, W_SCONV, W_ATTN, W_ATTN, W_ATTN)
D_IN_2 = sum(SPLIT_SIZES)
PEER_HEADS = 8
PEER_NKEYS = 128
PEER_EXPERTS = PEER_NKEYS * PEER_NKEYS
PEER_DKEY = 256
PEER_TOPK = 16
PEER_CHUNK = 128
DEEPNORM_ALPHA = (2 * DEPTH) ** 0.25
DEEPNORM_BETA = (8 * DEPTH) ** -0.25
LN_EPS = 1e-5


def layer_norm(x, g, b):
    xf = x.astype(jnp.float32)
    mu = jnp.mean(xf, axis=-1, keepdims=True)
    xc = xf - mu
    var = jnp.mean(xc * xc, axis=-1, keepdims=True)
    return (xc * lax.rsqrt(var + LN_EPS) * g + b).astype(x.dtype)

def depthwise_causal_conv(x, w):
    k_width, ch = w.shape
    return lax.conv_general_dilated(
        x, w[:, None, :].astype(x.dtype), window_strides=(1,), padding=[(k_width - 1, 0)],
        dimension_numbers=("NWC", "WIO", "NWC"), feature_group_count=ch)

def conformer_conv(a_val, a_gate, conv_w, conv_b, norm_g, norm_b):
    u = a_val * jax.nn.sigmoid(a_gate)
    h = depthwise_causal_conv(u, conv_w) + conv_b
    return jax.nn.silu(layer_norm(h, norm_g, norm_b))

def multiscale_pool(p, pool_w, pool_scale):
    bn, s, _ = p.shape
    groups = p.reshape(bn, s, len(POOL_WINDOWS), POOL_GROUP)
    t = jnp.arange(s)
    outs = []
    for g, win in enumerate(POOL_WINDOWS):
        xg = groups[:, :, g, :].astype(jnp.float32)
        cs = jnp.cumsum(xg, axis=1)
        prev = jnp.pad(cs, ((0, 0), (win, 0), (0, 0)))[:, :s]
        count = jnp.minimum(t + 1, win).astype(jnp.float32)
        outs.append((cs - prev) / count[None, :, None] - xg)
    pooled = jnp.stack(outs, axis=2).astype(p.dtype)
    mixed = jnp.einsum("bsgc,gce->bsge", pooled, pool_w)
    return mixed.reshape(bn, s, W_POOL) * pool_scale

def stick_breaking_attention(q, k, v):
    bn, s, _ = q.shape
    nb = s // ATTN_BLOCK

    def heads(a):
        return a.reshape(bn, s, ATTN_HEADS, ATTN_HEAD_DIM).transpose(0, 2, 1, 3)

    q, k, v = heads(q), heads(k), heads(v)
    q_blocks = q.reshape(bn, ATTN_HEADS, nb, ATTN_BLOCK, ATTN_HEAD_DIM).transpose(2, 0, 1, 3, 4)
    k_pos = jnp.arange(s)
    scale = ATTN_HEAD_DIM ** -0.5

    def block(args):
        q_blk, blk = args
        z = jnp.einsum("bhqd,bhkd->bhqk", q_blk, k).astype(jnp.float32) * scale
        q_pos = blk * ATTN_BLOCK + jnp.arange(ATTN_BLOCK)
        causal = k_pos[None, :] < q_pos[:, None]
        log_stay = jnp.where(causal, jax.nn.log_sigmoid(-z), 0.0)
        cum = jnp.cumsum(log_stay, axis=-1)
        log_w = jax.nn.log_sigmoid(z) + (cum[..., -1:] - cum)
        w = jnp.where(causal, jnp.exp(log_w), 0.0)
        return jnp.einsum("bhqk,bhkd->bhqd", w.astype(v.dtype), v)

    out = lax.map(block, (q_blocks, jnp.arange(nb)))
    return out.transpose(1, 0, 3, 2, 4).reshape(bn, s, W_ATTN)

def token_mix(x, w_in, conv_a_w, conv_a_b, norm_a_g, norm_a_b, pool_w, pool_scale, conv_c_w, w_out):
    proj = jnp.einsum("bsd,de->bse", x, w_in)
    split_points = [int(i) for i in np.cumsum(SPLIT_SIZES)[:-1]]
    a_val, a_gate, p_in, c_h, c_gate_b, c_gate_c, q, k, v = jnp.split(proj, split_points, axis=-1)
    y_a = conformer_conv(a_val, a_gate, conv_a_w, conv_a_b, norm_a_g, norm_a_b)
    y_b = multiscale_pool(p_in, pool_w, pool_scale)
    y_c = c_gate_b * depthwise_causal_conv(c_gate_c * c_h, conv_c_w)
    y_d = stick_breaking_attention(q, k, v)
    y = jnp.concatenate([y_a, y_b, y_c, y_d], axis=-1)
    return jnp.einsum("bse,ed->bsd", y, w_out)

def peer_ffn(x, wq, sub_keys, u_tab, v_tab):
    bn, s, d = x.shape
    t = bn * s
    xf = x.reshape(t, d)
    q = (xf @ wq).reshape(t, PEER_HEADS, 2, PEER_DKEY // 2)
    scores = jnp.einsum("thpc,hpnc->thpn", q, sub_keys).astype(jnp.float32)
    s_top, i_top = lax.top_k(scores, PEER_TOPK)
    cand_s = (s_top[:, :, 0, :, None] + s_top[:, :, 1, None, :]).reshape(t, PEER_HEADS, PEER_TOPK * PEER_TOPK)
    cand_i = (i_top[:, :, 0, :, None] * PEER_NKEYS + i_top[:, :, 1, None, :]).reshape(t, PEER_HEADS, PEER_TOPK * PEER_TOPK)
    best_s, best_pos = lax.top_k(cand_s, PEER_TOPK)
    expert_idx = jnp.take_along_axis(cand_i, best_pos, axis=-1)
    gates = jax.nn.softmax(best_s, axis=-1)
    n_chunks = t // PEER_CHUNK

    def chunk(args):
        xc, ec, gc = args
        u = jnp.take(u_tab, ec, axis=0)
        act = jax.nn.gelu(jnp.einsum("cd,chkd->chk", xc, u).astype(jnp.float32)) * gc
        vv = jnp.take(v_tab, ec, axis=0)
        return jnp.einsum("chk,chkd->cd", act.astype(vv.dtype), vv)

    out = lax.map(chunk, (xf.reshape(n_chunks, PEER_CHUNK, d),
                          expert_idx.reshape(n_chunks, PEER_CHUNK, PEER_HEADS, PEER_TOPK),
                          gates.reshape(n_chunks, PEER_CHUNK, PEER_HEADS, PEER_TOPK)))
    return out.reshape(bn, s, d).astype(x.dtype)

def second_inputs(seed: int = 0) -> dict:
    key = jax.random.key(seed)
    ks = jax.random.split(key, 20)
    L = DEPTH

    def nrm(k, shape, scale):
        return jax.random.normal(k, shape, jnp.float32) * scale

    return {
        "x": nrm(ks[0], (BATCH, SEQ, D_MODEL), 1.0),
        "w_in": nrm(ks[1], (L, D_MODEL, D_IN_2), D_MODEL ** -0.5),
        "conv_a_w": nrm(ks[2], (L, CONF_WIDTH, W_CONF), CONF_WIDTH ** -0.5),
        "conv_a_b": nrm(ks[3], (L, W_CONF), 0.02),
        "norm_a_g": 1.0 + nrm(ks[4], (L, W_CONF), 0.02),
        "norm_a_b": nrm(ks[5], (L, W_CONF), 0.02),
        "pool_w": nrm(ks[6], (L, len(POOL_WINDOWS), POOL_GROUP, POOL_GROUP), POOL_GROUP ** -0.5),
        "pool_scale": 1.0 + nrm(ks[7], (L, W_POOL), 0.02),
        "conv_c_w": nrm(ks[8], (L, SCONV_WIDTH, W_SCONV), SCONV_WIDTH ** -0.5),
        "w_out": nrm(ks[9], (L, D_MIX, D_MODEL), D_MIX ** -0.5 * DEEPNORM_BETA),
        "ln1_g": 1.0 + nrm(ks[10], (L, D_MODEL), 0.02),
        "ln1_b": nrm(ks[11], (L, D_MODEL), 0.02),
        "peer_wq": nrm(ks[12], (L, D_MODEL, PEER_HEADS * PEER_DKEY), D_MODEL ** -0.5),
        "peer_keys": nrm(ks[13], (L, PEER_HEADS, 2, PEER_NKEYS, PEER_DKEY // 2), (PEER_DKEY // 2) ** -0.5),
        "peer_u": nrm(ks[14], (L, PEER_EXPERTS, D_MODEL), D_MODEL ** -0.5),
        "peer_v": nrm(ks[15], (L, PEER_EXPERTS, D_MODEL), PEER_HEADS ** -0.5 * DEEPNORM_BETA),
        "ln2_g": 1.0 + nrm(ks[16], (L, D_MODEL), 0.02),
        "ln2_b": nrm(ks[17], (L, D_MODEL), 0.02),
    }

def second_block(x, w_in, conv_a_w, conv_a_b, norm_a_g, norm_a_b, pool_w, pool_scale, conv_c_w, w_out,
              ln1_g, ln1_b, peer_wq, peer_keys, peer_u, peer_v, ln2_g, ln2_b):
    for l in range(DEPTH):
        m = token_mix(x, w_in[l], conv_a_w[l], conv_a_b[l], norm_a_g[l], norm_a_b[l],
                      pool_w[l], pool_scale[l], conv_c_w[l], w_out[l])
        x = layer_norm(DEEPNORM_ALPHA * x + m, ln1_g[l], ln1_b[l])
        f = peer_ffn(x, peer_wq[l], peer_keys[l], peer_u[l], peer_v[l])
        x = layer_norm(DEEPNORM_ALPHA * x + f, ln2_g[l], ln2_b[l])
    return x


_first_inputs_2 = second_inputs


def second_inputs(seed=0):
    import zlib

    import numpy as np

    out = dict(_first_inputs_2(seed))
    spreads = {}
    factors = {'conv_a_b': 6.54,
     'norm_a_g': 8.0,
     'norm_a_b': 8.0,
     'pool_scale': 7.699,
     'ln2_g': 2.855,
     'ln2_b': 2.874}
    for name, (base, spread) in spreads.items():
        noise = np.random.default_rng([zlib.crc32(name.encode()), seed]).standard_normal(out[name].shape)
        drawn = base * np.exp(spread * noise) if base else spread * noise
        out[name] = __import__('jax').numpy.asarray(drawn.astype(out[name].dtype))
    for name, factor in factors.items():
        out[name] = (out[name] * factor).astype(out[name].dtype)
    return out


_narrow_inputs_2 = second_inputs


def second_inputs(seed=0):

    out = dict(_narrow_inputs_2(seed))
    wider = {'norm_a_g': 4.25, 'norm_a_b': 3.93, 'pool_scale': 3.59, 'ln2_g': 3.21, 'ln2_b': 3.21}
    for name, times in wider.items():
        mean = out[name].mean()
        out[name] = (mean + times * (out[name] - mean)).astype(out[name].dtype)
    return out


N_MOD = 9
GM_CHUNK = 128
GM_WIDTH = D_MODEL
GM_GROUPS = 8
GM_GROUP_DIM = GM_WIDTH // GM_GROUPS
DN_HEADS = 8
DN_HEAD_DIM = 128
DN_WIDTH = DN_HEADS * DN_HEAD_DIM
DN_CONV = 4
DN_CHUNK = 64
N_BRANCH = 2
IN_SPLITS = (GM_WIDTH, GM_WIDTH, DN_WIDTH, DN_WIDTH, DN_WIDTH, DN_WIDTH,
             DN_HEADS, DN_HEADS, N_BRANCH * D_MODEL)
IN_WIDTH = sum(IN_SPLITS)
IN_OFFSETS = tuple(int(o) for o in np.cumsum(IN_SPLITS)[:-1])


def rms_norm_3(x, g):
    xf = x.astype(jnp.float32)
    y = xf * lax.rsqrt(jnp.mean(xf * xf, axis=-1, keepdims=True) + EPS)
    return (y * g.astype(jnp.float32)).astype(x.dtype)

def layer_norm_3(x, g, b):
    xf = x.astype(jnp.float32)
    mu = jnp.mean(xf, axis=-1, keepdims=True)
    var = jnp.mean(jnp.square(xf - mu), axis=-1, keepdims=True)
    y = (xf - mu) * lax.rsqrt(var + EPS)
    return (y * g.astype(jnp.float32) + b.astype(jnp.float32)).astype(x.dtype)

def modulate(h, shift, scale):
    return h * (1.0 + scale[:, None, :]) + shift[:, None, :]

def swiglu_3(h, w_in, w_out):
    a, b = jnp.split(h @ w_in, 2, axis=-1)
    return (jax.nn.silu(a) * b) @ w_out

def l2_normalize(x):
    return x * lax.rsqrt(jnp.sum(x * x, axis=-1, keepdims=True) + EPS)

def causal_depthwise_conv(x, w):
    ch = x.shape[-1]
    return lax.conv_general_dilated(
        x, w[:, None, :].astype(x.dtype), window_strides=(1,),
        padding=[(DN_CONV - 1, 0)], dimension_numbers=('NWC', 'WIO', 'NWC'),
        feature_group_count=ch)

def chunked_spatial_gating(u, v, ln_g, ln_b, w_s, b_s):
    bsz, seq, _ = v.shape
    v = layer_norm_3(v, ln_g, ln_b)
    vc = v.reshape(bsz, seq // GM_CHUNK, GM_CHUNK, GM_GROUPS, GM_GROUP_DIM)
    causal = jnp.tril(jnp.ones((GM_CHUNK, GM_CHUNK), dtype=bool))
    w = jnp.where(causal, w_s, 0.0).astype(v.dtype)
    mixed = jnp.einsum('gts,bnsgc->bntgc', w, vc) + b_s.T[:, :, None]
    return u * mixed.reshape(bsz, seq, GM_WIDTH)

def chunk_gated_delta_rule(q, k, v, g, beta):
    bsz, seq, nh, dk = q.shape
    dv = v.shape[-1]
    C = DN_CHUNK
    n_chunks = seq // C

    def chunks(t):
        return t.reshape(bsz, n_chunks, C, nh, t.shape[-1]).transpose(1, 0, 3, 2, 4)

    q, k, v = chunks(q), chunks(k), chunks(v)
    g = chunks(g[..., None])[..., 0]
    beta = chunks(beta[..., None])
    g_cum = jnp.cumsum(g, axis=-1)
    causal = jnp.tril(jnp.ones((C, C), dtype=bool))
    strict = jnp.tril(jnp.ones((C, C), dtype=bool), -1)
    decay = jnp.exp(jnp.where(causal, g_cum[..., :, None] - g_cum[..., None, :], -jnp.inf))
    k_beta = k * beta
    a_low = jnp.where(strict, jnp.einsum('nbhcd,nbhed->nbhce', k_beta, k) * decay, 0.0)
    tri = a_low + jnp.eye(C, dtype=q.dtype)
    rhs = jnp.concatenate([v * beta, k_beta * jnp.exp(g_cum)[..., None]], axis=-1)
    sol = lax.linalg.triangular_solve(tri, rhs, left_side=True, lower=True, unit_diagonal=True)
    u, w = sol[..., :dv], sol[..., dv:]
    qk = jnp.einsum('nbhcd,nbhed->nbhce', q, k) * decay
    q_dec = q * jnp.exp(g_cum)[..., None]
    k_dec = k * jnp.exp(g_cum[..., -1:] - g_cum)[..., None]
    g_last = jnp.exp(g_cum[..., -1])[..., None, None]

    def step(state, xs):
        u_n, w_n, qk_n, qd_n, kd_n, gl_n = xs
        v_new = u_n - jnp.einsum('bhck,bhkv->bhcv', w_n, state)
        o_n = (jnp.einsum('bhck,bhkv->bhcv', qd_n, state)
               + jnp.einsum('bhce,bhev->bhcv', qk_n, v_new))
        state = state * gl_n + jnp.einsum('bhck,bhcv->bhkv', kd_n, v_new)
        return state, o_n

    state0 = jnp.zeros((bsz, nh, dk, dv), q.dtype)
    _, o = lax.scan(step, state0, (u, w, qk, q_dec, k_dec, g_last))
    return o.transpose(1, 0, 3, 2, 4).reshape(bsz, seq, nh, dv)

def gated_deltanet(q, k, v, z, a, b, conv_w, a_log, dt_bias, norm_g):
    bsz, seq, _ = q.shape
    f32 = jnp.float32
    qkv = jax.nn.silu(causal_depthwise_conv(jnp.concatenate([q, k, v], axis=-1), conv_w))
    q, k, v = jnp.split(qkv, 3, axis=-1)
    shp = (bsz, seq, DN_HEADS, DN_HEAD_DIM)
    q = l2_normalize(q.reshape(shp).astype(f32)) * (DN_HEAD_DIM ** -0.5)
    k = l2_normalize(k.reshape(shp).astype(f32))
    v = v.reshape(shp).astype(f32)
    beta = jax.nn.sigmoid(b.astype(f32))
    g = -jnp.exp(a_log.astype(f32)) * jax.nn.softplus(a.astype(f32) + dt_bias.astype(f32))
    o = chunk_gated_delta_rule(q, k, v, g, beta)
    o = o * lax.rsqrt(jnp.mean(o * o, axis=-1, keepdims=True) + EPS) * norm_g.astype(f32)
    o = o * jax.nn.silu(z.reshape(shp).astype(f32))
    return o.reshape(bsz, seq, DN_WIDTH).astype(z.dtype)

def third_inputs(seed: int = 0) -> dict:
    key = jax.random.key(seed)
    ks = iter(jax.random.split(key, 32))
    f32 = jnp.float32

    def nrm(shape, fan_in, gain=1.0):
        return jax.random.normal(next(ks), shape, f32) * (gain * fan_in ** -0.5)

    def gain_vec(shape):
        return 1.0 + 0.02 * jax.random.normal(next(ks), shape, f32)

    L = DEPTH
    x = jax.random.normal(next(ks), (BATCH, SEQ, D_MODEL), f32)
    c = jax.random.normal(next(ks), (BATCH, D_MODEL), f32)
    w_ada = nrm((L, D_MODEL, N_MOD * D_MODEL), D_MODEL, 0.5)
    b_ada = 0.01 * jax.random.normal(next(ks), (L, N_MOD * D_MODEL), f32)
    norm1_g = gain_vec((L, D_MODEL))
    ffn1_w_in = nrm((L, D_MODEL, 2 * D_FF), D_MODEL)
    ffn1_w_out = nrm((L, D_FF, D_MODEL), D_FF)
    norm2_g = gain_vec((L, D_MODEL))
    w_in = nrm((L, D_MODEL, IN_WIDTH), D_MODEL)
    conv_w = nrm((L, DN_CONV, 3 * DN_WIDTH), DN_CONV)
    a_log = jnp.log(jax.random.uniform(next(ks), (L, DN_HEADS), f32, 1.0, 16.0))
    dt = jnp.exp(jax.random.uniform(next(ks), (L, DN_HEADS), f32,
                                    math.log(1e-3), math.log(1e-1)))
    dt_bias = dt + jnp.log(-jnp.expm1(-dt))
    dn_norm_g = gain_vec((L, DN_HEAD_DIM))
    gm_ln_g = gain_vec((L, GM_WIDTH))
    gm_ln_b = 0.01 * jax.random.normal(next(ks), (L, GM_WIDTH), f32)
    gm_w_s = nrm((L, GM_GROUPS, GM_CHUNK, GM_CHUNK), GM_CHUNK)
    gm_b_s = 1.0 + 0.02 * jax.random.normal(next(ks), (L, GM_GROUPS, GM_CHUNK), f32)
    w_branch = nrm((L, N_BRANCH, GM_WIDTH, D_MODEL), GM_WIDTH)
    w_out = nrm((L, D_MODEL, D_MODEL), D_MODEL)
    norm3_g = gain_vec((L, D_MODEL))
    ffn2_w_in = nrm((L, D_MODEL, 2 * D_FF), D_MODEL)
    ffn2_w_out = nrm((L, D_FF, D_MODEL), D_FF)
    final_g = gain_vec((D_MODEL,))
    return {"x": x, "c": c, "w_ada": w_ada, "b_ada": b_ada,
            "norm1_g": norm1_g, "ffn1_w_in": ffn1_w_in, "ffn1_w_out": ffn1_w_out,
            "norm2_g": norm2_g, "w_in": w_in, "conv_w": conv_w, "a_log": a_log,
            "dt_bias": dt_bias, "dn_norm_g": dn_norm_g, "gm_ln_g": gm_ln_g,
            "gm_ln_b": gm_ln_b, "gm_w_s": gm_w_s, "gm_b_s": gm_b_s,
            "w_branch": w_branch, "w_out": w_out, "norm3_g": norm3_g,
            "ffn2_w_in": ffn2_w_in, "ffn2_w_out": ffn2_w_out, "final_g": final_g}

def third_block(x, c, w_ada, b_ada, norm1_g, ffn1_w_in, ffn1_w_out, norm2_g, w_in, conv_w,
              a_log, dt_bias, dn_norm_g, gm_ln_g, gm_ln_b, gm_w_s, gm_b_s, w_branch,
              w_out, norm3_g, ffn2_w_in, ffn2_w_out, final_g):
    c_act = jax.nn.silu(c)
    for l in range(DEPTH):
        mod = c_act @ w_ada[l] + b_ada[l]
        sh1, sc1, ga1, sh2, sc2, ga2, sh3, sc3, ga3 = jnp.split(mod, N_MOD, axis=-1)

        h = modulate(rms_norm_3(x, norm1_g[l]), sh1, sc1)
        x = x + 0.5 * ga1[:, None, :] * swiglu_3(h, ffn1_w_in[l], ffn1_w_out[l])

        h = modulate(rms_norm_3(x, norm2_g[l]), sh2, sc2)
        proj = h @ w_in[l]
        u_a, v_a, q_b, k_b, v_b, z_b, a_b, b_b, gate_logits = jnp.split(proj, IN_OFFSETS, axis=-1)
        u_a = jax.nn.gelu(u_a, approximate=False)
        v_a = jax.nn.gelu(v_a, approximate=False)
        o_a = chunked_spatial_gating(u_a, v_a, gm_ln_g[l], gm_ln_b[l], gm_w_s[l], gm_b_s[l])
        o_b = gated_deltanet(q_b, k_b, v_b, z_b, a_b, b_b, conv_w[l], a_log[l],
                             dt_bias[l], dn_norm_g[l])
        g_a, g_b = jnp.split(jax.nn.sigmoid(gate_logits), N_BRANCH, axis=-1)
        merged = g_a * (o_a @ w_branch[l, 0]) + g_b * (o_b @ w_branch[l, 1])
        x = x + ga2[:, None, :] * (merged @ w_out[l])

        h = modulate(rms_norm_3(x, norm3_g[l]), sh3, sc3)
        x = x + 0.5 * ga3[:, None, :] * swiglu_3(h, ffn2_w_in[l], ffn2_w_out[l])
    return rms_norm_3(x, final_g)


_first_inputs_3 = third_inputs


def third_inputs(seed=0):
    import zlib

    import numpy as np

    out = dict(_first_inputs_3(seed))
    spreads = {}
    factors = {'b_ada': 6.306,
     'norm1_g': 8.0,
     'norm2_g': 8.0,
     'a_log': 4.805,
     'dn_norm_g': 42.477,
     'gm_ln_g': 50.239,
     'gm_ln_b': 64.0,
     'gm_b_s': 35.894,
     'norm3_g': 40.565,
     'final_g': 7.841}
    for name, (base, spread) in spreads.items():
        noise = np.random.default_rng([zlib.crc32(name.encode()), seed]).standard_normal(out[name].shape)
        drawn = base * np.exp(spread * noise) if base else spread * noise
        out[name] = __import__('jax').numpy.asarray(drawn.astype(out[name].dtype))
    for name, factor in factors.items():
        out[name] = (out[name] * factor).astype(out[name].dtype)
    return out


_narrow_inputs_3 = third_inputs


def third_inputs(seed=0):

    out = dict(_narrow_inputs_3(seed))
    wider = {'dn_norm_g': 4.14, 'gm_ln_g': 4.24, 'gm_ln_b': 6.92, 'gm_b_s': 4.11, 'final_g': 3.17}
    for name, times in wider.items():
        mean = out[name].mean()
        out[name] = (mean + times * (out[name] - mean)).astype(out[name].dtype)
    return out


def setup_inputs(seed=0):
    out = dict(first_inputs(seed))
    for name, value in second_inputs(seed + 1).items():
        if name != "x":
            out[name + "_2"] = value
    for name, value in third_inputs(seed + 2).items():
        if name != "x":
            out[name + "_3"] = value
    return out


def reference(
    x, meta_tokens, ffn1_norm, ffn1_w_gate, ffn1_w_up, ffn1_w_down, mix_norm, w_in, hg_lb_fwd,
    hg_lb_bwd, hg_out_norm, q_norm, k_norm, w_up_a, w_up_b, w_out, ffn2_norm, ffn2_w_gate,
    ffn2_w_up, ffn2_w_down, w_in_2, conv_a_w_2, conv_a_b_2, norm_a_g_2, norm_a_b_2, pool_w_2,
    pool_scale_2, conv_c_w_2, w_out_2, ln1_g_2, ln1_b_2, peer_wq_2, peer_keys_2, peer_u_2,
    peer_v_2, ln2_g_2, ln2_b_2, c_3, w_ada_3, b_ada_3, norm1_g_3, ffn1_w_in_3, ffn1_w_out_3,
    norm2_g_3, w_in_3, conv_w_3, a_log_3, dt_bias_3, dn_norm_g_3, gm_ln_g_3, gm_ln_b_3,
    gm_w_s_3, gm_b_s_3, w_branch_3, w_out_3, norm3_g_3, ffn2_w_in_3, ffn2_w_out_3, final_g_3,
):
    x = first_block(
        x, meta_tokens, ffn1_norm, ffn1_w_gate, ffn1_w_up, ffn1_w_down, mix_norm, w_in,
        hg_lb_fwd, hg_lb_bwd, hg_out_norm, q_norm, k_norm, w_up_a, w_up_b, w_out, ffn2_norm,
        ffn2_w_gate, ffn2_w_up, ffn2_w_down,
    )
    x = second_block(
        x, w_in_2, conv_a_w_2, conv_a_b_2, norm_a_g_2, norm_a_b_2, pool_w_2, pool_scale_2,
        conv_c_w_2, w_out_2, ln1_g_2, ln1_b_2, peer_wq_2, peer_keys_2, peer_u_2, peer_v_2,
        ln2_g_2, ln2_b_2,
    )
    return third_block(
        x, c_3, w_ada_3, b_ada_3, norm1_g_3, ffn1_w_in_3, ffn1_w_out_3, norm2_g_3, w_in_3,
        conv_w_3, a_log_3, dt_bias_3, dn_norm_g_3, gm_ln_g_3, gm_ln_b_3, gm_w_s_3, gm_b_s_3,
        w_branch_3, w_out_3, norm3_g_3, ffn2_w_in_3, ffn2_w_out_3, final_g_3,
    )


_drawn_inputs = setup_inputs


def setup_inputs(seed=0):
    import zlib

    import numpy as np

    out = dict(_drawn_inputs(seed))
    spreads = {}
    factors = {'conv_a_w_2': 69.798,
     'conv_a_b_2': 200.0,
     'norm_a_g_2': 180.51,
     'norm_a_b_2': 200.0,
     'pool_scale_2': 18.86}
    for name, (base, spread) in spreads.items():
        noise = np.random.default_rng([zlib.crc32(name.encode()), seed]).standard_normal(out[name].shape)
        drawn = base * np.exp(spread * noise) if base else spread * noise
        out[name] = __import__('jax').numpy.asarray(drawn.astype(out[name].dtype))
    for name, factor in factors.items():
        out[name] = (out[name] * factor).astype(out[name].dtype)
    return out
```

```python
from contextlib import ExitStack

import numpy as np
import concourse.bass as bass
from concourse import mybir

P = 128
F32 = mybir.dt.float32
U32 = mybir.dt.uint32
I32 = mybir.dt.int32
ALU = mybir.AluOpType
ACT = mybir.ActivationFunctionType
AX_X = mybir.AxisListType.X

D = 1024
DC = D // P
SEQ = 512
META = 16
L = SEQ + META
FF = 2816
FC = FF // P
EPS = 1e-6
LN_EPS = 1e-5
BANK = 512
DEEP_ALPHA = 2.0 ** 0.25


class Phase:

    def __init__(self, nc, name):
        self.nc, self.name, self.ctx, self.sems = nc, name, ExitStack(), []

    def __enter__(self):
        return self

    def __exit__(self, *error):
        if self.sems and error[0] is None:
            for s in self.sems:
                self.nc.gpsimd.sem_clear(s)
                self.nc.release_semaphore(s)
        return self.ctx.__exit__(*error)

    def sb(self, name, shape, dt=F32):
        return self.ctx.enter_context(self.nc.sbuf_tensor(f"{self.name}_{name}", shape, dt))

    def ps(self, name, shape, dt=F32):
        return self.ctx.enter_context(self.nc.psum_tensor(f"{self.name}_{name}", shape, dt))

    def sem(self, name):
        self.sems.append(self.nc.alloc_semaphore(name=f"{self.name}_{name}"))
        return self.sems[-1]


def halves(T):
    n = -(-T // BANK)
    return n, T // n


def pieces(ps, T):
    n, w = halves(T)
    return ps[:, 0:n, 0:w]


def cut(x, T):
    n, w = halves(T)
    return x.rearrange("p (n w) -> p n w", n=n)


def over_steps(eng, steps, unroll, body):
    for s in range(min(unroll, steps)):
        body(s, s, True)
    rounds = steps // unroll
    if rounds > 1:
        with eng.Fori(1, rounds) as i:
            for s in range(unroll):
                body(i * unroll + s, s, False)
    for s in range(rounds * unroll, steps):
        if s >= unroll:
            body(s, s % unroll, False)


SLOTS = 2


def products(nc, ph, block, T, legs, steps):
    n, w = halves(T)
    ring = [[ph.sb(f"w{l}_{s}", [P, x.shape[1] * P]) for s in range(SLOTS)] for l, (_, x) in enumerate(legs)]
    out = [[ph.ps(f"o{l}_{s}", [P, n, BANK]) for s in range(SLOTS)] for l in range(len(legs))]
    weights_in = [[ph.sem(f"weights_in{l}_{s}") for s in range(SLOTS)] for l in range(len(legs))]
    products_done = ph.sem("products_done")
    results_read = ph.sem("results_read")

    @block.sync
    def _(sp):
        def load(m, s, first):
            if not first:
                sp.wait_ge(products_done, m - SLOTS + 1)
            for l, (weights, _) in enumerate(legs):
                sp.dma_start(ring[l][s][:, :], weights[m]).then_inc(weights_in[l][s], 16)

        over_steps(sp, steps, SLOTS, load)

    @block.tensor
    def _(pe):
        def step(m, s, first):
            if not first:
                pe.wait_ge(results_read, m - SLOTS + 1)
            for l, (_, x) in enumerate(legs):
                if isinstance(m, int):
                    pe.wait_ge(weights_in[l][s], 16 * (m // SLOTS + 1))
                else:
                    pe.wait_ge(weights_in[l][s], (m - s) * (16 // SLOTS) + 16)
                kc = x.shape[1]
                for j in range(n):
                    for k in range(kc):
                        mm = pe.matmul(out[l][s][:, j, 0:w], ring[l][s][:, k * P:(k + 1) * P],
                                       x[:, k, j * w:(j + 1) * w], start=(k == 0), stop=(k == kc - 1))
            mm.then_inc(products_done, 1)

        over_steps(pe, steps, SLOTS, step)

    return out, products_done, results_read


def project(nc, name, T, x, weights, steps, dst, scale=1.0, residual=False, column=None):
    with Phase(nc, name) as ph, nc.Block() as block:
        out, products_done, results_read = products(nc, ph, block, T, [(weights, x)], steps)

        @block.vector
        def _(dve):
            def take(m, s, first):
                dve.wait_ge(products_done, m + 1)
                to = cut(dst[:, m, :], T)
                factor = scale if column is None else column[:, m, :]
                if residual:
                    dve.scalar_tensor_tensor(out=to, in0=pieces(out[0][s], T), scalar=factor, in1=to,
                                             op0=ALU.mult, op1=ALU.add).then_inc(results_read, 1)
                else:
                    dve.tensor_scalar(to, pieces(out[0][s], T), factor, None,
                                      ALU.mult).then_inc(results_read, 1)

            over_steps(dve, steps, SLOTS, take)


def gated_up(nc, name, T, x, w_gate, w_up, steps, hidden):
    with Phase(nc, name) as ph, nc.Block() as block:
        out, products_done, results_read = products(nc, ph, block, T, [(w_gate, x), (w_up, x)], steps)
        gate = [ph.sb(f"gate{s}", [P, T]) for s in range(SLOTS)]
        gate_ready = ph.sem("gate_ready")

        @block.scalar
        def _(act):
            def silu(m, s, first):
                act.wait_ge(products_done, m + 1)
                act.activation(cut(gate[s][:, :], T), pieces(out[0][s], T), ACT.Silu).then_inc(gate_ready, 1)

            over_steps(act, steps, SLOTS, silu)

        @block.vector
        def _(dve):
            def times(m, s, first):
                dve.wait_ge(gate_ready, m + 1)
                dve.tensor_tensor(cut(hidden[:, m, :], T), pieces(out[1][s], T), cut(gate[s][:, :], T),
                                  ALU.mult).then_inc(results_read, 1)

            over_steps(dve, steps, SLOTS, times)


def merge(nc, name, T, xa, wa, ga, xb, wb, gb, steps, dst):
    with Phase(nc, name) as ph, nc.Block() as block:
        out, products_done, results_read = products(nc, ph, block, T, [(wa, xa), (wb, xb)], steps)
        part = [ph.sb(f"part{i}", [P, T]) for i in range(2)]

        @block.vector
        def _(dve):
            def add(m, s, first):
                dve.wait_ge(products_done, m + 1)
                dve.tensor_tensor(cut(part[0][:, :], T), pieces(out[0][s], T), cut(ga[:, m, :], T), ALU.mult)
                dve.tensor_tensor(cut(part[1][:, :], T), pieces(out[1][s], T), cut(gb[:, m, :], T), ALU.mult)
                dve.drain()
                dve.tensor_tensor(dst[:, m, :], part[0][:, :], part[1][:, :], ALU.add).then_inc(results_read, 1)
                dve.drain()

            over_steps(dve, steps, SLOTS, add)


def rms_norm(nc, name, T, ones, x, dst, gain, shift=None, eps=EPS):
    n, w = halves(T)
    chunks = x.shape[1]
    with Phase(nc, name) as ph, nc.Block() as block:
        root = ph.sb("root", [P, T])
        total = ph.ps("total", [P, n, BANK])
        squares_ready, total_ready = ph.sem("squares_ready"), ph.sem("total_ready")
        mean_ready, root_ready = ph.sem("mean_ready"), ph.sem("root_ready")

        @block.scalar
        def _(act):
            for c in range(chunks):
                act.activation(dst[:, c, :], x[:, c, :], ACT.Square).then_inc(squares_ready, 1)
            act.wait_ge(mean_ready, 1)
            act.activation(root[:, :], root[:, :], ACT.Sqrt).then_inc(root_ready, 1)

        @block.tensor
        def _(pe):
            for c in range(chunks):
                pe.wait_ge(squares_ready, c + 1)
                for j in range(n):
                    mm = pe.matmul(total[:, j, 0:w], ones[:, :], dst[:, c, j * w:(j + 1) * w],
                                   start=(c == 0), stop=(c == chunks - 1))
            mm.then_inc(total_ready, 1)

        @block.vector
        def _(dve):
            dve.wait_ge(total_ready, 1)
            dve.tensor_scalar(cut(root[:, :], T), pieces(total, T), 1.0 / (chunks * P), eps,
                              ALU.mult, ALU.add).then_inc(mean_ready, 1)
            dve.wait_ge(root_ready, 1)
            dve.reciprocal(root[:, :], root[:, :])
            dve.drain()
            for c in range(chunks):
                dve.scalar_tensor_tensor(out=dst[:, c, :], in0=x[:, c, :], scalar=gain[:, c:c + 1],
                                         in1=root[:, :], op0=ALU.mult, op1=ALU.mult)
            if shift is not None:
                dve.drain()
                for c in range(chunks):
                    dve.tensor_scalar(dst[:, c, :], dst[:, c, :], shift[:, c:c + 1], None, ALU.add)
            dve.drain()


def layer_norm(nc, name, T, ones, x, dst, gain, shift, eps, silu=False):
    chunks = x.shape[1]
    with Phase(nc, name) as ph, nc.Block() as block:
        root = ph.sb("root", [P, T])
        mean = ph.sb("mean", [P, T])
        total = ph.ps("total", [P, 2, BANK])
        mean_ready, centred, squares_ready = ph.sem("mean_ready"), ph.sem("centred"), ph.sem("squares_ready")
        total_ready, root_ready, scaled = ph.sem("total_ready"), ph.sem("root_ready"), ph.sem("scaled")

        @block.tensor
        def _(pe):
            for c in range(chunks):
                mm = pe.matmul(total[:, 0, 0:T], ones[:, :], x[:, c, :], start=(c == 0), stop=(c == chunks - 1))
            mm.then_inc(total_ready, 1)
            for c in range(chunks):
                pe.wait_ge(squares_ready, c + 1)
                mm = pe.matmul(total[:, 1, 0:T], ones[:, :], dst[:, c, :], start=(c == 0), stop=(c == chunks - 1))
            mm.then_inc(total_ready, 1)

        @block.scalar
        def _(act):
            for c in range(chunks):
                act.wait_ge(centred, c + 1)
                act.activation(dst[:, c, :], x[:, c, :], ACT.Square).then_inc(squares_ready, 1)
            act.wait_ge(mean_ready, 1)
            act.activation(root[:, :], root[:, :], ACT.Sqrt).then_inc(root_ready, 1)
            if silu:
                for c in range(chunks):
                    act.wait_ge(scaled, c + 1)
                    act.activation(dst[:, c, :], dst[:, c, :], ACT.Silu)

        @block.vector
        def _(dve):
            dve.wait_ge(total_ready, 1)
            dve.tensor_scalar(mean[:, :], total[:, 0, 0:T], 1.0 / (chunks * P), None, ALU.mult)
            dve.drain()
            for c in range(chunks):
                dve.tensor_tensor(x[:, c, :], x[:, c, :], mean[:, :], ALU.subtract).then_inc(centred, 1)
            dve.wait_ge(total_ready, 2)
            dve.tensor_scalar(root[:, :], total[:, 1, 0:T], 1.0 / (chunks * P), eps,
                              ALU.mult, ALU.add).then_inc(mean_ready, 1)
            dve.wait_ge(root_ready, 1)
            dve.reciprocal(root[:, :], root[:, :])
            dve.drain()
            for c in range(chunks):
                dve.scalar_tensor_tensor(out=dst[:, c, :], in0=x[:, c, :], scalar=gain[:, c:c + 1],
                                         in1=root[:, :], op0=ALU.mult, op1=ALU.mult)
            dve.drain()
            for c in range(chunks):
                dve.tensor_scalar(dst[:, c, :], dst[:, c, :], shift[:, c:c + 1], None, ALU.add).then_inc(scaled, 1)
            dve.drain()


def load(nc, ph, name, sources):
    there = {k: ph.sb(k, list(v.shape), v.dtype) for k, v in sources.items()}
    with Phase(nc, name) as p, nc.Block() as block:
        loaded = p.sem("loaded")

        @block.sync
        def _(sp):
            for k, v in sources.items():
                sp.dma_start(there[k][:], v).then_inc(loaded, 16)
            sp.wait_ge(loaded, 16 * len(sources))

    return there
HG = 4
CH = 128
NCH = 5
LP = NCH * CH
PADN = LP - L
AT_T = 88
AT_N = L // AT_T
AT_HEADS = 8
HD = 64
Z_Q, Z_I, Z_FF, Z_FB, Z_G, Z_END = 0, 4, 8, 12, 16, 20
A_Q, A_K, A_V, A_END = 0, 4, 6, 7
Z_GATES = Z_END + A_END


def hgrn(nc, V, C, z, y):
    W = HG * LP
    with Phase(nc, "hg") as ph:
        q, va, kf, kb = (z[:, c:c + HG, :].rearrange("p h t -> p (h t)") for c in (Z_Q, Z_I, Z_FF, Z_FB))
        lf, bsum = ph.sb("lf", [P, W]), ph.sb("bsum", [P, W])
        qe, ke = ph.sb("qe", [P, W]), ph.sb("ke", [P, W])
        vt = ph.sb("vt", [P, HG * NCH, P])
        attn = ph.sb("attn", [P, HG * NCH, P])
        state = ph.sb("state", [P, HG, P])
        decay = ph.sb("decay", [P, HG * NCH])
        lb = ph.sb("lb", [P, 2, HG])
        reset = ph.sb("reset", [P, LP])
        levels = [64, 32, 16, 8, 4, 2, 1]

        def tok(a):
            return a[:, :].rearrange("p (h t) -> p h t", h=HG)

        with Phase(nc, "hg_in") as p1, nc.Block() as block:
            edge = p1.sb("edge", [P, 4, HG])
            tr = p1.ps("tr", [P, 2, 4, P])
            padded, e_ready, s_ready, v_ready = p1.sem("padded"), p1.sem("e_ready"), p1.sem("s_ready"), p1.sem("v_ready")
            transposed, copied = p1.sem("transposed"), p1.sem("copied")
            top = p1.sb("top", [P, 2, HG])

            @block.scalar
            def _(act):
                act.wait_ge(e_ready, 1)
                act.activation(edge[:, :, :], edge[:, :, :], ACT.Exp).then_inc(s_ready, 1)
                act.activation(tok(kf)[:, :, PADN:], tok(kf)[:, :, PADN:], ACT.Sigmoid, scale=-1.0).then_inc(s_ready, 1)
                act.activation(tok(kb)[:, :, PADN:], tok(kb)[:, :, PADN:], ACT.Sigmoid, scale=-1.0).then_inc(s_ready, 1)
                act.activation(tok(q)[:, :, PADN:], tok(q)[:, :, PADN:], ACT.Silu)
                act.activation(z[:, Z_G:Z_G + HG, PADN:], z[:, Z_G:Z_G + HG, PADN:], ACT.Silu)
                act.drain()

            @block.vector
            def _(dve):
                for a in (kf, kb, q, va):
                    dve.memset(tok(a)[:, :, 0:PADN], 0.0)
                dve.memset(reset[:, :], 1.0)
                dve.memset(qe[:, :], 0.0)
                dve.memset(ke[:, :], 0.0)
                dve.drain()
                dve.memset(reset[:, :].rearrange("p (n t) -> p n t", t=CH)[:, :, 0:1], 0.0).then_inc(v_ready, 1)
                for d in range(2):
                    dve.tensor_tensor(top[:, d, :], V["lb"][:, 8 * d:8 * d + 4], V["lb"][:, 8 * d + 4:8 * d + 8], ALU.max)
                dve.drain()
                for d in range(2):
                    for r in range(2):
                        dve.tensor_tensor(edge[:, 2 * d + r, :], V["lb"][:, 8 * d + 4 * r:8 * d + 4 * r + 4],
                                          top[:, d, :], ALU.subtract)
                dve.drain()
                dve.nop().then_inc(e_ready, 1)
                dve.wait_ge(s_ready, 1)
                for d in range(2):
                    dve.tensor_tensor(top[:, d, :], edge[:, 2 * d, :], edge[:, 2 * d + 1, :], ALU.add)
                dve.drain()
                dve.reciprocal(top[:, :, :], top[:, :, :])
                dve.drain()
                for d in range(2):
                    dve.tensor_tensor(lb[:, d, :], edge[:, 2 * d, :], top[:, d, :], ALU.mult)
                dve.drain()
                dve.tensor_scalar(lb[:, :, :], lb[:, :, :], -1.0, 1.0, ALU.mult, ALU.add)
                dve.drain()
                for d, k in enumerate((kf, kb)):
                    dve.wait_ge(s_ready, 2 + d)
                    for h in range(HG):
                        dve.tensor_scalar(tok(k)[:, h, PADN:], tok(k)[:, h, PADN:], lb[:, d, h:h + 1], None, ALU.mult)
                for g in range(HG * NCH // 4):
                    dve.wait_ge(transposed, g + 1)
                    dve.tensor_copy(vt[:, 4 * g:4 * g + 4, :], tr[:, g % 2, :, :]).then_inc(copied, 1)
                dve.drain()

            @block.tensor
            def _(pe):
                pe.wait_ge(v_ready, 1)
                for g in range(HG * NCH // 4):
                    if g >= 2:
                        pe.wait_ge(copied, g - 1)
                    for i in range(4):
                        n = 4 * g + i
                        mm = pe.transpose(tr[:, g % 2, i, :], va[:, n * CH:(n + 1) * CH], C["ident"][:, :])
                    mm.then_inc(transposed, 1)

        def sequence(direction):
            k = kf if direction == 0 else kb
            with Phase(nc, f"hg_b{direction}") as p2, nc.Block() as block:
                key_ready, log_ready = p2.sem("key_ready"), p2.sem("log_ready")

                @block.scalar
                def _(act):
                    act.activation(lf[:, :], k[:, :], ACT.Ln, bias=1.0, scale=-1.0).then_inc(log_ready, 1)

                @block.vector
                def _(dve):
                    dve.wait_ge(log_ready, 1)
                    for h in range(HG):
                        row = slice(h * LP, (h + 1) * LP)
                        dve.tensor_tensor_scan(bsum[:, row], reset[:, :], lf[:, row], 0.0, ALU.mult, ALU.add)
                    dve.drain()
                    if direction == 1:
                        dve.tensor_tensor(lf[:, :], bsum[:, :], lf[:, :], ALU.subtract)
                        dve.drain()

            todo = [0] + levels if direction == 0 else levels
            with Phase(nc, f"hg_l{direction}") as p3, nc.Block() as block:
                sc = p3.ps("sc", [P, 5, 4, P])
                arg = [p3.sb(f"arg{i}", [P, W // 2]) for i in range(2)]
                args_ready, exp_ready, factors_ready = p3.sem("args_ready"), p3.sem("exp_ready"), p3.sem("factors_ready")
                scores_ready, scores_read = p3.sem("scores_ready"), p3.sem("scores_read")
                groups = HG * NCH // 4

                @block.scalar
                def _(act):
                    n = 0
                    for w in todo:
                        if w:
                            for i in range(2):
                                n += 1
                                act.wait_ge(args_ready, n)
                                act.activation(arg[i][:, :], arg[i][:, :], ACT.Exp).then_inc(exp_ready, 1)

                @block.vector
                def _(dve):
                    n = 0
                    for j, w in enumerate(todo):
                        if j:
                            dve.wait_ge(scores_ready, groups * j)
                        if w == 0:
                            dve.tensor_copy(qe[:, :], q[:, :])
                            dve.tensor_tensor(ke[:, :], kf[:, :], kb[:, :], ALU.add).then_inc(factors_ready, 1)
                        else:
                            def half(a, i):
                                return a[:, :].rearrange("p (n two w) -> p n two w", two=2, w=w)[:, :, i, :]

                            mid = bsum[:, :].rearrange("p (n two w) -> p n two w", two=2, w=w)[:, :, 0, w - 1:w]
                            mid = mid.to_broadcast([P, W // (2 * w), w])
                            late, early = (bsum, bsum) if direction == 0 else (lf, lf)
                            a0, a1 = (arg[i][:, :].rearrange("p (n w) -> p n w", w=w) for i in range(2))
                            dve.tensor_tensor(a0, half(late, 1), mid, ALU.subtract).then_inc(args_ready, 1)
                            dve.tensor_tensor(a1, mid, half(early, 0), ALU.subtract).then_inc(args_ready, 1)
                            n += 2
                            late_of, early_of = ((q, qe), (k, ke)) if direction == 0 else ((k, ke), (q, qe))
                            dve.wait_ge(exp_ready, n - 1)
                            dve.tensor_tensor(half(late_of[1], 1), half(late_of[0], 1), a0, ALU.mult)
                            dve.wait_ge(exp_ready, n)
                            dve.tensor_tensor(half(early_of[1], 0), half(early_of[0], 0), a1, ALU.mult)
                            dve.drain()
                            dve.nop().then_inc(factors_ready, 1)
                        mask = C["masks"][:, (direction * 8 if w else 0) + (levels.index(w) + 1 if w else 0), :]
                        for g in range(groups):
                            dve.wait_ge(scores_ready, groups * j + g + 1)
                            dve.copy_predicated(attn[:, 4 * g:4 * g + 4, :], mask.unsqueeze(1).to_broadcast([P, 4, P]),
                                                sc[:, g, :, :]).then_inc(scores_read, 1)
                        dve.drain()

                @block.tensor
                def _(pe):
                    for j, w in enumerate(todo):
                        pe.wait_ge(factors_ready, j + 1)
                        for g in range(groups):
                            if j:
                                pe.wait_ge(scores_read, groups * (j - 1) + g + 1)
                            for i in range(4):
                                c = slice((4 * g + i) * CH, (4 * g + i + 1) * CH)
                                mm = pe.matmul(sc[:, g, i, :], ke[:, c], qe[:, c], start=True, stop=True)
                            mm.then_inc(scores_ready, 1)

            with Phase(nc, f"hg_s{direction}") as p4, nc.Block() as block:
                kt = p4.sb("kt", [P, HG * NCH, P])
                tr = p4.ps("tr", [P, 2, 4, P])
                so = p4.ps("so", [P, HG, P])
                su = p4.ps("su", [P, HG, P])
                args_ready, exp_ready, k_ready = p4.sem("args_ready"), p4.sem("exp_ready"), p4.sem("k_ready")
                transposed, copied = p4.sem("transposed"), p4.sem("copied")
                done, taken, grown = p4.sem("done"), p4.sem("taken"), p4.sem("grown")
                chunked = [a[:, :].rearrange("p (n t) -> p n t", t=CH) for a in (bsum, lf, qe, ke)]
                last = chunked[0][:, :, CH - 1:CH].to_broadcast([P, HG * NCH, CH])
                order = list(range(NCH)) if direction == 0 else list(range(NCH - 1, -1, -1))

                @block.scalar
                def _(act):
                    act.wait_ge(args_ready, 1)
                    act.activation(qe[:, :], qe[:, :], ACT.Exp).then_inc(exp_ready, 1)
                    act.activation(ke[:, :], ke[:, :], ACT.Exp).then_inc(exp_ready, 1)
                    act.activation(decay[:, :], chunked[0][:, :, CH - 1], ACT.Exp).then_inc(exp_ready, 1)

                @block.vector
                def _(dve):
                    if direction == 0:
                        dve.tensor_copy(qe[:, :], bsum[:, :])
                        dve.tensor_tensor(chunked[3], last, chunked[0], ALU.subtract)
                    else:
                        dve.tensor_tensor(chunked[2], last, chunked[1], ALU.subtract)
                        dve.tensor_copy(ke[:, :], lf[:, :])
                    dve.memset(state[:, :, :], 0.0)
                    dve.drain()
                    dve.nop().then_inc(args_ready, 1)
                    dve.wait_ge(exp_ready, 3)
                    dve.tensor_tensor(ke[:, :], ke[:, :], k[:, :], ALU.mult)
                    dve.tensor_tensor(qe[:, :], qe[:, :], q[:, :], ALU.mult)
                    dve.drain()
                    dve.nop().then_inc(k_ready, 1)
                    for g in range(HG * NCH // 4):
                        dve.wait_ge(transposed, g + 1)
                        dve.tensor_copy(kt[:, 4 * g:4 * g + 4, :], tr[:, g % 2, :, :]).then_inc(copied, 1)
                    for i, c in enumerate(order):
                        lo = PADN if c == 0 else 0
                        t0 = c * CH + lo - PADN
                        dve.wait_ge(done, i + 1)
                        part = y[:, :, t0:t0 + CH - lo]
                        if direction == 0:
                            dve.tensor_copy(part, so[:, :, lo:])
                        else:
                            dve.tensor_tensor(part, part, so[:, :, lo:], ALU.add)
                        for h in range(HG):
                            dve.scalar_tensor_tensor(out=state[:, h, :], in0=state[:, h, :],
                                                     scalar=decay[:, h * NCH + c:h * NCH + c + 1],
                                                     in1=su[:, h, :], op0=ALU.mult, op1=ALU.add)
                        dve.drain()
                        dve.nop().then_inc(grown, 1)

                @block.tensor
                def _(pe):
                    pe.wait_ge(k_ready, 1)
                    for g in range(HG * NCH // 4):
                        if g >= 2:
                            pe.wait_ge(copied, g - 1)
                        for i in range(4):
                            n = 4 * g + i
                            mm = pe.transpose(tr[:, g % 2, i, :], ke[:, n * CH:(n + 1) * CH], C["ident"][:, :])
                        mm.then_inc(transposed, 1)
                    pe.wait_ge(copied, HG * NCH // 4)
                    for i, c in enumerate(order):
                        if i:
                            pe.wait_ge(grown, i)
                        for h in range(HG):
                            n = h * NCH + c
                            pe.matmul(so[:, h, :], state[:, h, :], qe[:, n * CH:(n + 1) * CH], start=True,
                                      stop=(direction == 0))
                            if direction == 1:
                                pe.matmul(so[:, h, :], vt[:, n, :], attn[:, n, :], start=False, stop=True)
                            mm = pe.matmul(su[:, h, :], kt[:, n, :], vt[:, n, :], start=True, stop=True)
                        mm.then_inc(done, 1)

        sequence(0)
        sequence(1)

    n, w = halves(L)
    with Phase(nc, "hg_n") as p5, nc.Block() as block:
        sq = p5.sb("sq", [P, HG, L])
        total = p5.ps("total", [P, 2, n, BANK])
        squares_ready, total_ready, mean_ready, root_ready = (p5.sem(s) for s in ("squares", "total", "mean", "root"))

        @block.scalar
        def _(act):
            act.activation(sq[:, :, :], y[:, :, :], ACT.Square).then_inc(squares_ready, 1)
            act.wait_ge(mean_ready, HG)
            act.activation(sq[:, :, :], sq[:, :, :], ACT.Sqrt).then_inc(root_ready, 1)

        @block.tensor
        def _(pe):
            pe.wait_ge(squares_ready, 1)
            for h in range(HG):
                if h >= 2:
                    pe.wait_ge(mean_ready, h - 1)
                for j in range(n):
                    mm = pe.matmul(total[:, h % 2, j, 0:w], C["ones"][:, :], sq[:, h, j * w:(j + 1) * w], start=True, stop=True)
                mm.then_inc(total_ready, 1)

        @block.vector
        def _(dve):
            for h in range(HG):
                dve.wait_ge(total_ready, h + 1)
                dve.tensor_scalar(cut(sq[:, h, :], L), total[:, h % 2, :, 0:w], 1.0 / P, EPS, ALU.mult,
                                  ALU.add).then_inc(mean_ready, 1)
            dve.wait_ge(root_ready, 1)
            dve.reciprocal(sq[:, :, :], sq[:, :, :])
            dve.drain()
            for h in range(HG):
                dve.scalar_tensor_tensor(out=y[:, h, :], in0=y[:, h, :], scalar=V["hg_out_norm"][:, h:h + 1],
                                         in1=sq[:, h, :], op0=ALU.mult, op1=ALU.mult)
            dve.drain()
            dve.tensor_tensor(y[:, :, :], y[:, :, :], z[:, Z_G:Z_G + HG, PADN:], ALU.mult)
            dve.drain()


def gqa(nc, V, C, z, y):
    n, w = halves(L)
    qk = z[:, A_Q:A_Q + 6, :]
    with Phase(nc, "at_n") as ph, nc.Block() as block:
        sq = ph.sb("sq", [P, 6, L])
        total = ph.ps("total", [P, 2, n, BANK])
        swap = ph.ps("swap", [P, 2, n, BANK])
        squares_ready, total_ready, mean_ready, root_ready = (ph.sem(s) for s in ("squares", "total", "mean", "root"))
        normed, swapped, rotated = ph.sem("normed"), ph.sem("swapped"), ph.sem("rotated")

        @block.scalar
        def _(act):
            act.activation(sq[:, :, :], qk, ACT.Square).then_inc(squares_ready, 1)
            act.wait_ge(mean_ready, 6)
            act.activation(sq[:, :, :], sq[:, :, :], ACT.Sqrt).then_inc(root_ready, 1)

        @block.tensor
        def _(pe):
            pe.wait_ge(squares_ready, 1)
            for c in range(6):
                if c >= 2:
                    pe.wait_ge(mean_ready, c - 1)
                for j in range(n):
                    mm = pe.matmul(total[:, c % 2, j, 0:w], C["ones64"][:, :], sq[:, c, j * w:(j + 1) * w], start=True, stop=True)
                mm.then_inc(total_ready, 1)
            pe.wait_ge(normed, 1)
            for c in range(6):
                if c >= 2:
                    pe.wait_ge(rotated, c - 1)
                for j in range(n):
                    mm = pe.matmul(swap[:, c % 2, j, 0:w], C["swap"][:, :], z[:, A_Q + c, j * w:(j + 1) * w], start=True, stop=True)
                mm.then_inc(swapped, 1)

        @block.vector
        def _(dve):
            for c in range(6):
                dve.wait_ge(total_ready, c + 1)
                dve.tensor_scalar(cut(sq[:, c, :], L), total[:, c % 2, :, 0:w], 1.0 / HD, EPS, ALU.mult,
                                  ALU.add).then_inc(mean_ready, 1)
            dve.wait_ge(root_ready, 1)
            dve.reciprocal(sq[:, :, :], sq[:, :, :])
            dve.drain()
            for c in range(6):
                gain = V["q_norm"] if c < 4 else V["k_norm"]
                dve.scalar_tensor_tensor(out=qk[:, c, :], in0=qk[:, c, :], scalar=gain[:, 0:1],
                                         in1=sq[:, c, :], op0=ALU.mult, op1=ALU.mult)
            dve.drain()
            dve.nop().then_inc(normed, 1)
            for c in range(6):
                dve.wait_ge(swapped, c + 1)
                dve.tensor_tensor(cut(sq[:, c, :], L), swap[:, c % 2, :, 0:w], cut(C["sin"][:, :], L), ALU.mult).then_inc(rotated, 1)
                dve.tensor_tensor(qk[:, c, :], qk[:, c, :], C["cos"][:, :], ALU.mult)
            dve.drain()
            dve.tensor_tensor(qk, qk, sq[:, :, :], ALU.add)
            dve.drain()

    with Phase(nc, "at") as ph, nc.Block() as block:
        vt = ph.sb("vt", [AT_T, AT_N, P])
        probs = [ph.sb(f"probs{i}", [AT_T, L]) for i in range(2)]
        pT = [ph.sb(f"pT{i}", [AT_T, AT_N, L]) for i in range(2)]
        top, total = ph.sb("top", [AT_T, 2]), ph.sb("total", [AT_T, 2])
        sc = [ph.ps(f"sc{i}", [AT_T, n, BANK]) for i in range(2)]
        turn = ph.ps("turn", [AT_T, 2, BANK])
        out = ph.ps("out", [P, n, BANK])
        scores_ready, exp_ready, probs_ready = ph.sem("scores_ready"), ph.sem("exp_ready"), ph.sem("probs_ready")
        max_ready, turned, turn_read = ph.sem("max_ready"), ph.sem("turned"), ph.sem("turn_read")
        out_ready, out_read = ph.sem("out_ready"), ph.sem("out_read")
        v_turned, v_read = ph.sem("v_turned"), ph.sem("v_read")
        tiles = AT_HEADS * AT_N
        half = AT_N // 2

        @block.tensor
        def _(pe):
            for j in range(AT_N):
                mm = pe.transpose(out[0:AT_T, j // 3, (j % 3) * P:(j % 3 + 1) * P], z[:, A_V, j * AT_T:(j + 1) * AT_T],
                                  C["ident"][:, :])
            mm.then_inc(v_turned, 1)
            pe.wait_ge(v_read, 1)

            def scores(i):
                h, t = divmod(i, AT_N)
                lo = HD * (h % 2)
                if i >= 2:
                    pe.wait_ge(exp_ready, i - 1)
                for j in range(n):
                    mm = pe.matmul(sc[i % 2][:, j, 0:w], z[lo:lo + HD, A_Q + h // 2, t * AT_T:(t + 1) * AT_T],
                                   z[lo:lo + HD, A_K + h // 4, j * w:(j + 1) * w], start=True, stop=True)
                mm.then_inc(scores_ready, 1)

            def values(h):
                lo = HD * (h % 2)
                pe.wait_ge(turn_read, (h + 1) * AT_N)
                if h:
                    pe.wait_ge(out_read, h)
                for j in range(n):
                    for s in range(AT_N):
                        mm = pe.matmul(out[lo:lo + HD, j, 0:w], vt[:, s, HD * (h // 4):HD * (h // 4) + HD],
                                       pT[h % 2][:, s, j * w:(j + 1) * w], start=(s == 0), stop=(s == AT_N - 1))
                mm.then_inc(out_ready, 1)

            scores(0)
            for i in range(tiles):
                if i + 1 < tiles:
                    scores(i + 1)
                pe.wait_ge(probs_ready, i + 1)
                if i:
                    pe.wait_ge(turn_read, i)
                for s in range(AT_N):
                    mm = pe.transpose(turn[:, s // half, (s % half) * AT_T:(s % half + 1) * AT_T],
                                      probs[i % 2][:, s * AT_T:(s + 1) * AT_T], C["ident"][0:AT_T, 0:AT_T])
                mm.then_inc(turned, 1)
                if i % AT_N == AT_N - 1:
                    values(i // AT_N)

        def take(act, i):
            h, t = divmod(i, AT_N)
            act.wait_ge(turned, i + 1)
            if h >= 2 and t == 0:
                act.wait_ge(out_ready, h - 1)
            for a in range(2):
                cp = act.activation(pT[h % 2][:, half * a:half * a + half, t * AT_T:(t + 1) * AT_T],
                                    turn[:, a, 0:half * AT_T].rearrange("p (s t) -> p s t", t=AT_T), ACT.Copy)
            cp.then_inc(turn_read, 1)

        @block.scalar
        def _(act):
            for i in range(tiles):
                act.wait_ge(max_ready, i + 1)
                if i >= 2:
                    act.wait_ge(turned, i - 1)
                act.activation(cut(probs[i % 2][:, :], L), sc[i % 2][:, :, 0:w], ACT.Exp, bias=top[:, i % 2:i % 2 + 1],
                               scale=HD ** -0.5, accum_out=total[:, i % 2:i % 2 + 1]).then_inc(exp_ready, 1)
                if i:
                    take(act, i - 1)
            take(act, tiles - 1)

        @block.vector
        def _(dve):
            dve.wait_ge(v_turned, 1)
            dve.tensor_copy(vt[:, :, :].rearrange("p (a b) e -> p a b e", a=2),
                            out[0:AT_T, :, 0:3 * P].rearrange("p a (b e) -> p a b e", b=3)).then_inc(v_read, 1)

            def maximum(i):
                dve.wait_ge(scores_ready, i + 1)
                dve.tensor_reduce(top[:, i % 2:i % 2 + 1], sc[i % 2][:, :, 0:w], mybir.AxisListType.XY, ALU.max)
                dve.drain()
                dve.tensor_scalar(top[:, i % 2:i % 2 + 1], top[:, i % 2:i % 2 + 1], -(HD ** -0.5), None,
                                  ALU.mult).then_inc(max_ready, 1)

            maximum(0)
            for i in range(tiles):
                dve.wait_ge(exp_ready, i + 1)
                if i + 1 < tiles:
                    maximum(i + 1)
                dve.reciprocal(total[:, i % 2:i % 2 + 1], total[:, i % 2:i % 2 + 1])
                dve.drain()
                dve.tensor_scalar(probs[i % 2][:, :], probs[i % 2][:, :], total[:, i % 2:i % 2 + 1], None,
                                  ALU.mult).then_inc(probs_ready, 1)
                if i % AT_N == AT_N - 1:
                    h = i // AT_N
                    lo = HD * (h % 2)
                    dve.wait_ge(out_ready, h + 1)
                    dve.tensor_copy(cut(y[lo:lo + HD, h // 2, :], L), out[lo:lo + HD, :, 0:w]).then_inc(out_read, 1)


def first_block(nc, W, V, C, x, h):
    h_out = h[:, :, META:]
    with Phase(nc, "b1") as ph:
        C = C | load(nc, ph, "c1", {k: W[k] for k in ("masks", "cos", "sin", "swap", "ones64")})
        xn = ph.sb("xn", [P, DC, L])
        with Phase(nc, "in1") as p0, nc.Block() as block:
            loaded = p0.sem("loaded")

            @block.sync
            def _(sp):
                sp.dma_start(h[:, :, 0:META], W["meta"]).then_inc(loaded, 16)
                sp.dma_start(h[:, :, META:], x).then_inc(loaded, 16)
                sp.wait_ge(loaded, 32)

        rms_norm(nc, "n1", L, C["ones"], h, xn, V["ffn1_norm"])
        with Phase(nc, "f1") as pf:
            hidden = pf.sb("hidden", [P, FC, L])
            gated_up(nc, "f1u", L, xn, W["ffn1_w_gate"], W["ffn1_w_up"], FC, hidden)
            project(nc, "f1d", L, hidden, W["ffn1_w_down"], DC, h, scale=0.5, residual=True)
        rms_norm(nc, "n2", L, C["ones"], h, xn, V["mix_norm"])
        with Phase(nc, "mix") as pm:
            ya = pm.sb("ya", [P, HG, L])
            yb = pm.sb("yb", [P, HG, L])
            with Phase(nc, "za") as pz:
                z = pz.sb("z", [P, A_END, L])
                project(nc, "zap", L, xn, W["w_in"][Z_END:Z_GATES], A_END, z)
                gqa(nc, V, C, z, yb)
            with Phase(nc, "zh") as pz:
                z = pz.sb("z", [P, Z_END, LP])
                project(nc, "zhp", L, xn, W["w_in"][0:Z_END], Z_END, z[:, :, PADN:])
                hgrn(nc, V, C, z, ya)
            gates = pm.sb("gates", [P, 2 * DC, L])
            project(nc, "gp", L, xn, W["w_in"][Z_GATES:Z_GATES + 2 * DC], 2 * DC, gates)
            with nc.Block() as block:
                @block.scalar
                def _(act):
                    act.activation(gates[:, :, :], gates[:, :, :], ACT.Sigmoid)
            merge(nc, "mg", L, ya, W["w_up_a"], gates[:, 0:DC, :], yb, W["w_up_b"], gates[:, DC:2 * DC, :], DC, xn)

        mixed = xn[:, :, META:]
        project(nc, "wo", SEQ, mixed, W["w_out"], DC, h_out, residual=True)
        rms_norm(nc, "n3", SEQ, C["ones"], h_out, xn[:, :, 0:SEQ], V["ffn2_norm"])
        with Phase(nc, "f2") as pf:
            hidden = pf.sb("hidden", [P, FC, SEQ])
            gated_up(nc, "f2u", SEQ, xn[:, :, 0:SEQ], W["ffn2_w_gate"], W["ffn2_w_up"], FC, hidden)
            project(nc, "f2d", SEQ, hidden, W["ffn2_w_down"], DC, h_out, scale=0.5, residual=True)
B2_AVAL, B2_AGATE, B2_POOL, B2_CH, B2_CB, B2_CC, B2_Q, B2_K, B2_V, B2_END = 0, 2, 4, 6, 8, 10, 12, 14, 16, 18
CONF = 31
SCONV = 3
POOL_PAD = 16
WINDOWS = (2, 4, 8, 16)
SB_HEADS = 4
TILES = SEQ // P
PK_HEADS = 8
PK_TOP = 16
NKEYS = 128
PICKS = PK_HEADS * PK_TOP
LOW = -3.0e38


def local_mixes(nc, V, C, W, x, z, y):
    with Phase(nc, "lm") as ph:
        with nc.Block() as block:
            u = ph.sb("u", [P, 2, CONF - 1 + SEQ])
            c = ph.sb("c", [P, 2, SCONV - 1 + SEQ])
            base = ph.sb("base", [P, 2, POOL_PAD + SEQ])
            sums = [ph.sb(f"sums{i}", [P, 2, POOL_PAD + SEQ]) for i in range(4)]
            gate_ready = ph.sem("gate_ready")

            @block.scalar
            def _(act):
                act.activation(z[:, B2_AGATE:B2_AGATE + 2, :], z[:, B2_AGATE:B2_AGATE + 2, :], ACT.Sigmoid).then_inc(gate_ready, 1)

            @block.vector
            def _(dve):
                dve.memset(u[:, :, 0:CONF - 1], 0.0)
                dve.memset(c[:, :, 0:SCONV - 1], 0.0)
                for a in [base] + sums:
                    dve.memset(a[:, :, 0:POOL_PAD], 0.0)
                dve.tensor_copy(base[:, :, POOL_PAD:], z[:, B2_POOL:B2_POOL + 2, :])
                dve.tensor_tensor(c[:, :, SCONV - 1:], z[:, B2_CC:B2_CC + 2, :], z[:, B2_CH:B2_CH + 2, :], ALU.mult)
                dve.tensor_scalar(x[:, :, :], x[:, :, :], DEEP_ALPHA, None, ALU.mult)
                dve.wait_ge(gate_ready, 1)
                dve.tensor_tensor(u[:, :, CONF - 1:], z[:, B2_AVAL:B2_AVAL + 2, :], z[:, B2_AGATE:B2_AGATE + 2, :], ALU.mult)
                dve.drain()
                for k in range(CONF):
                    for m in range(2):
                        tap = V["conv_a_w"][:, 2 * k + m:2 * k + m + 1]
                        if k == 0:
                            dve.tensor_scalar(y[:, m, :], u[:, m, 0:SEQ], tap, V["conv_a_b"][:, m:m + 1], ALU.mult, ALU.add)
                        else:
                            dve.scalar_tensor_tensor(out=y[:, m, :], in0=u[:, m, k:k + SEQ], scalar=tap, in1=y[:, m, :],
                                                     op0=ALU.mult, op1=ALU.add)
                    if k < SCONV:
                        for m in range(2):
                            tap = V["conv_c_w"][:, 2 * k + m:2 * k + m + 1]
                            if k == 0:
                                dve.tensor_scalar(y[:, 4 + m, :], c[:, m, 0:SEQ], tap, None, ALU.mult)
                            else:
                                dve.scalar_tensor_tensor(out=y[:, 4 + m, :], in0=c[:, m, k:k + SEQ], scalar=tap,
                                                         in1=y[:, 4 + m, :], op0=ALU.mult, op1=ALU.add)
                    if k < len(WINDOWS):
                        before = base if k == 0 else sums[k - 1]
                        lag = WINDOWS[k] // 2
                        dve.tensor_tensor(sums[k][:, :, POOL_PAD:], before[:, :, POOL_PAD:],
                                          before[:, :, POOL_PAD - lag:POOL_PAD - lag + SEQ], ALU.add)
                    dve.drain()
                dve.tensor_tensor(y[:, 4:6, :], y[:, 4:6, :], z[:, B2_CB:B2_CB + 2, :], ALU.mult)
                for g in range(len(WINDOWS)):
                    part, m = slice(64 * (g % 2), 64 * (g % 2) + 64), g // 2
                    dve.tensor_tensor(y[part, 2 + m, :], sums[g][part, m, POOL_PAD:], C["inv_count"][part, m, :], ALU.mult)
                dve.drain()
                dve.tensor_tensor(y[:, 2:4, :], y[:, 2:4, :], base[:, :, POOL_PAD:], ALU.subtract)
                dve.drain()

        with nc.Block() as block:
            pooled = ph.ps("pooled", [P, 2, BANK])
            weights = ph.sb("pool_w", [P, 2, P])
            loaded, mixed_ready = ph.sem("loaded"), ph.sem("mixed_ready")

            @block.sync
            def _(sp):
                sp.dma_start(weights[:, :, :], W["pool_w"]).then_inc(loaded, 16)

            @block.tensor
            def _(pe):
                pe.wait_ge(loaded, 16)
                for m in range(2):
                    mm = pe.matmul(pooled[:, m, :], weights[:, m, :], y[:, 2 + m, :], start=True, stop=True)
                mm.then_inc(mixed_ready, 1)

            @block.vector
            def _(dve):
                dve.wait_ge(mixed_ready, 1)
                for m in range(2):
                    dve.tensor_scalar(y[:, 2 + m, :], pooled[:, m, :], V["pool_scale"][:, m:m + 1], None, ALU.mult)
                dve.drain()


def stick_breaking(nc, C, z, y):
    with Phase(nc, "sb") as ph, nc.Block() as block:
        vt = ph.sb("vt", [P, TILES, 2 * P])
        zt, sp_, cum = ph.sb("zt", [P, SB_HEADS, SEQ]), ph.sb("softplus", [P, SB_HEADS, SEQ]), ph.sb("cum", [P, SB_HEADS, SEQ])
        one = ph.sb("one", [P, SEQ])
        wT = [ph.sb(f"wT{i}", [P, TILES, P]) for i in range(2)]
        sc = ph.ps("sc", [P, SB_HEADS, BANK])
        turn = ph.ps("turn", [P, 2, TILES, P])
        out = ph.ps("out", [P, 2, BANK])
        v_turned, v_read = ph.sem("v_turned"), ph.sem("v_read")
        scores_ready, scores_read = ph.sem("scores_ready"), ph.sem("scores_read")
        z_ready, log_ready = ph.sem("z_ready"), ph.sem("log_ready")
        logw_ready, exp_ready, w_ready = ph.sem("logw_ready"), ph.sem("exp_ready"), ph.sem("w_ready")
        turned, turn_read, out_ready, out_read = (ph.sem(s) for s in ("turned", "turn_read", "out_ready", "out_read"))

        @block.tensor
        def _(pe):
            for m in range(2):
                for b in range(TILES):
                    mm = pe.transpose(turn[:, m, b, :], z[:, B2_V + m, b * P:(b + 1) * P], C["ident"][:, :])
            mm.then_inc(v_turned, 1)
            pe.wait_ge(v_read, 1)
            for b in range(TILES):
                n = (b + 1) * P
                if b:
                    pe.wait_ge(scores_read, b)
                for h in range(SB_HEADS):
                    lo = HD * (h % 2)
                    mm = pe.matmul(sc[:, h, 0:n], z[lo:lo + HD, B2_Q + h // 2, b * P:n], z[lo:lo + HD, B2_K + h // 2, 0:n],
                                   start=True, stop=True)
                mm.then_inc(scores_ready, 1)
                pe.wait_ge(w_ready, b + 1)
                for h in range(SB_HEADS):
                    i = SB_HEADS * b + h
                    lo = HD * (h % 2)
                    if i >= 2:
                        pe.wait_ge(turn_read, i - 1)
                    for s in range(b + 1):
                        mm = pe.transpose(turn[:, i % 2, s, :], zt[:, h, s * P:(s + 1) * P], C["ident"][:, :])
                    mm.then_inc(turned, 1)
                    pe.wait_ge(turn_read, i + 1)
                    if i >= 2:
                        pe.wait_ge(out_read, i - 1)
                    for s in range(b + 1):
                        mm = pe.matmul(out[lo:lo + HD, i % 2, 0:P], vt[:, s, HD * h:HD * h + HD], wT[i % 2][:, s, :],
                                       start=(s == 0), stop=(s == b))
                    mm.then_inc(out_ready, 1)

        @block.scalar
        def _(act):
            for b in range(TILES):
                n = (b + 1) * P
                act.wait_ge(z_ready, b + 1)
                act.activation(sp_[:, :, 0:n], zt[:, :, 0:n], ACT.Abs)
                act.drain()
                act.activation(sp_[:, :, 0:n], sp_[:, :, 0:n], ACT.Exp, scale=-1.0)
                act.drain()
                act.activation(sp_[:, :, 0:n], sp_[:, :, 0:n], ACT.Ln, bias=1.0).then_inc(log_ready, 1)
                act.wait_ge(logw_ready, b + 1)
                for h in range(SB_HEADS):
                    ex = act.activation(zt[:, h, 0:n], zt[:, h, 0:n], ACT.Exp, bias=cum[:, h, n - 1:n])
                ex.then_inc(exp_ready, 1)
                for h in range(SB_HEADS):
                    i = SB_HEADS * b + h
                    act.wait_ge(turned, i + 1)
                    act.activation(wT[i % 2][:, 0:b + 1, :], turn[:, i % 2, 0:b + 1, :], ACT.Copy).then_inc(turn_read, 1)

        @block.vector
        def _(dve):
            dve.memset(one[:, :], 1.0)
            dve.wait_ge(v_turned, 1)
            for m in range(2):
                dve.tensor_copy(vt[:, :, m * P:(m + 1) * P], turn[:, m, :, :])
            dve.drain()
            dve.nop().then_inc(v_read, 1)
            for b in range(TILES):
                n = (b + 1) * P
                diag = slice(b * P, n)
                mask = C["before"][:, :].unsqueeze(1).to_broadcast([P, SB_HEADS, P])
                dve.wait_ge(scores_ready, b + 1)
                if b:
                    dve.wait_ge(turned, SB_HEADS * b)
                dve.tensor_scalar(zt[:, :, 0:n], sc[:, :, 0:n], HD ** -0.5, None, ALU.mult).then_inc(scores_read, 1)
                dve.drain()
                dve.nop().then_inc(z_ready, 1)
                dve.tensor_scalar(cum[:, :, 0:n], zt[:, :, 0:n], 0.0, None, ALU.max)
                dve.drain()
                dve.wait_ge(log_ready, b + 1)
                dve.tensor_tensor(sp_[:, :, 0:n], sp_[:, :, 0:n], cum[:, :, 0:n], ALU.add)
                dve.drain()
                dve.tensor_tensor(zt[:, :, 0:n], zt[:, :, 0:n], sp_[:, :, 0:n], ALU.subtract)
                dve.drain()
                dve.tensor_tensor(sp_[:, :, diag], sp_[:, :, diag], mask, ALU.mult)
                dve.drain()
                for h in range(SB_HEADS):
                    dve.tensor_tensor_scan(cum[:, h, 0:n], one[:, 0:n], sp_[:, h, 0:n], 0.0, ALU.mult, ALU.add)
                dve.drain()
                dve.tensor_tensor(zt[:, :, 0:n], zt[:, :, 0:n], cum[:, :, 0:n], ALU.add)
                dve.drain()
                for h in range(SB_HEADS):
                    dve.tensor_scalar(cum[:, h, n - 1:n], cum[:, h, n - 1:n], -1.0, None, ALU.mult)
                dve.drain()
                dve.nop().then_inc(logw_ready, 1)
                dve.wait_ge(exp_ready, b + 1)
                dve.tensor_tensor(zt[:, :, diag], zt[:, :, diag], mask, ALU.mult).then_inc(w_ready, 1)
                for h in range(SB_HEADS):
                    i = SB_HEADS * b + h
                    lo = HD * (h % 2)
                    dve.wait_ge(out_ready, i + 1)
                    dve.tensor_copy(y[lo:lo + HD, h // 2, b * P:n], out[lo:lo + HD, i % 2, 0:P]).then_inc(out_read, 1)


def choose_experts(nc, C, W, q, gates_dram):
    with Phase(nc, "pk") as ph:
        keys = ph.sb("keys", [P, 2 * PK_HEADS, NKEYS])
        scores = ph.sb("scores", [P, 2 * PK_HEADS, NKEYS])
        best = ph.sb("best", [P, 2 * PK_HEADS, PK_TOP])
        where = ph.sb("where", [P, 2 * PK_HEADS, PK_TOP], U32)
        wheref = ph.sb("wheref", [P, PK_HEADS, 2, PK_TOP])
        pair = ph.sb("pair", [P, PK_HEADS, PK_TOP * PK_TOP])
        top = ph.sb("top", [P, PK_HEADS, PK_TOP])
        at = ph.sb("at", [P, PICKS], U32)
        half = ph.sb("half", [P, 2, PICKS], U32)
        halff = ph.sb("halff", [P, 2, PICKS])
        hot = ph.sb("hot", [P, PICKS, PK_TOP])
        picks = ph.sb("picks", [P, 3, PICKS])
        sums = ph.sb("sums", [P, PK_HEADS])
        by_pick = ph.sb("by_pick", [P, 3, P])
        grid = ph.sb("grid", [P, NKEYS, P])
        GROUP = 4
        first_hot = [ph.sb(f"first_hot{s}", [P, P]) for s in range(2 * GROUP)]
        second_hot = [ph.sb(f"second_hot{s}", [P, P]) for s in range(2 * GROUP)]

        with nc.Block() as block:
            loaded = ph.sem("loaded")

            @block.sync
            def _(sp):
                sp.dma_start(keys[:, :, :], W["peer_keys"]).then_inc(loaded, 16)
                sp.wait_ge(loaded, 16)

        for t in range(TILES):
            with Phase(nc, f"pt{t}") as p1, nc.Block() as block:
                sc = p1.ps("sc", [P, 4, 4, NKEYS])
                turn = p1.ps("turn", [P, 3, P])
                scores_ready, sub_ready, exp_ready = p1.sem("scores_ready"), p1.sem("sub_ready"), p1.sem("exp_ready")
                picks_ready, turned = p1.sem("picks_ready"), p1.sem("turned")

                @block.tensor
                def _(pe):
                    for g in range(2 * PK_HEADS):
                        mm = pe.matmul(sc[:, g // 4, g % 4, :], q[:, g, t * P:(t + 1) * P], keys[:, g, :], start=True, stop=True)
                        if g % 4 == 3:
                            mm.then_inc(scores_ready, 1)
                    pe.wait_ge(picks_ready, 1)
                    for i in range(3):
                        mm = pe.transpose(turn[:, i, :], picks[:, i, :], C["ident"][:, :])
                    mm.then_inc(turned, 1)

                @block.scalar
                def _(act):
                    act.wait_ge(sub_ready, 1)
                    act.activation(picks[:, 2, :], picks[:, 2, :], ACT.Exp).then_inc(exp_ready, 1)

                @block.vector
                def _(dve):
                    for g in range(4):
                        dve.wait_ge(scores_ready, g + 1)
                        dve.tensor_copy(scores[:, 4 * g:4 * g + 4, :], sc[:, g, :, :])
                    dve.drain()

                    def top16(values, best, where, lists):
                        for r in range(2):
                            for g in range(lists):
                                dve.max(best(g)[:, 8 * r:8 * r + 8], values(g))
                            dve.drain()
                            for g in range(lists):
                                dve.max_index(where(g)[:, 8 * r:8 * r + 8], best(g)[:, 8 * r:8 * r + 8], values(g))
                            if r == 0:
                                dve.drain()
                                for g in range(lists):
                                    dve.match_replace(values(g), best(g)[:, 0:8], values(g), LOW)
                            dve.drain()

                    top16(lambda g: scores[:, g, :], lambda g: best[:, g, :], lambda g: where[:, g, :], 2 * PK_HEADS)
                    dve.tensor_copy(wheref[:, :, :, :].rearrange("p h a k -> p (h a k)"),
                                    where[:, :, :].rearrange("p g k -> p (g k)"))
                    halves_of = best[:, :, :].rearrange("p (h a) k -> p h a k", a=2)
                    dve.tensor_tensor(pair[:, :, :].rearrange("p h (a b) -> p h a b", a=PK_TOP),
                                      halves_of[:, :, 0, :].unsqueeze(3).to_broadcast([P, PK_HEADS, PK_TOP, PK_TOP]),
                                      halves_of[:, :, 1, :].unsqueeze(2).to_broadcast([P, PK_HEADS, PK_TOP, PK_TOP]), ALU.add)
                    dve.drain()
                    top16(lambda h: pair[:, h, :], lambda h: top[:, h, :],
                          lambda h: at[:, h * PK_TOP:(h + 1) * PK_TOP], PK_HEADS)
                    gates = picks[:, 2, :].rearrange("p (h k) -> p h k", h=PK_HEADS)
                    dve.tensor_tensor(gates, top[:, :, :], top[:, :, 0:1].to_broadcast([P, PK_HEADS, PK_TOP]),
                                      ALU.subtract).then_inc(sub_ready, 1)
                    dve.tensor_scalar(half[:, 0, :], at[:, :], 4, None, ALU.logical_shift_right)
                    dve.tensor_scalar(half[:, 1, :], at[:, :], 15, None, ALU.bitwise_and)
                    dve.drain()
                    dve.tensor_copy(halff[:, :, :], half[:, :, :])
                    dve.drain()
                    for i in range(2):
                        dve.tensor_tensor(hot[:, :, :], halff[:, i, :].unsqueeze(2).to_broadcast([P, PICKS, PK_TOP]),
                                          C["iota"][:, 0:PK_TOP].unsqueeze(1).to_broadcast([P, PICKS, PK_TOP]), ALU.is_equal)
                        dve.drain()
                        hot4 = hot[:, :, :].rearrange("p (h k) a -> p h k a", h=PK_HEADS)
                        dve.tensor_tensor(hot4, hot4, wheref[:, :, i, :].unsqueeze(2).to_broadcast(
                            [P, PK_HEADS, PK_TOP, PK_TOP]), ALU.mult)
                        dve.drain()
                        dve.tensor_reduce(picks[:, i, :], hot[:, :, :], AX_X, ALU.add)
                        dve.drain()
                    dve.wait_ge(exp_ready, 1)
                    dve.tensor_reduce(sums[:, :], gates, AX_X, ALU.add)
                    dve.drain()
                    dve.reciprocal(sums[:, :], sums[:, :])
                    dve.drain()
                    dve.tensor_tensor(gates, gates, sums[:, :].unsqueeze(2).to_broadcast([P, PK_HEADS, PK_TOP]), ALU.mult)
                    dve.drain()
                    dve.nop().then_inc(picks_ready, 1)
                    dve.wait_ge(turned, 1)
                    dve.tensor_copy(by_pick[:, :, :], turn[:, :, :])
                    dve.drain()

            with Phase(nc, f"pg{t}") as p2, nc.Block() as block:
                cell = [p2.ps(f"cell{s}", [P, GROUP, NKEYS]) for s in range(2)]
                hot_ready, cells_ready, cells_read, stored = (p2.sem(s) for s in ("hot_ready", "cells_ready", "cells_read", "stored"))
                groups = P // GROUP

                @block.vector
                def _(dve):
                    def make(g, s, first):
                        if not first:
                            dve.wait_ge(cells_ready, g - 1)
                        for i in range(GROUP):
                            token = g * GROUP + i
                            dve.tensor_scalar(first_hot[s * GROUP + i][:, :], C["iota"][:, :],
                                              by_pick[:, 0, token:token + 1] if isinstance(token, int) else by_pick[:, 0, bass.ds(token, 1)],
                                              None, ALU.is_equal)
                            col = slice(token, token + 1) if isinstance(token, int) else bass.ds(token, 1)
                            last = dve.tensor_scalar(second_hot[s * GROUP + i][:, :], C["iota"][:, :], by_pick[:, 1, col],
                                                     by_pick[:, 2, col], ALU.is_equal, ALU.mult)
                        last.then_inc(hot_ready, 1)

                    def read(g, s, first):
                        dve.wait_ge(cells_ready, g + 1)
                        tokens = slice(g * GROUP, (g + 1) * GROUP) if isinstance(g, int) else bass.ds(g * GROUP, GROUP)
                        dve.tensor_scalar(grid[:, :, tokens].rearrange("p j t -> p t j"), cell[s][:, :, :], 1.0, None,
                                          ALU.mult).then_inc(cells_read, 1)

                    def step(g, s, first):
                        make(g, s, first)
                        if g is not None and not (isinstance(g, int) and g == 0):
                            read(g - 1, 1 - s, first)

                    over_steps(dve, groups, 2, step)
                    read(groups - 1, (groups - 1) % 2, False)

                @block.tensor
                def _(pe):
                    def step(g, s, first):
                        pe.wait_ge(hot_ready, g + 1)
                        if not first:
                            pe.wait_ge(cells_read, g - 1)
                        for i in range(GROUP):
                            mm = pe.matmul(cell[s][:, i, :], first_hot[s * GROUP + i][:, :], second_hot[s * GROUP + i][:, :],
                                           start=True, stop=True)
                        mm.then_inc(cells_ready, 1)

                    over_steps(pe, groups, 2, step)

                @block.sync
                def _(sp):
                    sp.wait_ge(cells_read, groups)
                    sp.dma_start(gates_dram[:, :, t * P:(t + 1) * P].rearrange("j i t -> i j t"), grid[:, :, :]).then_inc(stored, 16)
                    sp.wait_ge(stored, 16)


def experts(nc, W, x, gates_dram, f):
    GROUP = 4
    groups = NKEYS // GROUP
    with Phase(nc, "ex") as ph, nc.Block() as block:
        u_ring = [ph.sb(f"u{s}", [P, D]) for s in range(GROUP)]
        g_ring = [ph.sb(f"g{s}", [P, SEQ]) for s in range(GROUP)]
        v_ring = [[ph.sb(f"v{b}_{s}", [P, D]) for s in range(GROUP)] for b in range(2)]
        hidden = [[ph.sb(f"a{b}_{s}", [P, SEQ]) for s in range(GROUP)] for b in range(2)]
        raw = [ph.sb(f"raw{s}", [P, SEQ]) for s in range(2)]
        up = [ph.ps(f"up{s}", [P, BANK]) for s in range(2)]
        down = [ph.ps(f"down{s}", [P, BANK]) for s in range(4)]
        u_in = [ph.sem(f"u_in{s}") for s in range(GROUP)]
        g_in = [ph.sem(f"g_in{s}") for s in range(GROUP)]
        v_in = [ph.sem(f"v_in{b}") for b in range(2)]
        up_done, gelu_done, gated, down_done, added = (ph.sem(s) for s in ("up_done", "gelu_done", "gated", "down_done", "added"))

        def over_groups(eng, body):
            body(0, 0, True)
            with eng.Fori(1, groups // 2) as i:
                body(2 * i - 1, 1, False)
                body(2 * i, 0, False)
            body(groups - 1, 1, False)

        @block.sync
        def _(sp):
            def load(g, b, first):
                for s in range(GROUP):
                    j = g * GROUP + s
                    if not first:
                        sp.wait_ge(up_done, j - GROUP + 1)
                    sp.dma_start(u_ring[s][:, :], W["peer_u"][j]).then_inc(u_in[s], 16)
                    if not first:
                        sp.wait_ge(gated, j - GROUP + 1)
                    sp.dma_start(g_ring[s][:, :], gates_dram[j]).then_inc(g_in[s], 16)
                if not (isinstance(g, int) and g < 2):
                    if not isinstance(g, int) or g >= 2:
                        sp.wait_ge(down_done, (g - 1) * DC)
                for s in range(GROUP):
                    sp.dma_start(v_ring[b][s][:, :], W["peer_v"][g * GROUP + s]).then_inc(v_in[b], 16)

            load(0, 0, True)
            load(1, 1, False)
            with sp.Fori(1, groups // 2) as i:
                load(2 * i, 0, False)
                load(2 * i + 1, 1, False)

        @block.tensor
        def _(pe):
            def ups(g):
                for s in range(GROUP):
                    j = g * GROUP + s
                    pe.wait_ge(u_in[s], 16 * g + 16)
                    if not (isinstance(j, int) and j < 2):
                        pe.wait_ge(gelu_done, j - 1)
                    for k in range(DC):
                        mm = pe.matmul(up[s % 2][:, :], u_ring[s][:, k * P:(k + 1) * P], x[:, k, :],
                                       start=(k == 0), stop=(k == DC - 1))
                    mm.then_inc(up_done, 1)

            def downs(g, b, first):
                pe.wait_ge(gated, GROUP * g + GROUP)
                pe.wait_ge(v_in[b], (g - b) * (8 * GROUP) + 16 * GROUP)
                for c in range(DC):
                    if not (first and c < 4):
                        pe.wait_ge(added, g * DC + c - 3)
                    for s in range(GROUP):
                        mm = pe.matmul(down[c % 4][:, :], v_ring[b][s][:, c * P:(c + 1) * P], hidden[b][s][:, :],
                                       start=(s == 0), stop=(s == GROUP - 1))
                    mm.then_inc(down_done, 1)

            def group(g, b, first):
                if not (isinstance(g, int) and g == groups - 1):
                    ups(g + 1)
                downs(g, b, first)

            ups(0)
            over_groups(pe, group)

        @block.scalar
        def _(act):
            def group(g, b, first):
                for s in range(GROUP):
                    j = g * GROUP + s
                    act.wait_ge(up_done, j + 1)
                    if not (first and s < 2):
                        act.wait_ge(gated, j - 1)
                    act.activation(raw[s % 2][:, :], up[s % 2][:, :], ACT.Gelu_apprx_tanh).then_inc(gelu_done, 1)

            over_groups(act, group)

        @block.vector
        def _(dve):
            def gate(g, b, first):
                if not (isinstance(g, int) and g < 2):
                    dve.wait_ge(down_done, (g - 1) * DC)
                for s in range(GROUP):
                    j = g * GROUP + s
                    dve.wait_ge(g_in[s], 16 * g + 16)
                    dve.wait_ge(gelu_done, j + 1)
                    dve.tensor_tensor(hidden[b][s][:, :], raw[s % 2][:, :], g_ring[s][:, :], ALU.mult).then_inc(gated, 1)

            def add(g, b, first):
                for c in range(DC):
                    dve.wait_ge(down_done, g * DC + c + 1)
                    if first:
                        dve.tensor_copy(f[:, c, :], down[c % 4][:, :]).then_inc(added, 1)
                    else:
                        dve.tensor_tensor(f[:, c, :], f[:, c, :], down[c % 4][:, :], ALU.add).then_inc(added, 1)
                dve.drain()

            def group(g, b, first):
                if not (isinstance(g, int) and g == groups - 1):
                    gate(g + 1, 1 - b, False)
                add(g, b, first)

            gate(0, 0, True)
            over_groups(dve, group)


def second_block(nc, W, V, C, x, gates_dram):
    with Phase(nc, "b2") as ph:
        C = C | load(nc, ph, "c2", {k: W[k] for k in ("iota", "before", "inv_count")})
        y = ph.sb("y", [P, DC, SEQ])
        with Phase(nc, "b2z") as pz:
            z = pz.sb("z", [P, B2_END, SEQ])
            project(nc, "p2", SEQ, x, W["w_in_2"], B2_END, z)
            local_mixes(nc, V, C, W, x, z, y)
            stick_breaking(nc, C, z, y[:, 6:8, :])
            conf = pz.sb("conf", [P, 2, SEQ])
            layer_norm(nc, "lna", SEQ, C["ones"], y[:, 0:2, :], conf, V["norm_a_g"], V["norm_a_b"], LN_EPS, silu=True)
            with nc.Block() as block:
                @block.vector
                def _(dve):
                    dve.tensor_copy(y[:, 0:2, :], conf[:, :, :])
        project(nc, "wo2", SEQ, y, W["w_out_2"], DC, x, residual=True)
        layer_norm(nc, "ln1", SEQ, C["ones"], x, y, V["ln1_g"], V["ln1_b"], LN_EPS)
        with Phase(nc, "pq") as pq:
            q = pq.sb("q", [P, 2 * PK_HEADS, SEQ])
            project(nc, "pqp", SEQ, y, W["peer_wq"], 2 * PK_HEADS, q)
            choose_experts(nc, C, W, q, gates_dram)
        with Phase(nc, "pf") as pf:
            f = pf.sb("f", [P, DC, SEQ])
            experts(nc, W, y, gates_dram, f)
            with nc.Block() as block:
                @block.vector
                def _(dve):
                    for c in range(DC):
                        dve.scalar_tensor_tensor(out=f[:, c, :], in0=y[:, c, :], scalar=DEEP_ALPHA, in1=f[:, c, :],
                                                 op0=ALU.mult, op1=ALU.add)
            layer_norm(nc, "ln2", SEQ, C["ones"], f, x, V["ln2_g"], V["ln2_b"], LN_EPS)
MODS = 9
U3, V3, DQ, DV_END, DZ, DAB, G3, END3 = 0, 8, 16, 40, 40, 48, 49, 65
DN = 8
DCONV = 4
DCH = 64
NDC = SEQ // DCH
GRP = 4
DN_LEVELS = (1, 2, 4, 8, 16, 32)
ROW_G, ROW_B, ROW_BG, ROW_KD = 0, 32, 64, 96
GONE = -110.0


def spatial_gating(nc, V, C, W, xn, o_a):
    with Phase(nc, "sg") as ph:
        z = ph.sb("z", [P, 2 * DC, SEQ])
        vn = ph.sb("vn", [P, DC, SEQ])
        project(nc, "sgp", SEQ, xn, W["w_in_3"][U3:DQ], 2 * DC, z)
        with nc.Block() as block:
            @block.scalar
            def _(act):
                act.activation(z[:, :, :], z[:, :, :], ACT.Gelu)
        layer_norm(nc, "sgl", SEQ, C["ones"], z[:, DC:, :], vn, V["gm_ln_g"], V["gm_ln_b"], EPS)
        with nc.Block() as block:
            w = ph.sb("w", [P, DC, P])
            bias = ph.sb("bias", [1, DC * P])
            vt = [ph.sb(f"vt{i}", [P, TILES, P]) for i in range(2)]
            turn = ph.ps("turn", [P, 2, TILES, P])
            mixed = ph.ps("mixed", [P, 2, TILES, P])
            loaded, masked, turned, turn_read, mixed_ready, mixed_read = (
                ph.sem(s) for s in ("loaded", "masked", "turned", "turn_read", "mixed_ready", "mixed_read"))

            @block.sync
            def _(sp):
                sp.dma_start(w[:, :, :], W["gm_w_s"]).then_inc(loaded, 16)
                sp.dma_start(bias[:, :], W["gm_b_s"]).then_inc(loaded, 16)

            @block.vector
            def _(dve):
                dve.wait_ge(loaded, 32)
                dve.tensor_tensor(w[:, :, :], w[:, :, :], C["upto"][:, :].unsqueeze(1).to_broadcast([P, DC, P]),
                                  ALU.mult).then_inc(masked, 1)
                for g in range(DC):
                    dve.wait_ge(mixed_ready, g + 1)
                    dve.tensor_tensor(o_a[:, g, :], z[:, g, :], mixed[:, g % 2, :, :].rearrange("p a b -> p (a b)"),
                                      ALU.mult).then_inc(mixed_read, 1)

            @block.scalar
            def _(act):
                for g in range(DC):
                    act.wait_ge(turned, g + 1)
                    if g >= 2:
                        act.wait_ge(mixed_ready, g - 1)
                    act.activation(vt[g % 2][:, :, :], turn[:, g % 2, :, :], ACT.Copy).then_inc(turn_read, 1)

            @block.tensor
            def _(pe):
                def turns(g):
                    if g >= 2:
                        pe.wait_ge(turn_read, g - 1)
                    for n in range(TILES):
                        mm = pe.transpose(turn[:, g % 2, n, :], vn[:, g, n * P:(n + 1) * P], C["ident"][:, :])
                    mm.then_inc(turned, 1)

                turns(0)
                pe.wait_ge(masked, 1)
                for g in range(DC):
                    if g + 1 < DC:
                        turns(g + 1)
                    pe.wait_ge(turn_read, g + 1)
                    if g >= 2:
                        pe.wait_ge(mixed_read, g - 1)
                    for n in range(TILES):
                        pe.matmul(mixed[:, g % 2, n, :], vt[g % 2][:, n, :], w[:, g, :], start=True, stop=False)
                        mm = pe.matmul(mixed[:, g % 2, n, :], C["ones"][0:1, :], bias[0:1, g * P:(g + 1) * P],
                                       start=False, stop=True)
                    mm.then_inc(mixed_ready, 1)


def delta_rows(nc, V, C, W, ab, rows, cols, ends):
    with Phase(nc, "dr") as ph, nc.Block() as block:
        a, e, beta = ph.sb("a", [DN, SEQ]), ph.sb("e", [DN, SEQ]), ph.sb("beta", [DN, SEQ])
        g = ph.sb("g", [DN, SEQ])
        t1, t2 = ph.sb("t1", [DN, SEQ]), ph.sb("t2", [DN, SEQ])
        keep = ph.sb("keep", [DN, SEQ])
        rate = ph.sb("rate", [DN, 1])
        turn = ph.ps("turn", [P, TILES, P])
        wide = ph.ps("wide", [P, 2, BANK])
        a_ready, log_ready, g_ready, parts_ready = (ph.sem(s) for s in ("a_ready", "log_ready", "g_ready", "parts_ready"))
        rows_ready, turned, wide_ready, wide_read = (ph.sem(s) for s in ("rows_ready", "turned", "wide_ready", "wide_read"))

        def chunked(x):
            return x[:, :].rearrange("p (n c) -> p n c", c=DCH)

        @block.vector
        def _(dve):
            dve.memset(rows[:, :], 0.0)
            dve.memset(keep[:, :], 1.0)
            dve.tensor_scalar(a[:, :], ab[0:DN, :], V["dt_bias"][0:DN, 0:1], None, ALU.add)
            dve.drain()
            dve.memset(chunked(keep)[:, :, 0:1], 0.0)
            dve.nop().then_inc(a_ready, 1)
            dve.wait_ge(log_ready, 1)
            dve.scalar_tensor_tensor(out=e[:, :], in0=a[:, :], scalar=0.0, in1=e[:, :], op0=ALU.max, op1=ALU.add)
            dve.drain()
            dve.tensor_scalar(e[:, :], e[:, :], rate[:, 0:1], -1.0, ALU.mult, ALU.mult)
            dve.drain()
            dve.tensor_scalar(e[:, :], e[:, :], GONE, None, ALU.max)
            dve.drain()
            dve.tensor_tensor_scan(g[:, :], keep[:, :], e[:, :], 0.0, ALU.mult, ALU.add)
            dve.drain()
            dve.tensor_tensor(chunked(t1), chunked(g)[:, :, DCH - 1:DCH].to_broadcast([DN, NDC, DCH]), chunked(g), ALU.subtract)
            dve.drain()
            dve.nop().then_inc(g_ready, 1)
            dve.wait_ge(parts_ready, 1)
            dve.tensor_copy(rows[ROW_G:ROW_G + DN, :], g[:, :])
            dve.tensor_copy(rows[ROW_B:ROW_B + DN, :], beta[:, :])
            dve.tensor_tensor(rows[ROW_BG:ROW_BG + DN, :], beta[:, :], t2[:, :], ALU.mult)
            dve.tensor_copy(rows[ROW_KD:ROW_KD + DN, :], t1[:, :])
            dve.drain()
            dve.nop().then_inc(rows_ready, 1)
            dve.wait_ge(turned, 1)
            dve.tensor_copy(cols[:, :, :], turn[:, :, :])
            dve.drain()

        @block.scalar
        def _(act):
            act.activation(rate[:, :], V["a_log"][0:DN, 0:1], ACT.Exp)
            act.wait_ge(a_ready, 1)
            act.activation(e[:, :], a[:, :], ACT.Abs)
            act.drain()
            act.activation(e[:, :], e[:, :], ACT.Exp, scale=-1.0)
            act.drain()
            act.activation(e[:, :], e[:, :], ACT.Ln, bias=1.0)
            act.drain()
            act.nop().then_inc(log_ready, 1)
            act.wait_ge(g_ready, 1)
            act.activation(t2[:, :], g[:, :], ACT.Exp)
            act.activation(t1[:, :], t1[:, :], ACT.Exp)
            act.activation(beta[:, :], ab[ROW_B:ROW_B + DN, :], ACT.Sigmoid)
            act.drain()
            act.nop().then_inc(parts_ready, 1)
            for h in range(DN):
                act.wait_ge(wide_ready, h + 1)
                act.activation(ends[:, h, :], wide[:, h % 2, DCH - 1:SEQ:DCH], ACT.Exp).then_inc(wide_read, 1)

        @block.tensor
        def _(pe):
            pe.wait_ge(rows_ready, 1)
            for n in range(TILES):
                mm = pe.transpose(turn[:, n, :], rows[:, n * P:(n + 1) * P], C["ident"][:, :])
            mm.then_inc(turned, 1)
            for h in range(DN):
                if h >= 2:
                    pe.wait_ge(wide_read, h - 1)
                pe.matmul(wide[:, h % 2, :], C["sel"][0:DN, h, :], rows[ROW_G:ROW_G + DN, :],
                          start=True, stop=True).then_inc(wide_ready, 1)


def delta_inputs(nc, V, C, W, xn, cv):
    n3 = 3 * DN
    with Phase(nc, "di") as ph:
        z = ph.sb("z", [P, n3, DCONV - 1 + SEQ])
        with nc.Block() as block:
            @block.gpsimd
            def _(pool):
                pool.memset(z[:, :, 0:DCONV - 1], 0.0)
        project(nc, "dip", SEQ, xn, W["w_in_3"][DQ:DV_END], n3, z[:, :, DCONV - 1:])
        with nc.Block() as block:
            conv_ready = ph.sem("conv_ready")

            @block.vector
            def _(dve):
                for k in range(DCONV):
                    for m in range(n3):
                        tap = V["conv_w"][:, n3 * k + m:n3 * k + m + 1]
                        if k == 0:
                            dve.tensor_scalar(cv[:, m, :], z[:, m, 0:SEQ], tap, None, ALU.mult)
                        else:
                            last = dve.scalar_tensor_tensor(out=cv[:, m, :], in0=z[:, m, k:k + SEQ], scalar=tap, in1=cv[:, m, :],
                                                            op0=ALU.mult, op1=ALU.add)
                            if k == DCONV - 1:
                                last.then_inc(conv_ready, 1)
                    dve.drain()

            @block.scalar
            def _(act):
                for m in range(n3):
                    act.wait_ge(conv_ready, m + 1)
                    act.activation(cv[:, m, :], cv[:, m, :], ACT.Silu)
    with Phase(nc, "dl") as ph, nc.Block() as block:
        sq = ph.sb("sq", [P, 2 * DN, SEQ])
        total = ph.ps("total", [P, 4, BANK])
        squares, total_ready, total_read, roots = (ph.sem(s) for s in ("squares", "total_ready", "total_read", "roots"))

        @block.scalar
        def _(act):
            for m in range(2 * DN):
                act.activation(sq[:, m, :], cv[:, m, :], ACT.Square).then_inc(squares, 1)
            act.wait_ge(total_read, 2 * DN)
            for m in range(2 * DN):
                act.activation(sq[:, m, :], sq[:, m, :], ACT.Sqrt).then_inc(roots, 1)

        @block.tensor
        def _(pe):
            for m in range(2 * DN):
                pe.wait_ge(squares, m + 1)
                if m >= 4:
                    pe.wait_ge(total_read, m - 3)
                pe.matmul(total[:, m % 4, :], C["ones"][:, :], sq[:, m, :], start=True, stop=True).then_inc(total_ready, 1)

        @block.vector
        def _(dve):
            for m in range(2 * DN):
                dve.wait_ge(total_ready, m + 1)
                dve.tensor_scalar(sq[:, m, :], total[:, m % 4, :], EPS, None, ALU.add).then_inc(total_read, 1)
            for m in range(2 * DN):
                dve.wait_ge(roots, m + 1)
                dve.reciprocal(sq[:, m, :], sq[:, m, :])
            dve.drain()
            for m in range(2 * DN):
                dve.scalar_tensor_tensor(out=cv[:, m, :], in0=cv[:, m, :], scalar=P ** -0.5 if m < DN else 1.0,
                                         in1=sq[:, m, :], op0=ALU.mult, op1=ALU.mult)
            dve.drain()


def delta_factors(nc, C, rows, cols, cv, qk, kd):
    with Phase(nc, "df") as ph:
        dt, at, inv, invT, tmp = (ph.sb(s, [P, GRP, SEQ]) for s in ("dt", "at", "inv", "invT", "tmp"))
        pa, pb = ph.ps("pa", [P, GRP, BANK]), ph.ps("pb", [P, GRP, BANK])

        def tiles(x):
            return x.rearrange("p (n t) -> p n t", t=P)

        def mask(i):
            return C["fmasks"][:, i, :].unsqueeze(1).to_broadcast([P, TILES, P])

        def tile(n):
            return slice(n * P, (n + 1) * P)

        for group in range(DN // GRP):
            heads = [(i, group * GRP + i) for i in range(GRP)]
            kq = lambda h: cv[:, h, :]
            kk = lambda h: cv[:, DN + h, :]
            kv = lambda h: cv[:, 2 * DN + h, :]

            with Phase(nc, f"f1{group}") as p, nc.Block() as block:
                wide, args, exps = p.sem("wide"), p.sem("args"), p.sem("exps")

                @block.tensor
                def _(pe):
                    for i, h in heads:
                        pe.matmul(pa[:, i, :], C["sel"][0:DN, h, :], rows[ROW_G:ROW_G + DN, :], start=True, stop=True)
                        pe.matmul(pb[:, i, :], C["sel"][ROW_B:ROW_B + DN, h, :], rows[ROW_B:ROW_B + DN, :],
                                  start=True, stop=True).then_inc(wide, 1)

                @block.vector
                def _(dve):
                    for i, h in heads:
                        dve.wait_ge(wide, i + 1)
                        dve.tensor_tensor(invT[:, i, :], kk(h), pb[:, i, :], ALU.mult)
                        for n in range(TILES):
                            last = dve.tensor_scalar(dt[:, i, tile(n)], pa[:, i, tile(n)], cols[:, n, ROW_G + h:ROW_G + h + 1],
                                                     0.0, ALU.subtract, ALU.min)
                        last.then_inc(args, 1)

                @block.scalar
                def _(act):
                    for i, h in heads:
                        act.wait_ge(args, i + 1)
                        act.activation(inv[:, i, :], pa[:, i, :], ACT.Exp)
                        act.activation(dt[:, i, :], dt[:, i, :], ACT.Exp)

            with Phase(nc, f"f2{group}") as p, nc.Block() as block:
                products_ready = p.sem("products")

                @block.tensor
                def _(pe):
                    for i, h in heads:
                        for n in range(TILES):
                            pe.matmul(pa[:, i, tile(n)], kk(h)[:, tile(n)], invT[:, i, tile(n)], start=True, stop=True)
                            mm = pe.matmul(pb[:, i, tile(n)], kk(h)[:, tile(n)], kq(h)[:, tile(n)], start=True, stop=True)
                        mm.then_inc(products_ready, 1)

                @block.vector
                def _(dve):
                    for i, h in heads:
                        dve.wait_ge(products_ready, i + 1)
                        dve.tensor_tensor(at[:, i, :], pa[:, i, :], dt[:, i, :], ALU.mult)
                        dve.tensor_tensor(qk[:, h, :], pb[:, i, :], dt[:, i, :], ALU.mult)
                        dve.tensor_tensor(kq(h), kq(h), inv[:, i, :], ALU.mult)
                    dve.drain()
                    for i, h in heads:
                        dve.tensor_tensor(tiles(at[:, i, :]), tiles(at[:, i, :]), mask(1), ALU.mult)
                        dve.tensor_tensor(tiles(qk[:, h, :]), tiles(qk[:, h, :]), mask(0), ALU.mult)
                    dve.drain()
                    for i, h in heads:
                        dve.tensor_tensor(tiles(dt[:, i, :]), tiles(at[:, i, :]), mask(2), ALU.mult)
                    dve.drain()
                    for i, h in heads:
                        dve.tensor_tensor(tiles(invT[:, i, :]), C["ident"][:, :].unsqueeze(1).to_broadcast([P, TILES, P]),
                                          tiles(dt[:, i, :]), ALU.subtract)
                    dve.drain()

            with Phase(nc, f"f3{group}") as p, nc.Block() as block:
                turned = p.sem("turned")

                @block.tensor
                def _(pe):
                    for i, h in heads:
                        for n in range(TILES):
                            pe.transpose(pa[:, i, tile(n)], kk(h)[:, tile(n)], C["ident"][:, :])
                            mm = pe.transpose(pb[:, i, tile(n)], kv(h)[:, tile(n)], C["ident"][:, :])
                        mm.then_inc(turned, 1)

                @block.vector
                def _(dve):
                    for i, h in heads:
                        dve.wait_ge(turned, i + 1)
                        for n in range(TILES):
                            col = lambda r: cols[:, n, r + h:r + h + 1]
                            dve.tensor_scalar(kv(h)[:, tile(n)], pb[:, i, tile(n)], col(ROW_B), None, ALU.mult)
                            dve.tensor_scalar(kk(h)[:, tile(n)], pa[:, i, tile(n)], col(ROW_BG), None, ALU.mult)
                            dve.tensor_scalar(kd[:, h, tile(n)], pa[:, i, tile(n)], col(ROW_KD), None, ALU.mult)
                    dve.drain()

            with Phase(nc, f"f4{group}") as p, nc.Block() as block:
                turned = p.sem("turned")

                @block.tensor
                def _(pe):
                    for i, h in heads:
                        for n in range(TILES):
                            mm = pe.transpose(pa[:, i, tile(n)], invT[:, i, tile(n)], C["ident"][:, :])
                        mm.then_inc(turned, 1)

                @block.scalar
                def _(act):
                    for i, h in heads:
                        act.wait_ge(turned, i + 1)
                        act.activation(inv[:, i, :], pa[:, i, :], ACT.Copy)

            for level in range(1, len(DN_LEVELS)):
                with Phase(nc, f"f5{group}{level}") as p, nc.Block() as block:
                    cut_ready, y_ready, y_copied, both_ready = (p.sem(s) for s in ("cut_ready", "y_ready", "y_copied", "both_ready"))

                    @block.vector
                    def _(dve):
                        for i, h in heads:
                            dve.tensor_tensor(tiles(dt[:, i, :]), tiles(at[:, i, :]), mask(2 + level), ALU.mult).then_inc(cut_ready, 1)
                        for i, h in heads:
                            dve.wait_ge(both_ready, i + 1)
                            dve.tensor_tensor(inv[:, i, :], inv[:, i, :], pa[:, i, :], ALU.subtract)
                            dve.tensor_tensor(invT[:, i, :], invT[:, i, :], pb[:, i, :], ALU.subtract)
                        dve.drain()

                    @block.tensor
                    def _(pe):
                        for i, h in heads:
                            pe.wait_ge(cut_ready, i + 1)
                            for n in range(TILES):
                                mm = pe.matmul(pb[:, i, tile(n)], dt[:, i, tile(n)], inv[:, i, tile(n)], start=True, stop=True)
                            mm.then_inc(y_ready, 1)
                        for i, h in heads:
                            pe.wait_ge(y_copied, i + 1)
                            for n in range(TILES):
                                pe.matmul(pa[:, i, tile(n)], invT[:, i, tile(n)], tmp[:, i, tile(n)], start=True, stop=True)
                                mm = pe.matmul(pb[:, i, tile(n)], tmp[:, i, tile(n)], invT[:, i, tile(n)], start=True, stop=True)
                            mm.then_inc(both_ready, 1)

                    @block.scalar
                    def _(act):
                        for i, h in heads:
                            act.wait_ge(y_ready, i + 1)
                            act.activation(tmp[:, i, :], pb[:, i, :], ACT.Copy).then_inc(y_copied, 1)

            with Phase(nc, f"f6{group}") as p, nc.Block() as block:
                done = p.sem("done")

                @block.tensor
                def _(pe):
                    for i, h in heads:
                        for n in range(TILES):
                            pe.matmul(pa[:, i, tile(n)], invT[:, i, tile(n)], kv(h)[:, tile(n)], start=True, stop=True)
                            mm = pe.matmul(pb[:, i, tile(n)], kk(h)[:, tile(n)], invT[:, i, tile(n)], start=True, stop=True)
                        mm.then_inc(done, 1)

                @block.scalar
                def _(act):
                    for i, h in heads:
                        act.wait_ge(done, i + 1)
                        act.activation(kv(h), pa[:, i, :], ACT.Copy)

                @block.vector
                def _(dve):
                    for i, h in heads:
                        dve.wait_ge(done, i + 1)
                        dve.tensor_copy(kk(h), pb[:, i, :])
                    dve.drain()


def delta_scan(nc, cv, qk, kd, ends, o):
    with Phase(nc, "ds") as ph, nc.Block() as block:
        state = ph.sb("state", [P, DN, P])
        vnew = ph.sb("vnew", [P, DN, P])
        ws = ph.ps("ws", [P, DN, P])
        su = ph.ps("su", [P, DN, P])
        out = ph.ps("out", [P, 2, DN, DCH])
        zeroed, ws_ready, v_ready, out_ready, state_ready, out_read = (
            ph.sem(s) for s in ("zeroed", "ws_ready", "v_ready", "out_ready", "state_ready", "out_read"))

        @block.tensor
        def _(pe):
            for n in range(NDC):
                t, lo = n // 2, DCH * (n % 2)
                rows, tok = slice(lo, lo + DCH), slice(n * DCH, (n + 1) * DCH)
                pe.wait_ge(state_ready, n + 1)
                for h in range(DN):
                    mm = pe.matmul(ws[rows, h, :], cv[:, DN + h, tok], state[:, h, :], start=True, stop=True)
                mm.then_inc(ws_ready, 1)
                pe.wait_ge(v_ready, n + 1)
                for h in range(DN):
                    mm = pe.matmul(su[:, h, :], kd[rows, h, t * P:(t + 1) * P], vnew[rows, h, :], start=True, stop=True)
                if n >= 2:
                    pe.wait_ge(out_read, n - 1)
                for h in range(DN):
                    pe.matmul(out[:, n % 2, h, :], state[:, h, :], cv[:, h, tok], start=True, stop=False)
                    mm = pe.matmul(out[:, n % 2, h, :], vnew[rows, h, :], qk[rows, h, tok], start=False, stop=True)
                mm.then_inc(out_ready, 1)

        @block.vector
        def _(dve):
            dve.memset(state[:, :, :], 0.0).then_inc(state_ready, 1)
            for n in range(NDC):
                t, lo = n // 2, DCH * (n % 2)
                rows = slice(lo, lo + DCH)
                dve.wait_ge(ws_ready, n + 1)
                dve.tensor_tensor(vnew[rows, :, :], cv[rows, 2 * DN:3 * DN, t * P:(t + 1) * P], ws[rows, :, :],
                                  ALU.subtract).then_inc(v_ready, 1)
                dve.wait_ge(out_ready, n + 1)
                for h in range(DN):
                    dve.scalar_tensor_tensor(out=state[:, h, :], in0=state[:, h, :], scalar=ends[:, h, n:n + 1],
                                             in1=su[:, h, :], op0=ALU.mult, op1=ALU.add)
                dve.drain()
                dve.nop().then_inc(state_ready, 1)

        @block.scalar
        def _(act):
            for n in range(NDC):
                act.wait_ge(out_ready, n + 1)
                act.activation(o[:, :, n * DCH:(n + 1) * DCH], out[:, n % 2, :, :], ACT.Copy).then_inc(out_read, 1)


def delta_out(nc, V, C, W, xn, o):
    with Phase(nc, "do") as ph:
        z = ph.sb("z", [P, DN, SEQ])
        project(nc, "dop", SEQ, xn, W["w_in_3"][DZ:DAB], DN, z)
        with nc.Block() as block:
            sq = ph.sb("sq", [P, DN, SEQ])
            total = ph.ps("total", [P, 4, BANK])
            squares, total_ready, total_read, roots = (ph.sem(s) for s in ("squares", "total_ready", "total_read", "roots"))

            @block.scalar
            def _(act):
                for m in range(DN):
                    act.activation(sq[:, m, :], o[:, m, :], ACT.Square).then_inc(squares, 1)
                act.activation(z[:, :, :], z[:, :, :], ACT.Silu)
                act.wait_ge(total_read, DN)
                act.activation(sq[:, :, :], sq[:, :, :], ACT.Sqrt).then_inc(roots, 1)

            @block.tensor
            def _(pe):
                for m in range(DN):
                    pe.wait_ge(squares, m + 1)
                    if m >= 4:
                        pe.wait_ge(total_read, m - 3)
                    pe.matmul(total[:, m % 4, :], C["ones"][:, :], sq[:, m, :], start=True, stop=True).then_inc(total_ready, 1)

            @block.vector
            def _(dve):
                for m in range(DN):
                    dve.wait_ge(total_ready, m + 1)
                    dve.tensor_scalar(sq[:, m, :], total[:, m % 4, :], 1.0 / P, EPS, ALU.mult, ALU.add).then_inc(total_read, 1)
                dve.wait_ge(roots, 1)
                dve.reciprocal(sq[:, :, :], sq[:, :, :])
                dve.drain()
                for m in range(DN):
                    dve.scalar_tensor_tensor(out=o[:, m, :], in0=o[:, m, :], scalar=V["dn_norm_g"][:, 0:1],
                                             in1=sq[:, m, :], op0=ALU.mult, op1=ALU.mult)
                dve.drain()
                dve.tensor_tensor(o[:, :, :], o[:, :, :], z[:, :, :], ALU.mult)
                dve.drain()


def third_block(nc, W, V, C, x, out):
    with Phase(nc, "b3") as ph:
        C = C | load(nc, ph, "c3", {k: W[k] for k in ("fmasks", "upto", "sel")})
        mod = ph.sb("mod", [P, MODS * DC, 1])
        gains = ph.sb("gains", [P, 3, DC])
        xn = ph.sb("xn", [P, DC, SEQ])
        with Phase(nc, "ad") as pa:
            c = pa.sb("c", [P, DC, 1])
            with nc.Block() as block:
                @block.scalar
                def _(act):
                    act.activation(c[:, :, 0], V["c"], ACT.Silu)
            project(nc, "ada", 1, c, W["w_ada"], MODS * DC, mod)
        with nc.Block() as block:
            @block.vector
            def _(dve):
                dve.tensor_tensor(mod[:, :, 0], mod[:, :, 0], V["b_ada"], ALU.add)
                dve.drain()
                for i, g in enumerate(("norm1_g", "norm2_g", "norm3_g")):
                    dve.scalar_tensor_tensor(out=gains[:, i, :], in0=mod[:, (3 * i + 1) * DC:(3 * i + 2) * DC, 0], scalar=1.0,
                                             in1=V[g], op0=ALU.add, op1=ALU.mult)
                    if i != 1:
                        gate = mod[:, (3 * i + 2) * DC:(3 * i + 3) * DC, 0]
                        dve.tensor_scalar(gate, gate, 0.5, None, ALU.mult)
                dve.drain()

        def shift(i):
            return mod[:, 3 * i * DC:(3 * i + 1) * DC, 0]

        def gate(i):
            return mod[:, (3 * i + 2) * DC:(3 * i + 3) * DC, :]

        def swiglu(i, w_in, w_out):
            rms_norm(nc, f"m{i}", SEQ, C["ones"], x, xn, gains[:, i, :], shift=shift(i))
            with Phase(nc, f"s{i}") as pf:
                hidden = pf.sb("hidden", [P, FC, SEQ])
                gated_up(nc, f"s{i}u", SEQ, xn, w_in[0:FC], w_in[FC:2 * FC], FC, hidden)
                project(nc, f"s{i}d", SEQ, hidden, w_out, DC, x, residual=True, column=gate(i))

        swiglu(0, W["ffn1_w_in_3"], W["ffn1_w_out_3"])
        rms_norm(nc, "m1", SEQ, C["ones"], x, xn, gains[:, 1, :], shift=shift(1))
        with Phase(nc, "mx3") as pm:
            o_a, o_b = pm.sb("o_a", [P, DC, SEQ]), pm.sb("o_b", [P, DC, SEQ])
            spatial_gating(nc, V, C, W, xn, o_a)
            with Phase(nc, "dn") as pd:
                rows, cols = pd.sb("rows", [P, SEQ]), pd.sb("cols", [P, TILES, P])
                ends = pd.sb("ends", [P, DN, NDC])
                cv = pd.sb("cv", [P, 3 * DN, SEQ])
                with Phase(nc, "ab") as pa:
                    ab = pa.sb("ab", [P, 1, SEQ])
                    project(nc, "abp", SEQ, xn, W["w_in_3"][DAB:G3], 1, ab)
                    delta_rows(nc, V, C, W, ab[:, 0, :], rows, cols, ends)
                delta_inputs(nc, V, C, W, xn, cv)
                qk, kd = pd.sb("qk", [P, DN, SEQ]), pd.sb("kd", [P, DN, SEQ])
                delta_factors(nc, C, rows, cols, cv, qk, kd)
                delta_scan(nc, cv, qk, kd, ends, o_b)
            delta_out(nc, V, C, W, xn, o_b)
            with Phase(nc, "gt") as pg:
                gates = pg.sb("gates", [P, 2 * DC, SEQ])
                mixed = pg.sb("mixed", [P, DC, SEQ])
                project(nc, "g3p", SEQ, xn, W["w_in_3"][G3:END3], 2 * DC, gates)
                with nc.Block() as block:
                    @block.scalar
                    def _(act):
                        act.activation(gates[:, :, :], gates[:, :, :], ACT.Sigmoid)
                merge(nc, "mg3", SEQ, o_a, W["w_branch"][0], gates[:, 0:DC, :], o_b, W["w_branch"][1],
                      gates[:, DC:2 * DC, :], DC, mixed)
                project(nc, "wo3", SEQ, mixed, W["w_out_3"], DC, x, residual=True, column=gate(1))
        swiglu(2, W["ffn2_w_in_3"], W["ffn2_w_out_3"])
        rms_norm(nc, "fin", SEQ, C["ones"], x, xn, V["final_g"])
        with nc.Block() as block:
            stored = ph.sem("stored")

            @block.sync
            def _(sp):
                sp.dma_start(out, xn[:, :, :]).then_inc(stored, 16)
                sp.wait_ge(stored, 16)
def tiles_of(w):
    k, n = w.shape
    return w.reshape(k // P, P, n // P, P).transpose(2, 1, 0, 3).reshape(n // P, P, k)


def columns(v):
    return v.reshape(-1, P).T


def first_constants():
    c = {}
    i = np.arange(P)
    c["ident"] = np.eye(P, dtype=np.float32)
    c["ones"] = np.ones((P, P), np.float32)
    c["ones64"] = (i[:, None] // HD == i[None, :] // HD).astype(np.float32)
    swap = np.zeros((P, P), np.float32)
    swap[i[1::2], i[0::2]] = -1.0
    swap[i[0::2], i[1::2]] = 1.0
    c["swap"] = swap
    width, theta, axis = 64, 10000.0, HD // 2
    rows = SEQ // width
    row = np.concatenate([np.zeros(META), np.repeat(np.arange(rows), width)]).astype(np.float32)
    col = np.concatenate([np.zeros(META), np.tile(np.arange(width), rows)]).astype(np.float32)
    inv = (np.float32(theta) ** (-np.arange(0, axis, 2, dtype=np.float32) / np.float32(axis))).astype(np.float32)
    angle = np.concatenate([row[:, None] * inv, col[:, None] * inv], axis=-1)
    pair = (i % HD) // 2
    c["cos"] = np.cos(angle).astype(np.float32)[:, pair].T
    c["sin"] = np.sin(angle).astype(np.float32)[:, pair].T
    s, t = i[:, None], i[None, :]
    masks = np.zeros((16, P, P), np.uint32)
    masks[0] = s == t
    for n, w in enumerate((64, 32, 16, 8, 4, 2, 1)):
        late = (s // (2 * w) == t // (2 * w)) & (s // w % 2 == 0) & (t // w % 2 == 1)
        masks[1 + n], masks[9 + n] = late, late.T
    c["masks"] = masks.transpose(1, 0, 2)
    return {k: np.ascontiguousarray(v) for k, v in c.items()}


def first_weights(a):
    w = a["w_in"][0]
    cut_at = np.cumsum([512] * 6 + [128, 128])
    k0, k1 = w[:, cut_at[5]:cut_at[5] + HD], w[:, cut_at[5] + HD:cut_at[6]]
    w_in = np.concatenate([w[:, :cut_at[5]], k0, k0, k1, k1, w[:, cut_at[6]:]], axis=1)
    weights = {"w_in": tiles_of(w_in)}
    for n in ("ffn1_w_gate", "ffn1_w_up", "ffn1_w_down", "ffn2_w_gate", "ffn2_w_up", "ffn2_w_down", "w_up_a", "w_up_b", "w_out"):
        weights[n] = tiles_of(a[n][0])
    weights["meta"] = np.ascontiguousarray(a["meta_tokens"].T.reshape(DC, P, META).transpose(1, 0, 2))
    vectors = {n: columns(a[n]) for n in ("ffn1_norm", "mix_norm", "ffn2_norm", "hg_out_norm")}
    vectors["lb"] = np.concatenate([columns(a["hg_lb_fwd"]), columns(a["hg_lb_bwd"])], axis=1)
    for n in ("q_norm", "k_norm"):
        vectors[n] = np.concatenate([a[n], a[n]], axis=1).T
    return weights, vectors


def second_constants():
    c = {}
    i = np.arange(P)
    c["iota"] = np.broadcast_to(i.astype(np.float32), (P, P))
    c["before"] = (i[None, :] < i[:, None]).astype(np.float32)
    t = np.arange(SEQ)
    count = np.stack([np.minimum(t + 1, w) for w in WINDOWS]).astype(np.float32)
    c["inv_count"] = np.repeat((np.float32(1.0) / count).reshape(2, 2, SEQ), 64, axis=1).transpose(1, 0, 2)
    return {k: np.ascontiguousarray(v) for k, v in c.items()}


def second_weights(a):
    weights = {n: tiles_of(a[n][0]) for n in ("w_in_2", "w_out_2")}
    weights["peer_wq"] = tiles_of(a["peer_wq_2"][0])
    u = a["peer_u_2"][0].reshape(P, NKEYS, DC, P)
    weights["peer_u"] = u.transpose(1, 3, 2, 0).reshape(NKEYS, P, D)
    weights["peer_v"] = a["peer_v_2"][0].reshape(P, NKEYS, D).transpose(1, 0, 2)
    weights["peer_keys"] = a["peer_keys_2"][0].reshape(2 * PK_HEADS, NKEYS, P).transpose(2, 0, 1)
    pool = np.zeros((P, 2, P), np.float32)
    for g in range(len(WINDOWS)):
        lo = 64 * (g % 2)
        pool[lo:lo + 64, g // 2, lo:lo + 64] = a["pool_w_2"][0, g]
    weights["pool_w"] = pool
    vectors = {n: columns(a[n + "_2"]) for n in ("conv_a_b", "norm_a_g", "norm_a_b", "pool_scale", "ln1_g", "ln1_b",
                                                 "ln2_g", "ln2_b", "conv_a_w", "conv_c_w")}
    return weights, vectors


def third_constants():
    c = {}
    i = np.arange(P)
    e, t = i[:, None], i[None, :]
    same = e // DCH == t // DCH
    masks = [same & (e <= t), same & (e < t)]
    for w in DN_LEVELS:
        masks.append((e // (2 * w) == t // (2 * w)) & (e // w % 2 == 0) & (t // w % 2 == 1))
    c["fmasks"] = np.stack(masks, axis=1).astype(np.float32)
    c["upto"] = (e <= t).astype(np.float32)
    sel = np.zeros((P, DN, P), np.float32)
    for h in range(DN):
        sel[h, h, :] = 1.0
        sel[ROW_B + h, h, :] = 1.0
    c["sel"] = sel
    return {k: np.ascontiguousarray(v) for k, v in c.items()}


def third_weights(a):
    weights = {n: tiles_of(a[n][0]) for n in ("ffn1_w_in_3", "ffn1_w_out_3", "ffn2_w_in_3", "ffn2_w_out_3", "w_out_3")}
    weights["w_ada"] = tiles_of(a["w_ada_3"][0])
    weights["w_branch"] = np.stack([tiles_of(a["w_branch_3"][0, i]) for i in range(2)])
    w = a["w_in_3"][0]
    small = 6 * D
    ab = np.zeros((D, P), w.dtype)
    ab[:, 0:DN], ab[:, ROW_B:ROW_B + DN] = w[:, small:small + DN], w[:, small + DN:small + 2 * DN]
    weights["w_in_3"] = tiles_of(np.concatenate([w[:, :small], ab, w[:, small + 2 * DN:]], axis=1))
    weights["gm_w_s"] = a["gm_w_s_3"][0].transpose(2, 0, 1)
    weights["gm_b_s"] = a["gm_b_s_3"].reshape(1, DC * P)
    vectors = {n: columns(a[n + "_3"]) for n in ("norm1_g", "norm2_g", "norm3_g", "final_g", "gm_ln_g", "gm_ln_b", "dn_norm_g",
                                                 "b_ada", "c", "conv_w")}
    for n in ("a_log", "dt_bias"):
        vectors[n] = np.zeros((P, 1), np.float32)
        vectors[n][0:DN, 0] = a[n + "_3"][0]
    return weights, vectors


def whole_program(nc, tensors, vector_columns, out):
    gates = nc.dram_tensor("expert_gates", [NKEYS, P, SEQ], F32).ap()
    with Phase(nc, "all") as ph:
        there = load(nc, ph, "first_load", {k: tensors[k] for k in ("vectors", "ident", "ones")})
        vectors = {k: there["vectors"][:, a:b] for k, (a, b) in vector_columns.items()}
        hidden = ph.sb("hidden", [P, DC, L])
        first_block(nc, tensors, vectors, there, tensors["x"], hidden)
        x = hidden[:, :, META:]
        second_block(nc, tensors, vectors, there, x, gates)
        third_block(nc, tensors, vectors, there, x, out)


def kernel(**inputs):
    import concourse.bacc as _bacc
    from concourse.bass_utils import run_bass_kernel_spmd as _run

    a = {k: np.asarray(v) for k, v in inputs.items()}
    tensors, vectors = {}, {}
    for weights, small in (first_weights(a), second_weights(a), third_weights(a)):
        tensors.update(weights)
        vectors.update(small)
    for constants in (first_constants(), second_constants(), third_constants()):
        tensors.update(constants)
    tensors["x"] = a["x"][0].T.reshape(DC, P, SEQ).transpose(1, 0, 2)
    ends = np.cumsum([v.shape[1] for v in vectors.values()])
    vector_columns = {k: (int(e) - v.shape[1], int(e)) for (k, v), e in zip(vectors.items(), ends)}
    tensors["vectors"] = np.concatenate(list(vectors.values()), axis=1)

    nc = _bacc.Bacc("TRN2", target_bir_lowering=False, num_devices=1)
    arrays, drams = {}, {}
    for name, t in tensors.items():
        arrays[f"in_{name}"] = np.ascontiguousarray(t)
        drams[name] = nc.dram_tensor(f"in_{name}", t.shape, mybir.dt.from_np(t.dtype), kind="ExternalInput").ap()
    out = nc.dram_tensor("out", [P, DC, SEQ], F32, kind="ExternalOutput").ap()
    whole_program(nc, drams, vector_columns, out)
    r = _run(nc, [arrays], core_ids=[0])
    got = r.results[0]["out"]
    return np.ascontiguousarray(got.transpose(1, 0, 2).reshape(D, SEQ).T)[None]
```

```python
from contextlib import ExitStack

import numpy as np
import concourse.bass as bass
from concourse import mybir

P = 128
F32 = mybir.dt.float32
U32 = mybir.dt.uint32
I32 = mybir.dt.int32
ALU = mybir.AluOpType
ACT = mybir.ActivationFunctionType
AX_X = mybir.AxisListType.X

D = 1024
DC = D // P
SEQ = 512
META = 16
L = SEQ + META
FF = 2816
FC = FF // P
EPS = 1e-6
LN_EPS = 1e-5
BANK = 512
DEEP_ALPHA = 2.0 ** 0.25


class Phase:

    def __init__(self, nc, name):
        self.nc, self.name, self.ctx, self.sems = nc, name, ExitStack(), []

    def __enter__(self):
        return self

    def __exit__(self, *error):
        if self.sems and error[0] is None:
            for s in self.sems:
                self.nc.gpsimd.sem_clear(s)
                self.nc.release_semaphore(s)
        return self.ctx.__exit__(*error)

    def sb(self, name, shape, dt=F32):
        return self.ctx.enter_context(self.nc.sbuf_tensor(f"{self.name}_{name}", shape, dt))

    def ps(self, name, shape, dt=F32):
        return self.ctx.enter_context(self.nc.psum_tensor(f"{self.name}_{name}", shape, dt))

    def sem(self, name):
        self.sems.append(self.nc.alloc_semaphore(name=f"{self.name}_{name}"))
        return self.sems[-1]


def halves(T):
    n = -(-T // BANK)
    return n, T // n


def pieces(ps, T):
    n, w = halves(T)
    return ps[:, 0:n, 0:w]


def cut(x, T):
    n, w = halves(T)
    return x.rearrange("p (n w) -> p n w", n=n)


def over_steps(eng, steps, unroll, body):
    for s in range(min(unroll, steps)):
        body(s, s, True)
    rounds = steps // unroll
    if rounds > 1:
        with eng.Fori(1, rounds) as i:
            for s in range(unroll):
                body(i * unroll + s, s, False)
    for s in range(rounds * unroll, steps):
        if s >= unroll:
            body(s, s % unroll, False)


F32R = mybir.dt.float32r
SLOTS = 2
MAX_KC = 11


def wait_from(eng, sem, count):
    if not (isinstance(count, int) and count < 1):
        eng.wait_ge(sem, count)


class Pair:

    def __init__(self, ph, name, shape):
        self.shape = shape
        self.high, self.low = ph.sb(f"{name}_high", shape, F32R), ph.sb(f"{name}_low", shape, F32R)

    def part(self, *index):
        view = Pair.__new__(Pair)
        view.high, view.low = self.high[index], self.low[index]
        view.shape = view.high.shape
        return view


def multiply(pe, out, weights, x, start, stop):
    pe.matmul(out, weights[0], x[0], start=start, stop=False)
    pe.matmul(out, weights[0], x[1], start=False, stop=False)
    return pe.matmul(out, weights[1], x[0], start=False, stop=stop)


def products(nc, ph, block, T, legs, steps):
    n, w = halves(T)
    items = []
    for l, (_, x) in enumerate(legs):
        kc = x.shape[1]
        cuts = [0, kc] if kc <= MAX_KC else [0, kc // 2, kc]
        items += [(l, a, b) for a, b in zip(cuts, cuts[1:])]
    per = len(items)
    assert per in (1, SLOTS)
    size = max(b - a for _, a, b in items) * P
    raw = [ph.sb(f"raw{s}", [P, size]) for s in range(SLOTS)]
    high = [ph.sb(f"high{s}", [P, size], F32R) for s in range(SLOTS)]
    low = [ph.sb(f"low{s}", [P, size], F32R) for s in range(SLOTS)]
    out = [[ph.ps(f"o{l}_{s}", [P, n, BANK]) for s in range(SLOTS)] for l in range(len(legs))]
    raw_in = [ph.sem(f"raw_in{s}") for s in range(SLOTS)]
    high_ready, low_ready = ph.sem("high_ready"), ph.sem("low_ready")
    item_done, results_read = ph.sem("item_done"), ph.sem("results_read")

    def slot(s, i):
        return s if per == 1 else i

    @block.sync
    def _(sp):
        def load(m, s, first):
            for i, (l, a, b) in enumerate(items):
                wait_from(sp, low_ready, m * per + i - 1)
                z = slot(s, i)
                sp.dma_start(raw[z][:, 0:(b - a) * P], legs[l][0][m][:, a * P:b * P]).then_inc(raw_in[z], 16)

        over_steps(sp, steps, SLOTS, load)

    @block.tensor
    def _(pe):
        def step(m, s, first):
            wait_from(pe, results_read, m - 1)
            for i, (l, a, b) in enumerate(items):
                z = slot(s, i)
                x = legs[l][1]
                pe.wait_ge(low_ready, m * per + i + 1)
                for j in range(n):
                    t = slice(j * w, (j + 1) * w)
                    for k in range(a, b):
                        part = slice((k - a) * P, (k - a + 1) * P)
                        mm = multiply(pe, out[l][s][:, j, 0:w], (high[z][:, part], low[z][:, part]),
                                      (x.high[:, k, t], x.low[:, k, t]), k == 0, k == x.shape[1] - 1)
                mm.then_inc(item_done, 1)

        over_steps(pe, steps, SLOTS, step)

    def round_item(act, m, s, i):
        _, a, b = items[i]
        z = slot(s, i)
        act.wait_ge(raw_in[z], 16 * (m // SLOTS + 1) if per == 1 and isinstance(m, int) else
                    (m - s) * (16 // SLOTS) + 16 if per == 1 else m * 16 + 16)
        wait_from(act, item_done, m * per + i - 1)
        act.activation(high[z][:, 0:(b - a) * P], raw[z][:, 0:(b - a) * P], ACT.Copy).then_inc(high_ready, 1)

    def subtract_item(dve, m, s, i):
        _, a, b = items[i]
        z = slot(s, i)
        dve.wait_ge(high_ready, m * per + i + 1)
        dve.tensor_tensor(low[z][:, 0:(b - a) * P], raw[z][:, 0:(b - a) * P], high[z][:, 0:(b - a) * P],
                          ALU.subtract).then_inc(low_ready, 1)

    return out, item_done, results_read, per, round_item, subtract_item


def ahead(eng, steps, prepare, finish):
    prepare(0, 0)

    def both(m, s, first):
        prepare(m + 1, (s + 1) % SLOTS)
        finish(m, s)

    if steps > 1:
        over_steps(eng, steps - 1, SLOTS, both)
    finish(steps - 1, (steps - 1) % SLOTS)


def project(nc, name, T, x, weights, steps, dst, scale=1.0, residual=False, column=None, function=None):
    with Phase(nc, name) as ph, nc.Block() as block:
        out, item_done, results_read, per, round_item, subtract_item = products(nc, ph, block, T, [(weights, x)], steps)

        @block.scalar
        def _(act):
            def apply(m, s):
                act.wait_ge(item_done, (m + 1) * per)
                act.wait_ge(item_done, 1)
                act.activation(cut(dst[:, m, :], T), pieces(out[0][s], T), function).then_inc(results_read, 1)

            if function is None:
                over_steps(act, steps, SLOTS, lambda m, s, first: [round_item(act, m, s, i) for i in range(per)])
            else:
                ahead(act, steps, lambda m, s: [round_item(act, m, s, i) for i in range(per)], apply)

        @block.vector
        def _(dve):
            def take(m, s):
                dve.wait_ge(item_done, (m + 1) * per)
                to = cut(dst[:, m, :], T)
                factor = scale if column is None else column[:, m, :]
                if residual:
                    dve.scalar_tensor_tensor(out=to, in0=pieces(out[0][s], T), scalar=factor, in1=to,
                                             op0=ALU.mult, op1=ALU.add).then_inc(results_read, 1)
                else:
                    dve.tensor_scalar(to, pieces(out[0][s], T), factor, None,
                                      ALU.mult).then_inc(results_read, 1)

            if function is None:
                ahead(dve, steps, lambda m, s: [subtract_item(dve, m, s, i) for i in range(per)], take)
            else:
                over_steps(dve, steps, SLOTS, lambda m, s, first: [subtract_item(dve, m, s, i) for i in range(per)])


def store_pair(dve, pair, m, value):
    dve.tensor_scalar(pair.high[:, m, :], value, 1.0, None, ALU.mult)
    dve.drain()
    return dve.tensor_tensor(pair.low[:, m, :], value, pair.high[:, m, :], ALU.subtract)


def gated_up(nc, name, T, x, w_gate, w_up, steps, hidden):
    with Phase(nc, name) as ph, nc.Block() as block:
        out, item_done, results_read, per, round_item, subtract_item = products(
            nc, ph, block, T, [(w_gate, x), (w_up, x)], steps)
        gate = [ph.sb(f"gate{s}", [P, T]) for s in range(SLOTS)]
        gate_ready = ph.sem("gate_ready")

        @block.scalar
        def _(act):
            def silu(m, s):
                act.wait_ge(item_done, m * per + 1)
                wait_from(act, results_read, m - 1)
                act.activation(cut(gate[s][:, :], T), pieces(out[0][s], T), ACT.Silu).then_inc(gate_ready, 1)

            ahead(act, steps, lambda m, s: [round_item(act, m, s, i) for i in range(per)], silu)

        @block.vector
        def _(dve):
            def times(m, s):
                dve.wait_ge(gate_ready, m + 1)
                dve.wait_ge(item_done, (m + 1) * per)
                dve.tensor_tensor(cut(gate[s][:, :], T), pieces(out[1][s], T), cut(gate[s][:, :], T), ALU.mult)
                dve.drain()
                store_pair(dve, hidden, m, gate[s][:, :]).then_inc(results_read, 1)

            ahead(dve, steps, lambda m, s: [subtract_item(dve, m, s, i) for i in range(per)], times)


def merge(nc, name, T, xa, wa, ga, xb, wb, gb, steps, dst):
    with Phase(nc, name) as ph, nc.Block() as block:
        out, item_done, results_read, per, round_item, subtract_item = products(
            nc, ph, block, T, [(wa, xa), (wb, xb)], steps)
        part = [ph.sb(f"part{i}", [P, T]) for i in range(2)]

        @block.scalar
        def _(act):
            over_steps(act, steps, SLOTS, lambda m, s, first: [round_item(act, m, s, i) for i in range(per)])

        @block.vector
        def _(dve):
            def add(m, s):
                dve.wait_ge(item_done, (m + 1) * per)
                dve.tensor_tensor(cut(part[0][:, :], T), pieces(out[0][s], T), cut(ga[:, m, :], T), ALU.mult)
                dve.tensor_tensor(cut(part[1][:, :], T), pieces(out[1][s], T), cut(gb[:, m, :], T), ALU.mult)
                dve.drain()
                dve.tensor_tensor(part[0][:, :], part[0][:, :], part[1][:, :], ALU.add)
                dve.drain()
                store_pair(dve, dst, m, part[0][:, :]).then_inc(results_read, 1)
                dve.drain()

            ahead(dve, steps, lambda m, s: [subtract_item(dve, m, s, i) for i in range(per)], add)


def split(nc, name, x, pair):
    with Phase(nc, name) as ph, nc.Block() as block:
        rounded = ph.sem("rounded")

        @block.scalar
        def _(act):
            for c in range(x.shape[1]):
                act.activation(pair.high[:, c, :], x[:, c, :], ACT.Copy).then_inc(rounded, 1)

        @block.vector
        def _(dve):
            for c in range(x.shape[1]):
                dve.wait_ge(rounded, c + 1)
                dve.tensor_tensor(pair.low[:, c, :], x[:, c, :], pair.high[:, c, :], ALU.subtract)


def fold(dve, sums, chunks):
    while chunks > 1:
        chunks //= 2
        last = dve.tensor_tensor(sums[:, 0:chunks, :], sums[:, 0:chunks, :], sums[:, chunks:2 * chunks, :], ALU.add)
        if chunks > 1:
            dve.drain()
    return last


def rms_norm(nc, name, T, ones, x, dst, gain, shift=None, eps=EPS, plain=None):
    n, w = halves(T)
    chunks = x.shape[1]
    with Phase(nc, name) as ph, nc.Block() as block:
        root = ph.sb("root", [P, T])
        tmp = ph.sb("tmp", [P, chunks, T])
        total = ph.ps("total", [P, n, BANK])
        squares_ready, sums_ready, total_ready = ph.sem("squares_ready"), ph.sem("sums_ready"), ph.sem("total_ready")
        mean_ready, root_ready = ph.sem("mean_ready"), ph.sem("root_ready")
        scaled, rounded = ph.sem("scaled"), ph.sem("rounded")

        @block.scalar
        def _(act):
            act.activation(tmp[:, chunks // 2:chunks, :], x[:, chunks // 2:chunks, :], ACT.Square).then_inc(squares_ready, 1)
            act.wait_ge(mean_ready, 1)
            act.activation(root[:, :], root[:, :], ACT.Sqrt).then_inc(root_ready, 1)
            if plain is None:
                for c in range(chunks):
                    act.wait_ge(scaled, c + 1)
                    act.activation(dst.high[:, c, :], tmp[:, c, :], ACT.Copy).then_inc(rounded, 1)

        @block.tensor
        def _(pe):
            pe.wait_ge(sums_ready, 1)
            for j in range(n):
                mm = pe.matmul(total[:, j, 0:w], ones[:, :], tmp[:, 0, j * w:(j + 1) * w], start=True, stop=True)
            mm.then_inc(total_ready, 1)

        @block.vector
        def _(dve):
            first_half = slice(0, chunks // 2)
            dve.tensor_tensor(tmp[:, first_half, :], x[:, first_half, :], x[:, first_half, :], ALU.mult)
            dve.drain()
            dve.wait_ge(squares_ready, 1)
            fold(dve, tmp, chunks).then_inc(sums_ready, 1)
            dve.wait_ge(total_ready, 1)
            dve.tensor_scalar(cut(root[:, :], T), pieces(total, T), 1.0 / (chunks * P), eps,
                              ALU.mult, ALU.add).then_inc(mean_ready, 1)
            dve.wait_ge(root_ready, 1)
            dve.reciprocal(root[:, :], root[:, :])
            dve.drain()
            to = tmp if plain is None else plain
            for c in range(chunks):
                last = dve.scalar_tensor_tensor(out=to[:, c, :], in0=x[:, c, :], scalar=gain[:, c:c + 1],
                                                in1=root[:, :], op0=ALU.mult, op1=ALU.mult)
                if shift is not None:
                    dve.drain()
                    last = dve.tensor_scalar(to[:, c, :], to[:, c, :], shift[:, c:c + 1], None, ALU.add)
                last.then_inc(scaled, 1)
            if plain is None:
                for c in range(chunks):
                    dve.wait_ge(rounded, c + 1)
                    dve.tensor_tensor(dst.low[:, c, :], tmp[:, c, :], dst.high[:, c, :], ALU.subtract)
            dve.drain()


def layer_norm(nc, name, T, ones, x, dst, gain, shift, eps, silu=False):
    chunks = x.shape[1]
    with Phase(nc, name) as ph, nc.Block() as block:
        root = ph.sb("root", [P, T])
        mean = ph.sb("mean", [P, T])
        total = ph.ps("total", [P, 2, BANK])
        sums_ready, mean_ready, centred, squares_ready = (ph.sem(s) for s in ("sums_ready", "mean_ready", "centred", "squares_ready"))
        total_ready, root_ready, scaled = ph.sem("total_ready"), ph.sem("root_ready"), ph.sem("scaled")
        half = chunks // 2

        @block.tensor
        def _(pe):
            for i in range(2):
                pe.wait_ge(sums_ready, i + 1)
                pe.matmul(total[:, i, 0:T], ones[:, :], dst[:, 0, :], start=True, stop=True).then_inc(total_ready, 1)

        @block.scalar
        def _(act):
            for c in range(chunks):
                act.wait_ge(centred, c + 1)
                act.activation(dst[:, c, :], x[:, c, :], ACT.Square).then_inc(squares_ready, 1)
            act.wait_ge(mean_ready, 1)
            act.activation(root[:, :], root[:, :], ACT.Sqrt).then_inc(root_ready, 1)
            if silu:
                for c in range(chunks):
                    act.wait_ge(scaled, c + 1)
                    act.activation(dst[:, c, :], dst[:, c, :], ACT.Silu)

        @block.vector
        def _(dve):
            first = dve.tensor_tensor(dst[:, 0:half, :], x[:, 0:half, :], x[:, half:chunks, :], ALU.add)
            if half > 1:
                dve.drain()
                first = fold(dve, dst, half)
            first.then_inc(sums_ready, 1)
            dve.wait_ge(total_ready, 1)
            dve.tensor_scalar(mean[:, :], total[:, 0, 0:T], 1.0 / (chunks * P), None, ALU.mult)
            dve.drain()
            for c in range(chunks):
                dve.tensor_tensor(x[:, c, :], x[:, c, :], mean[:, :], ALU.subtract).then_inc(centred, 1)
            dve.wait_ge(squares_ready, chunks)
            fold(dve, dst, chunks).then_inc(sums_ready, 1)
            dve.wait_ge(total_ready, 2)
            dve.tensor_scalar(root[:, :], total[:, 1, 0:T], 1.0 / (chunks * P), eps,
                              ALU.mult, ALU.add).then_inc(mean_ready, 1)
            dve.wait_ge(root_ready, 1)
            dve.reciprocal(root[:, :], root[:, :])
            dve.drain()
            for c in range(chunks):
                dve.scalar_tensor_tensor(out=dst[:, c, :], in0=x[:, c, :], scalar=gain[:, c:c + 1],
                                         in1=root[:, :], op0=ALU.mult, op1=ALU.mult)
            dve.drain()
            for c in range(chunks):
                dve.tensor_scalar(dst[:, c, :], dst[:, c, :], shift[:, c:c + 1], None, ALU.add).then_inc(scaled, 1)
            dve.drain()


def load(nc, ph, name, sources):
    there = {k: ph.sb(k, list(v.shape), v.dtype) for k, v in sources.items()}
    with Phase(nc, name) as p, nc.Block() as block:
        loaded = p.sem("loaded")

        @block.sync
        def _(sp):
            for k, v in sources.items():
                sp.dma_start(there[k][:], v).then_inc(loaded, 16)
            sp.wait_ge(loaded, 16 * len(sources))

    return there


def head_norms(nc, name, T, C, sides, factors, mean, gate=None):
    heads, n = sides[0].shape[1], len(sides)
    parts, w = halves(T)
    with Phase(nc, name) as ph, nc.Block() as block:
        sq = ph.sb("sq", [P, n, heads, T])
        root = ph.sb("root", [heads, n, T])
        total = ph.ps("total", [heads, n, parts, BANK])
        wide = ph.ps("wide", [P, 2, parts, BANK])
        squares, total_ready, mean_ready, root_ready, inverse_ready, wide_ready, wide_read = (
            ph.sem(s) for s in ("squares", "total_ready", "mean_ready", "root_ready", "inverse_ready", "wide_ready", "wide_read"))

        @block.scalar
        def _(act):
            for i, side in enumerate(sides):
                for h in range(heads):
                    act.activation(sq[:, i, h, :], side[:, h, :], ACT.Square).then_inc(squares, 1)
            act.wait_ge(mean_ready, n)
            act.activation(root[:, :, :], root[:, :, :], ACT.Sqrt).then_inc(root_ready, 1)

        @block.tensor
        def _(pe):
            for i in range(n):
                for h in range(heads):
                    pe.wait_ge(squares, i * heads + h + 1)
                    for j in range(parts):
                        mm = pe.matmul(total[:, i, j, 0:w], C["pick"][:, h, 0:heads], sq[:, i, h, j * w:(j + 1) * w],
                                       start=h == 0, stop=h == heads - 1)
            mm.then_inc(total_ready, 1)
            pe.wait_ge(inverse_ready, 1)
            for i in range(n):
                for h in range(heads):
                    k = i * heads + h
                    if k >= 2:
                        pe.wait_ge(wide_read, k - 1)
                    for j in range(parts):
                        mm = pe.matmul(wide[:, k % 2, j, 0:w], C["sel"][0:heads, h, :], root[:, i, j * w:(j + 1) * w],
                                       start=True, stop=True)
                    mm.then_inc(wide_ready, 1)

        @block.vector
        def _(dve):
            dve.wait_ge(total_ready, 1)
            for i in range(n):
                dve.tensor_scalar(cut(root[:, i, :], T), total[:, i, :, 0:w], mean, EPS, ALU.mult, ALU.add).then_inc(mean_ready, 1)
            dve.wait_ge(root_ready, 1)
            dve.reciprocal(root[:, :, :], root[:, :, :]).then_inc(inverse_ready, 1)
            for i, side in enumerate(sides):
                for h in range(heads):
                    k = i * heads + h
                    dve.wait_ge(wide_ready, k + 1)
                    dve.scalar_tensor_tensor(out=cut(side[:, h, :], T), in0=cut(side[:, h, :], T), scalar=factors[i](h),
                                             in1=wide[:, k % 2, :, 0:w], op0=ALU.mult, op1=ALU.mult).then_inc(wide_read, 1)
                if gate is not None:
                    dve.drain()
                    dve.tensor_tensor(side[:, :, :], side[:, :, :], gate, ALU.mult)
            dve.drain()
HG = 4
CH = 128
NCH = 5
LP = NCH * CH
PADN = LP - L
AT_T = 88
AT_N = L // AT_T
AT_HEADS = 8
HD = 64
Z_Q, Z_I, Z_FF, Z_FB, Z_G, Z_END = 0, 4, 8, 12, 16, 20
A_Q, A_K, A_V, A_END = 0, 4, 6, 7
Z_GATES = Z_END + A_END


def hgrn(nc, V, C, W, z, y):
    width = HG * LP
    with Phase(nc, "hg") as ph:
        q, va, kf, kb = (z[:, c:c + HG, :].rearrange("p h t -> p (h t)") for c in (Z_Q, Z_I, Z_FF, Z_FB))
        lf, bsum = ph.sb("lf", [P, width]), ph.sb("bsum", [P, width])
        qe, ke = ph.sb("qe", [P, width]), ph.sb("ke", [P, width])
        vt = ph.sb("vt", [P, HG * NCH, P])
        attn = ph.sb("attn", [P, HG * NCH, P])
        state = ph.sb("state", [P, HG, P])
        decay = ph.sb("decay", [P, HG * NCH])
        lb = ph.sb("lb", [P, 2, HG])
        reset = ph.sb("reset", [P, LP])
        levels = [64, 32, 16, 8, 4, 2, 1]

        def tok(a):
            return a[:, :].rearrange("p (h t) -> p h t", h=HG)

        with Phase(nc, "hg_in") as p1, nc.Block() as block:
            edge = p1.sb("edge", [P, 4, HG])
            tr = p1.ps("tr", [P, 2, 4, P])
            padded, e_ready, s_ready, v_ready = p1.sem("padded"), p1.sem("e_ready"), p1.sem("s_ready"), p1.sem("v_ready")
            transposed, copied = p1.sem("transposed"), p1.sem("copied")
            top = p1.sb("top", [P, 2, HG])

            @block.scalar
            def _(act):
                act.wait_ge(e_ready, 1)
                act.activation(edge[:, :, :], edge[:, :, :], ACT.Exp).then_inc(s_ready, 1)
                act.activation(tok(kf)[:, :, PADN:], tok(kf)[:, :, PADN:], ACT.Sigmoid, scale=-1.0).then_inc(s_ready, 1)
                act.activation(tok(kb)[:, :, PADN:], tok(kb)[:, :, PADN:], ACT.Sigmoid, scale=-1.0).then_inc(s_ready, 1)
                act.activation(tok(q)[:, :, PADN:], tok(q)[:, :, PADN:], ACT.Silu)
                act.activation(z[:, Z_G:Z_G + HG, PADN:], z[:, Z_G:Z_G + HG, PADN:], ACT.Silu)
                act.drain()

            @block.vector
            def _(dve):
                for a in (kf, kb, q, va):
                    dve.memset(tok(a)[:, :, 0:PADN], 0.0)
                dve.memset(reset[:, :], 1.0)
                dve.memset(qe[:, :], 0.0)
                dve.memset(ke[:, :], 0.0)
                dve.drain()
                dve.memset(reset[:, :].rearrange("p (n t) -> p n t", t=CH)[:, :, 0:1], 0.0).then_inc(v_ready, 1)
                for d in range(2):
                    dve.tensor_tensor(top[:, d, :], V["lb"][:, 8 * d:8 * d + 4], V["lb"][:, 8 * d + 4:8 * d + 8], ALU.max)
                dve.drain()
                for d in range(2):
                    for r in range(2):
                        dve.tensor_tensor(edge[:, 2 * d + r, :], V["lb"][:, 8 * d + 4 * r:8 * d + 4 * r + 4],
                                          top[:, d, :], ALU.subtract)
                dve.drain()
                dve.nop().then_inc(e_ready, 1)
                dve.wait_ge(s_ready, 1)
                for d in range(2):
                    dve.tensor_tensor(top[:, d, :], edge[:, 2 * d, :], edge[:, 2 * d + 1, :], ALU.add)
                dve.drain()
                dve.reciprocal(top[:, :, :], top[:, :, :])
                dve.drain()
                for d in range(2):
                    dve.tensor_tensor(lb[:, d, :], edge[:, 2 * d, :], top[:, d, :], ALU.mult)
                dve.drain()
                dve.tensor_scalar(lb[:, :, :], lb[:, :, :], -1.0, 1.0, ALU.mult, ALU.add)
                dve.drain()
                for d, k in enumerate((kf, kb)):
                    dve.wait_ge(s_ready, 2 + d)
                    for h in range(HG):
                        dve.tensor_scalar(tok(k)[:, h, PADN:], tok(k)[:, h, PADN:], lb[:, d, h:h + 1], None, ALU.mult)
                for g in range(HG * NCH // 4):
                    dve.wait_ge(transposed, g + 1)
                    dve.tensor_copy(vt[:, 4 * g:4 * g + 4, :], tr[:, g % 2, :, :]).then_inc(copied, 1)
                dve.drain()

            @block.tensor
            def _(pe):
                pe.wait_ge(v_ready, 1)
                for g in range(HG * NCH // 4):
                    if g >= 2:
                        pe.wait_ge(copied, g - 1)
                    for i in range(4):
                        n = 4 * g + i
                        mm = pe.transpose(tr[:, g % 2, i, :], va[:, n * CH:(n + 1) * CH], C["ident"][:, :])
                    mm.then_inc(transposed, 1)

        def sequence(direction):
            k = kf if direction == 0 else kb
            with Phase(nc, f"hg_b{direction}") as p2, nc.Block() as block:
                key_ready, log_ready = p2.sem("key_ready"), p2.sem("log_ready")

                @block.scalar
                def _(act):
                    act.activation(lf[:, :], k[:, :], ACT.Ln, bias=1.0, scale=-1.0).then_inc(log_ready, 1)

                @block.vector
                def _(dve):
                    dve.wait_ge(log_ready, 1)
                    for h in range(HG):
                        row = slice(h * LP, (h + 1) * LP)
                        dve.tensor_tensor_scan(bsum[:, row], reset[:, :], lf[:, row], 0.0, ALU.mult, ALU.add)
                    dve.drain()
                    if direction == 1:
                        dve.tensor_tensor(lf[:, :], bsum[:, :], lf[:, :], ALU.subtract)
                        dve.drain()

            todo = [0] + levels if direction == 0 else levels
            with Phase(nc, f"hg_l{direction}") as p3, nc.Block() as block:
                sc = p3.ps("sc", [P, 5, 4, P])
                args_ready, exp_ready, factors_ready = p3.sem("args_ready"), p3.sem("exp_ready"), p3.sem("factors_ready")
                scores_ready, scores_read = p3.sem("scores_ready"), p3.sem("scores_read")
                groups = HG * NCH // 4

                @block.scalar
                def _(act):
                    n = 0
                    for w in todo:
                        if w:
                            for i in range(2):
                                n += 1
                                act.wait_ge(args_ready, n)
                                factor = (qe if i == direction else ke)[:, :].rearrange(
                                    "p (n two w) -> p n two w", two=2, w=w)[:, :, 1 - i, :]
                                act.activation(factor, factor, ACT.Exp).then_inc(exp_ready, 1)

                @block.vector
                def _(dve):
                    n = 0
                    for j, w in enumerate(todo):
                        if j:
                            dve.wait_ge(scores_ready, groups * j)
                        if w == 0:
                            dve.tensor_copy(qe[:, :], q[:, :])
                            dve.tensor_tensor(ke[:, :], kf[:, :], kb[:, :], ALU.add).then_inc(factors_ready, 1)
                        else:
                            def half(a, i):
                                return a[:, :].rearrange("p (n two w) -> p n two w", two=2, w=w)[:, :, i, :]

                            mid = bsum[:, :].rearrange("p (n two w) -> p n two w", two=2, w=w)[:, :, 0, w - 1:w]
                            mid = mid.to_broadcast([P, width // (2 * w), w])
                            late, early = (bsum, bsum) if direction == 0 else (lf, lf)
                            late_of, early_of = ((q, qe), (k, ke)) if direction == 0 else ((k, ke), (q, qe))
                            a0, a1 = half(late_of[1], 1), half(early_of[1], 0)
                            dve.tensor_tensor(a0, half(late, 1), mid, ALU.subtract).then_inc(args_ready, 1)
                            dve.tensor_tensor(a1, mid, half(early, 0), ALU.subtract).then_inc(args_ready, 1)
                            n += 2
                            dve.wait_ge(exp_ready, n - 1)
                            dve.tensor_tensor(a0, half(late_of[0], 1), a0, ALU.mult)
                            dve.wait_ge(exp_ready, n)
                            dve.tensor_tensor(a1, half(early_of[0], 0), a1, ALU.mult)
                            dve.drain()
                            dve.nop().then_inc(factors_ready, 1)
                        mask = C["masks"][:, (direction * 8 if w else 0) + (levels.index(w) + 1 if w else 0), :]
                        for g in range(groups):
                            dve.wait_ge(scores_ready, groups * j + g + 1)
                            dve.copy_predicated(attn[:, 4 * g:4 * g + 4, :], mask.unsqueeze(1).to_broadcast([P, 4, P]),
                                                sc[:, g, :, :]).then_inc(scores_read, 1)
                        dve.drain()

                @block.tensor
                def _(pe):
                    for j, w in enumerate(todo):
                        pe.wait_ge(factors_ready, j + 1)
                        for g in range(groups):
                            if j:
                                pe.wait_ge(scores_read, groups * (j - 1) + g + 1)
                            for i in range(4):
                                c = slice((4 * g + i) * CH, (4 * g + i + 1) * CH)
                                mm = pe.matmul(sc[:, g, i, :], ke[:, c], qe[:, c], start=True, stop=True)
                            mm.then_inc(scores_ready, 1)

            with Phase(nc, f"hg_s{direction}") as p4, nc.Block() as block:
                kt = p4.sb("kt", [P, HG * NCH, P])
                tr = p4.ps("tr", [P, 2, 4, P])
                so = p4.ps("so", [P, HG, P])
                su = p4.ps("su", [P, HG, P])
                args_ready, exp_ready, k_ready = p4.sem("args_ready"), p4.sem("exp_ready"), p4.sem("k_ready")
                transposed, copied = p4.sem("transposed"), p4.sem("copied")
                done, taken, grown = p4.sem("done"), p4.sem("taken"), p4.sem("grown")
                chunked = [a[:, :].rearrange("p (n t) -> p n t", t=CH) for a in (bsum, lf, qe, ke)]
                last = chunked[0][:, :, CH - 1:CH].to_broadcast([P, HG * NCH, CH])
                order = list(range(NCH)) if direction == 0 else list(range(NCH - 1, -1, -1))

                @block.scalar
                def _(act):
                    act.wait_ge(args_ready, 1)
                    act.activation(qe[:, :], qe[:, :], ACT.Exp).then_inc(exp_ready, 1)
                    act.activation(ke[:, :], ke[:, :], ACT.Exp).then_inc(exp_ready, 1)
                    act.activation(decay[:, :], chunked[0][:, :, CH - 1], ACT.Exp).then_inc(exp_ready, 1)

                @block.vector
                def _(dve):
                    if direction == 0:
                        dve.tensor_copy(qe[:, :], bsum[:, :])
                        dve.tensor_tensor(chunked[3], last, chunked[0], ALU.subtract)
                    else:
                        dve.tensor_tensor(chunked[2], last, chunked[1], ALU.subtract)
                        dve.tensor_copy(ke[:, :], lf[:, :])
                    dve.memset(state[:, :, :], 0.0)
                    dve.drain()
                    dve.nop().then_inc(args_ready, 1)
                    dve.wait_ge(exp_ready, 3)
                    dve.tensor_tensor(ke[:, :], ke[:, :], k[:, :], ALU.mult)
                    dve.tensor_tensor(qe[:, :], qe[:, :], q[:, :], ALU.mult)
                    dve.drain()
                    dve.nop().then_inc(k_ready, 1)
                    for g in range(HG * NCH // 4):
                        dve.wait_ge(transposed, g + 1)
                        dve.tensor_copy(kt[:, 4 * g:4 * g + 4, :], tr[:, g % 2, :, :]).then_inc(copied, 1)
                    for i, c in enumerate(order):
                        lo = PADN if c == 0 else 0
                        t0 = c * CH + lo - PADN
                        dve.wait_ge(done, i + 1)
                        part = y[:, :, t0:t0 + CH - lo]
                        if direction == 0:
                            dve.tensor_copy(part, so[:, :, lo:])
                        else:
                            dve.tensor_tensor(part, part, so[:, :, lo:], ALU.add)
                        for h in range(HG):
                            dve.scalar_tensor_tensor(out=state[:, h, :], in0=state[:, h, :],
                                                     scalar=decay[:, h * NCH + c:h * NCH + c + 1],
                                                     in1=su[:, h, :], op0=ALU.mult, op1=ALU.add)
                        dve.drain()
                        dve.nop().then_inc(grown, 1)

                @block.tensor
                def _(pe):
                    pe.wait_ge(k_ready, 1)
                    for g in range(HG * NCH // 4):
                        if g >= 2:
                            pe.wait_ge(copied, g - 1)
                        for i in range(4):
                            n = 4 * g + i
                            mm = pe.transpose(tr[:, g % 2, i, :], ke[:, n * CH:(n + 1) * CH], C["ident"][:, :])
                        mm.then_inc(transposed, 1)
                    pe.wait_ge(copied, HG * NCH // 4)
                    for i, c in enumerate(order):
                        if i:
                            pe.wait_ge(grown, i)
                        for h in range(HG):
                            n = h * NCH + c
                            pe.matmul(so[:, h, :], state[:, h, :], qe[:, n * CH:(n + 1) * CH], start=True,
                                      stop=(direction == 0))
                            if direction == 1:
                                pe.matmul(so[:, h, :], vt[:, n, :], attn[:, n, :], start=False, stop=True)
                            mm = pe.matmul(su[:, h, :], kt[:, n, :], vt[:, n, :], start=True, stop=True)
                        mm.then_inc(done, 1)

        sequence(0)
        sequence(1)

    with Phase(nc, "hgo") as ph:
        C = C | load(nc, ph, "hgc", {k: W[k] for k in ("pick", "sel")})
        head_norms(nc, "hg_n", L, C, [y], [lambda h: V["hg_out_norm"][:, h:h + 1]], 1.0 / P,
                   gate=z[:, Z_G:Z_G + HG, PADN:])


def gqa(nc, V, C, z, y):
    n, w = halves(L)
    qk = z[:, A_Q:A_Q + 6, :]
    with Phase(nc, "at_n") as ph, nc.Block() as block:
        sq = ph.sb("sq", [P, 6, L])
        total = ph.ps("total", [P, 2, n, BANK])
        swap = ph.ps("swap", [P, 2, n, BANK])
        squares_ready, total_ready, mean_ready, root_ready = (ph.sem(s) for s in ("squares", "total", "mean", "root"))
        normed, swapped, rotated = ph.sem("normed"), ph.sem("swapped"), ph.sem("rotated")

        @block.scalar
        def _(act):
            act.activation(sq[:, :, :], qk, ACT.Square).then_inc(squares_ready, 1)
            act.wait_ge(mean_ready, 6)
            act.activation(sq[:, :, :], sq[:, :, :], ACT.Sqrt).then_inc(root_ready, 1)

        @block.tensor
        def _(pe):
            pe.wait_ge(squares_ready, 1)
            for c in range(6):
                if c >= 2:
                    pe.wait_ge(mean_ready, c - 1)
                for j in range(n):
                    mm = pe.matmul(total[:, c % 2, j, 0:w], C["ones64"][:, :], sq[:, c, j * w:(j + 1) * w], start=True, stop=True)
                mm.then_inc(total_ready, 1)
            pe.wait_ge(normed, 1)
            for c in range(6):
                if c >= 2:
                    pe.wait_ge(rotated, c - 1)
                for j in range(n):
                    mm = pe.matmul(swap[:, c % 2, j, 0:w], C["swap"][:, :], z[:, A_Q + c, j * w:(j + 1) * w], start=True, stop=True)
                mm.then_inc(swapped, 1)

        @block.vector
        def _(dve):
            for c in range(6):
                dve.wait_ge(total_ready, c + 1)
                dve.tensor_scalar(cut(sq[:, c, :], L), total[:, c % 2, :, 0:w], 1.0 / HD, EPS, ALU.mult,
                                  ALU.add).then_inc(mean_ready, 1)
            dve.wait_ge(root_ready, 1)
            dve.reciprocal(sq[:, :, :], sq[:, :, :])
            dve.drain()
            for c in range(6):
                gain = V["q_norm"] if c < 4 else V["k_norm"]
                dve.scalar_tensor_tensor(out=qk[:, c, :], in0=qk[:, c, :], scalar=gain[:, 0:1],
                                         in1=sq[:, c, :], op0=ALU.mult, op1=ALU.mult)
            dve.drain()
            dve.nop().then_inc(normed, 1)
            for c in range(6):
                dve.wait_ge(swapped, c + 1)
                dve.tensor_tensor(cut(sq[:, c, :], L), swap[:, c % 2, :, 0:w], cut(C["sin"][:, :], L), ALU.mult).then_inc(rotated, 1)
                dve.tensor_tensor(qk[:, c, :], qk[:, c, :], C["cos"][:, :], ALU.mult)
            dve.drain()
            dve.tensor_tensor(qk, qk, sq[:, :, :], ALU.add)
            dve.drain()

    with Phase(nc, "at") as ph, nc.Block() as block:
        vt = ph.sb("vt", [AT_T, AT_N, P])
        probs = [ph.sb(f"probs{i}", [AT_T, L]) for i in range(2)]
        pT = [ph.sb(f"pT{i}", [AT_T, AT_N, L]) for i in range(2)]
        top, total = ph.sb("top", [AT_T, 2]), ph.sb("total", [AT_T, 2])
        sc = [ph.ps(f"sc{i}", [AT_T, n, BANK]) for i in range(2)]
        turn = ph.ps("turn", [AT_T, 2, BANK])
        out = ph.ps("out", [P, n, BANK])
        scores_ready, exp_ready, probs_ready = ph.sem("scores_ready"), ph.sem("exp_ready"), ph.sem("probs_ready")
        max_ready, turned, turn_read = ph.sem("max_ready"), ph.sem("turned"), ph.sem("turn_read")
        out_ready, out_read = ph.sem("out_ready"), ph.sem("out_read")
        v_turned, v_read = ph.sem("v_turned"), ph.sem("v_read")
        tiles = AT_HEADS * AT_N
        half = AT_N // 2

        @block.tensor
        def _(pe):
            for j in range(AT_N):
                mm = pe.transpose(out[0:AT_T, j // 3, (j % 3) * P:(j % 3 + 1) * P], z[:, A_V, j * AT_T:(j + 1) * AT_T],
                                  C["ident"][:, :])
            mm.then_inc(v_turned, 1)
            pe.wait_ge(v_read, 1)

            def scores(i):
                h, t = divmod(i, AT_N)
                lo = HD * (h % 2)
                if i >= 2:
                    pe.wait_ge(exp_ready, i - 1)
                for j in range(n):
                    mm = pe.matmul(sc[i % 2][:, j, 0:w], z[lo:lo + HD, A_Q + h // 2, t * AT_T:(t + 1) * AT_T],
                                   z[lo:lo + HD, A_K + h // 4, j * w:(j + 1) * w], start=True, stop=True)
                mm.then_inc(scores_ready, 1)

            def values(h):
                lo = HD * (h % 2)
                pe.wait_ge(turn_read, (h + 1) * AT_N)
                if h:
                    pe.wait_ge(out_read, h)
                for j in range(n):
                    for s in range(AT_N):
                        mm = pe.matmul(out[lo:lo + HD, j, 0:w], vt[:, s, HD * (h // 4):HD * (h // 4) + HD],
                                       pT[h % 2][:, s, j * w:(j + 1) * w], start=(s == 0), stop=(s == AT_N - 1))
                mm.then_inc(out_ready, 1)

            scores(0)
            scores(1)
            for i in range(tiles):
                if i + 2 < tiles:
                    scores(i + 2)
                pe.wait_ge(probs_ready, i + 1)
                if i:
                    pe.wait_ge(turn_read, i)
                for s in range(AT_N):
                    mm = pe.transpose(turn[:, s // half, (s % half) * AT_T:(s % half + 1) * AT_T],
                                      probs[i % 2][:, s * AT_T:(s + 1) * AT_T], C["ident"][0:AT_T, 0:AT_T])
                mm.then_inc(turned, 1)
                if i % AT_N == AT_N - 1:
                    values(i // AT_N)

        def take(act, i):
            h, t = divmod(i, AT_N)
            act.wait_ge(turned, i + 1)
            if h >= 2 and t == 0:
                act.wait_ge(out_ready, h - 1)
            for a in range(2):
                cp = act.activation(pT[h % 2][:, half * a:half * a + half, t * AT_T:(t + 1) * AT_T],
                                    turn[:, a, 0:half * AT_T].rearrange("p (s t) -> p s t", t=AT_T), ACT.Copy)
            cp.then_inc(turn_read, 1)

        @block.scalar
        def _(act):
            for i in range(tiles):
                act.wait_ge(max_ready, i + 1)
                if i >= 2:
                    act.wait_ge(turned, i - 1)
                act.activation(cut(probs[i % 2][:, :], L), sc[i % 2][:, :, 0:w], ACT.Exp, bias=top[:, i % 2:i % 2 + 1],
                               scale=HD ** -0.5, accum_out=total[:, i % 2:i % 2 + 1]).then_inc(exp_ready, 1)
                if i:
                    take(act, i - 1)
            take(act, tiles - 1)

        @block.vector
        def _(dve):
            dve.wait_ge(v_turned, 1)
            dve.tensor_copy(vt[:, :, :].rearrange("p (a b) e -> p a b e", a=2),
                            out[0:AT_T, :, 0:3 * P].rearrange("p a (b e) -> p a b e", b=3)).then_inc(v_read, 1)

            def maximum(i):
                dve.wait_ge(scores_ready, i + 1)
                dve.tensor_reduce(top[:, i % 2:i % 2 + 1], sc[i % 2][:, :, 0:w], mybir.AxisListType.XY, ALU.max)
                dve.drain()
                dve.tensor_scalar(top[:, i % 2:i % 2 + 1], top[:, i % 2:i % 2 + 1], -(HD ** -0.5), None,
                                  ALU.mult).then_inc(max_ready, 1)

            maximum(0)
            maximum(1)
            for i in range(tiles):
                dve.wait_ge(exp_ready, i + 1)
                dve.reciprocal(total[:, i % 2:i % 2 + 1], total[:, i % 2:i % 2 + 1])
                dve.drain()
                dve.tensor_scalar(probs[i % 2][:, :], probs[i % 2][:, :], total[:, i % 2:i % 2 + 1], None,
                                  ALU.mult).then_inc(probs_ready, 1)
                if i + 2 < tiles:
                    maximum(i + 2)
                if i % AT_N == AT_N - 1:
                    h = i // AT_N
                    lo = HD * (h % 2)
                    dve.wait_ge(out_ready, h + 1)
                    dve.tensor_copy(cut(y[lo:lo + HD, h // 2, :], L), out[lo:lo + HD, :, 0:w]).then_inc(out_read, 1)


def first_block(nc, W, V, C, x, h):
    h_out = h[:, :, META:]
    with Phase(nc, "b1") as ph:
        C = C | load(nc, ph, "c1", {k: W[k] for k in ("masks", "cos", "sin", "swap", "ones64")})
        xn = Pair(ph, "xn", [P, DC, L])
        with Phase(nc, "in1") as p0, nc.Block() as block:
            loaded = p0.sem("loaded")

            @block.sync
            def _(sp):
                sp.dma_start(h[:, :, 0:META], W["meta"]).then_inc(loaded, 16)
                sp.dma_start(h[:, :, META:], x).then_inc(loaded, 16)
                sp.wait_ge(loaded, 32)

        rms_norm(nc, "n1", L, C["ones"], h, xn, V["ffn1_norm"])
        with Phase(nc, "f1") as pf:
            hidden = Pair(pf, "hidden", [P, FC, L])
            gated_up(nc, "f1u", L, xn, W["ffn1_w_gate"], W["ffn1_w_up"], FC, hidden)
            project(nc, "f1d", L, hidden, W["ffn1_w_down"], DC, h, scale=0.5, residual=True)
        rms_norm(nc, "n2", L, C["ones"], h, xn, V["mix_norm"])
        with Phase(nc, "mix") as pm:
            ya = pm.sb("ya", [P, HG, L])
            yb = pm.sb("yb", [P, HG, L])
            with Phase(nc, "za") as pz:
                z = pz.sb("z", [P, A_END, L])
                project(nc, "zap", L, xn, W["w_in"][Z_END:Z_GATES], A_END, z)
                gqa(nc, V, C, z, yb)
            with Phase(nc, "zh") as pz:
                z = pz.sb("z", [P, Z_END, LP])
                project(nc, "zhp", L, xn, W["w_in"][0:Z_END], Z_END, z[:, :, PADN:])
                hgrn(nc, V, C, W, z, ya)
            pairs = [Pair(pm, f"{k}_pair", [P, HG, L]) for k in ("ya", "yb")]
            split(nc, "sya", ya[:, :, :], pairs[0])
            split(nc, "syb", yb[:, :, :], pairs[1])
            gates = pm.sb("gates", [P, 2 * DC, L])
            project(nc, "gp", L, xn, W["w_in"][Z_GATES:Z_GATES + 2 * DC], 2 * DC, gates, function=ACT.Sigmoid)
            merge(nc, "mg", L, pairs[0], W["w_up_a"], gates[:, 0:DC, :], pairs[1], W["w_up_b"], gates[:, DC:2 * DC, :], DC, xn)

        every = slice(None)
        mixed = xn.part(every, every, slice(META, L))
        real = xn.part(every, every, slice(0, SEQ))
        project(nc, "wo", SEQ, mixed, W["w_out"], DC, h_out, residual=True)
        rms_norm(nc, "n3", SEQ, C["ones"], h_out, real, V["ffn2_norm"])
        with Phase(nc, "f2") as pf:
            hidden = Pair(pf, "hidden", [P, FC, SEQ])
            gated_up(nc, "f2u", SEQ, real, W["ffn2_w_gate"], W["ffn2_w_up"], FC, hidden)
            project(nc, "f2d", SEQ, hidden, W["ffn2_w_down"], DC, h_out, scale=0.5, residual=True)
B2_AVAL, B2_AGATE, B2_POOL, B2_CH, B2_CB, B2_CC, B2_Q, B2_K, B2_V, B2_END = 0, 2, 4, 6, 8, 10, 12, 14, 16, 18
CONF = 31
SCONV = 3
POOL_PAD = 16
WINDOWS = (2, 4, 8, 16)
SB_HEADS = 4
TILES = SEQ // P
MODS = 9
PK_HEADS = 8
PK_TOP = 16
NKEYS = 128
PICKS = PK_HEADS * PK_TOP
LOW = -3.0e38


class LocalMixes:

    def __init__(self, nc, ph, V, C, x, z, y):
        self.V, self.C, self.x, self.z, self.y = V, C, x, z, y
        self.u = ph.sb("u", [P, 2, CONF - 1 + SEQ])
        self.c = ph.sb("c", [P, 2, SCONV - 1 + SEQ])
        self.base = ph.sb("base", [P, 2, POOL_PAD + SEQ])
        self.sums = [ph.sb(f"sums{i}", [P, 2, POOL_PAD + SEQ]) for i in range(4)]
        self.gate_ready = ph.sem("gate_ready")

    def gate(self, act):
        gate = self.z[:, B2_AGATE:B2_AGATE + 2, :]
        act.activation(gate, gate, ACT.Sigmoid).then_inc(self.gate_ready, 1)

    def start(self, dve):
        x, z, u, c, base = self.x, self.z, self.u, self.c, self.base
        dve.memset(u[:, :, 0:CONF - 1], 0.0)
        dve.memset(c[:, :, 0:SCONV - 1], 0.0)
        for a in [base] + self.sums:
            dve.memset(a[:, :, 0:POOL_PAD], 0.0)
        dve.tensor_copy(base[:, :, POOL_PAD:], z[:, B2_POOL:B2_POOL + 2, :])
        dve.tensor_tensor(c[:, :, SCONV - 1:], z[:, B2_CC:B2_CC + 2, :], z[:, B2_CH:B2_CH + 2, :], ALU.mult)
        dve.tensor_scalar(x[:, :, :], x[:, :, :], DEEP_ALPHA, None, ALU.mult)
        dve.wait_ge(self.gate_ready, 1)
        dve.tensor_tensor(u[:, :, CONF - 1:], z[:, B2_AVAL:B2_AVAL + 2, :], z[:, B2_AGATE:B2_AGATE + 2, :], ALU.mult)
        dve.drain()

    def taps(self, dve, first, end):
        V, u, c, y = self.V, self.u, self.c, self.y
        for k in range(first, min(end, CONF)):
            for m in range(2):
                tap = V["conv_a_w"][:, 2 * k + m:2 * k + m + 1]
                if k == 0:
                    dve.tensor_scalar(y[:, m, :], u[:, m, 0:SEQ], tap, V["conv_a_b"][:, m:m + 1], ALU.mult, ALU.add)
                else:
                    dve.scalar_tensor_tensor(out=y[:, m, :], in0=u[:, m, k:k + SEQ], scalar=tap, in1=y[:, m, :],
                                             op0=ALU.mult, op1=ALU.add)
            if k < SCONV:
                for m in range(2):
                    tap = V["conv_c_w"][:, 2 * k + m:2 * k + m + 1]
                    if k == 0:
                        dve.tensor_scalar(y[:, 4 + m, :], c[:, m, 0:SEQ], tap, None, ALU.mult)
                    else:
                        dve.scalar_tensor_tensor(out=y[:, 4 + m, :], in0=c[:, m, k:k + SEQ], scalar=tap,
                                                 in1=y[:, 4 + m, :], op0=ALU.mult, op1=ALU.add)
            if k < len(WINDOWS):
                before = self.base if k == 0 else self.sums[k - 1]
                lag = WINDOWS[k] // 2
                dve.tensor_tensor(self.sums[k][:, :, POOL_PAD:], before[:, :, POOL_PAD:],
                                  before[:, :, POOL_PAD - lag:POOL_PAD - lag + SEQ], ALU.add)
            dve.drain()

    def finish(self, dve):
        z, y = self.z, self.y
        dve.tensor_tensor(y[:, 4:6, :], y[:, 4:6, :], z[:, B2_CB:B2_CB + 2, :], ALU.mult)
        for g in range(len(WINDOWS)):
            part, m = slice(64 * (g % 2), 64 * (g % 2) + 64), g // 2
            dve.tensor_tensor(y[part, 2 + m, :], self.sums[g][part, m, POOL_PAD:], self.C["inv_count"][part, m, :], ALU.mult)
        dve.drain()
        dve.tensor_tensor(y[:, 2:4, :], y[:, 2:4, :], self.base[:, :, POOL_PAD:], ALU.subtract)
        dve.drain()


def pool_weights(nc, V, W, y):
    with Phase(nc, "pw") as ph, nc.Block() as block:
        pooled = ph.ps("pooled", [P, 2, BANK])
        weights = ph.sb("pool_w", [P, 2, P])
        loaded, mixed_ready = ph.sem("loaded"), ph.sem("mixed_ready")

        @block.sync
        def _(sp):
            sp.dma_start(weights[:, :, :], W["pool_w"]).then_inc(loaded, 16)

        @block.tensor
        def _(pe):
            pe.wait_ge(loaded, 16)
            for m in range(2):
                mm = pe.matmul(pooled[:, m, :], weights[:, m, :], y[:, 2 + m, :], start=True, stop=True)
            mm.then_inc(mixed_ready, 1)

        @block.vector
        def _(dve):
            dve.wait_ge(mixed_ready, 1)
            for m in range(2):
                dve.tensor_scalar(y[:, 2 + m, :], pooled[:, m, :], V["pool_scale"][:, m:m + 1], None, ALU.mult)
            dve.drain()


def stick_breaking(nc, V, C, x, z, y_all):
    y = y_all[:, 6:8, :]
    with Phase(nc, "sb") as ph, nc.Block() as block:
        mixes = LocalMixes(nc, ph, V, C, x, z, y_all)
        share = -(-CONF // (4 * TILES))
        vt = ph.sb("vt", [P, TILES, 2 * P])
        zt, sp_, cum = ph.sb("zt", [P, SB_HEADS, SEQ]), ph.sb("softplus", [P, SB_HEADS, SEQ]), ph.sb("cum", [P, SB_HEADS, SEQ])
        one = ph.sb("one", [P, SEQ])
        wT = [ph.sb(f"wT{i}", [P, TILES, P]) for i in range(2)]
        sc = ph.ps("sc", [P, SB_HEADS, BANK])
        turn = ph.ps("turn", [P, 2, TILES, P])
        out = ph.ps("out", [P, 2, BANK])
        v_turned, v_read = ph.sem("v_turned"), ph.sem("v_read")
        scores_ready, scores_read = ph.sem("scores_ready"), ph.sem("scores_read")
        z_ready, log_ready = ph.sem("z_ready"), ph.sem("log_ready")
        logw_ready, exp_ready, w_ready = ph.sem("logw_ready"), ph.sem("exp_ready"), ph.sem("w_ready")
        turned, turn_read, out_ready, out_read = (ph.sem(s) for s in ("turned", "turn_read", "out_ready", "out_read"))

        @block.tensor
        def _(pe):
            for m in range(2):
                for b in range(TILES):
                    mm = pe.transpose(turn[:, m, b, :], z[:, B2_V + m, b * P:(b + 1) * P], C["ident"][:, :])
            mm.then_inc(v_turned, 1)
            pe.wait_ge(v_read, 1)
            for b in range(TILES):
                n = (b + 1) * P
                if b:
                    pe.wait_ge(scores_read, b)
                for h in range(SB_HEADS):
                    lo = HD * (h % 2)
                    mm = pe.matmul(sc[:, h, 0:n], z[lo:lo + HD, B2_Q + h // 2, b * P:n], z[lo:lo + HD, B2_K + h // 2, 0:n],
                                   start=True, stop=True)
                mm.then_inc(scores_ready, 1)
                pe.wait_ge(w_ready, b + 1)
                for h in range(SB_HEADS):
                    i = SB_HEADS * b + h
                    lo = HD * (h % 2)
                    if i >= 2:
                        pe.wait_ge(turn_read, i - 1)
                    for s in range(b + 1):
                        mm = pe.transpose(turn[:, i % 2, s, :], zt[:, h, s * P:(s + 1) * P], C["ident"][:, :])
                    mm.then_inc(turned, 1)
                    pe.wait_ge(turn_read, i + 1)
                    if i >= 2:
                        pe.wait_ge(out_read, i - 1)
                    for s in range(b + 1):
                        mm = pe.matmul(out[lo:lo + HD, i % 2, 0:P], vt[:, s, HD * h:HD * h + HD], wT[i % 2][:, s, :],
                                       start=(s == 0), stop=(s == b))
                    mm.then_inc(out_ready, 1)

        @block.scalar
        def _(act):
            mixes.gate(act)
            for b in range(TILES):
                n = (b + 1) * P
                act.wait_ge(z_ready, b + 1)
                act.activation(sp_[:, :, 0:n], zt[:, :, 0:n], ACT.Abs)
                act.drain()
                act.activation(sp_[:, :, 0:n], sp_[:, :, 0:n], ACT.Exp, scale=-1.0)
                act.drain()
                act.activation(sp_[:, :, 0:n], sp_[:, :, 0:n], ACT.Ln, bias=1.0).then_inc(log_ready, 1)
                act.wait_ge(logw_ready, b + 1)
                for h in range(SB_HEADS):
                    ex = act.activation(zt[:, h, 0:n], zt[:, h, 0:n], ACT.Exp, bias=cum[:, h, n - 1:n])
                ex.then_inc(exp_ready, 1)
                for h in range(SB_HEADS):
                    i = SB_HEADS * b + h
                    act.wait_ge(turned, i + 1)
                    act.activation(wT[i % 2][:, 0:b + 1, :], turn[:, i % 2, 0:b + 1, :], ACT.Copy).then_inc(turn_read, 1)

        @block.vector
        def _(dve):
            dve.memset(one[:, :], 1.0)
            dve.wait_ge(v_turned, 1)
            for m in range(2):
                dve.tensor_copy(vt[:, :, m * P:(m + 1) * P], turn[:, m, :, :])
            dve.drain()
            dve.nop().then_inc(v_read, 1)
            mixes.start(dve)
            for b in range(TILES):
                place = 4 * b * share
                n = (b + 1) * P
                diag = slice(b * P, n)
                mask = C["before"][:, :].unsqueeze(1).to_broadcast([P, SB_HEADS, P])
                dve.wait_ge(scores_ready, b + 1)
                if b:
                    dve.wait_ge(turned, SB_HEADS * b)
                dve.tensor_scalar(zt[:, :, 0:n], sc[:, :, 0:n], HD ** -0.5, None, ALU.mult).then_inc(scores_read, 1)
                dve.drain()
                dve.nop().then_inc(z_ready, 1)
                dve.tensor_scalar(cum[:, :, 0:n], zt[:, :, 0:n], 0.0, None, ALU.max)
                dve.drain()
                mixes.taps(dve, place, place + 2 * share)
                dve.wait_ge(log_ready, b + 1)
                dve.tensor_tensor(sp_[:, :, 0:n], sp_[:, :, 0:n], cum[:, :, 0:n], ALU.add)
                dve.drain()
                dve.tensor_tensor(zt[:, :, 0:n], zt[:, :, 0:n], sp_[:, :, 0:n], ALU.subtract)
                dve.drain()
                dve.tensor_tensor(sp_[:, :, diag], sp_[:, :, diag], mask, ALU.mult)
                dve.drain()
                for h in range(SB_HEADS):
                    dve.tensor_tensor_scan(cum[:, h, 0:n], one[:, 0:n], sp_[:, h, 0:n], 0.0, ALU.mult, ALU.add)
                dve.drain()
                dve.tensor_tensor(zt[:, :, 0:n], zt[:, :, 0:n], cum[:, :, 0:n], ALU.add)
                dve.drain()
                for h in range(SB_HEADS):
                    dve.tensor_scalar(cum[:, h, n - 1:n], cum[:, h, n - 1:n], -1.0, None, ALU.mult)
                dve.drain()
                dve.nop().then_inc(logw_ready, 1)
                mixes.taps(dve, place + 2 * share, place + 3 * share)
                dve.wait_ge(exp_ready, b + 1)
                dve.tensor_tensor(zt[:, :, diag], zt[:, :, diag], mask, ALU.mult).then_inc(w_ready, 1)
                mixes.taps(dve, place + 3 * share, place + 4 * share)
                for h in range(SB_HEADS):
                    i = SB_HEADS * b + h
                    lo = HD * (h % 2)
                    dve.wait_ge(out_ready, i + 1)
                    dve.tensor_copy(y[lo:lo + HD, h // 2, b * P:n], out[lo:lo + HD, i % 2, 0:P]).then_inc(out_read, 1)
            mixes.finish(dve)


def choose_experts(nc, C, W, q, gates_dram, c_silu, mod):
    with Phase(nc, "pk") as ph:
        keys = ph.sb("keys", [P, 2 * PK_HEADS, NKEYS])
        scores = ph.sb("scores", [P, 2 * PK_HEADS, NKEYS])
        best = ph.sb("best", [P, 2 * PK_HEADS, PK_TOP])
        where = ph.sb("where", [P, 2 * PK_HEADS, PK_TOP], U32)
        wheref = ph.sb("wheref", [P, PK_HEADS, 2, PK_TOP])
        pair = ph.sb("pair", [P, PK_HEADS, PK_TOP * PK_TOP])
        top = ph.sb("top", [P, PK_HEADS, PK_TOP])
        at = ph.sb("at", [P, PICKS], U32)
        half = ph.sb("half", [P, 2, PICKS], U32)
        halff = ph.sb("halff", [P, 2, PICKS])
        hot = scores[:, :, :].rearrange("p g n -> p (g n)").rearrange("p (k a) -> p k a", a=PK_TOP)
        picks = ph.sb("picks", [P, 3, PICKS])
        sums = ph.sb("sums", [P, PK_HEADS])
        by_pick = ph.sb("by_pick", [P, 3, P])
        grid = ph.sb("grid", [P, NKEYS, P])
        ADA_SLOTS = 7
        columns_here = MODS * DC // TILES
        ada = [ph.sb(f"ada{s}", [P, D]) for s in range(ADA_SLOTS)]
        ada_in = [ph.sem(f"ada_in{s}") for s in range(ADA_SLOTS)]
        ada_used = ph.sem("ada_used")
        stored = ph.sem("stored")
        GROUP = 4
        first_hot = [ph.sb(f"first_hot{s}", [P, P]) for s in range(2 * GROUP)]
        second_hot = [ph.sb(f"second_hot{s}", [P, P]) for s in range(2 * GROUP)]

        def load_ada(sp, column):
            wait_from(sp, ada_used, column - ADA_SLOTS + 1)
            sp.dma_start(ada[column % ADA_SLOTS][:, :], W["w_ada"][column]).then_inc(ada_in[column % ADA_SLOTS], 16)

        with nc.Block() as block:
            loaded = ph.sem("loaded")

            @block.sync
            def _(sp):
                sp.dma_start(keys[:, :, :], W["peer_keys"]).then_inc(loaded, 16)
                for i in range(ADA_SLOTS):
                    load_ada(sp, i)
                sp.wait_ge(loaded, 16)

        for t in range(TILES):
            with Phase(nc, f"pt{t}") as p1, nc.Block() as block:
                sc = p1.ps("sc", [P, 4, 4, NKEYS])
                turn = p1.ps("turn", [P, 3, P])
                scores_ready, sub_ready, exp_ready = p1.sem("scores_ready"), p1.sem("sub_ready"), p1.sem("exp_ready")
                picks_ready, turned = p1.sem("picks_ready"), p1.sem("turned")
                modulation = p1.ps("modulation", [P, columns_here])

                @block.sync
                def _(sp):
                    for i in range(ADA_SLOTS, columns_here):
                        load_ada(sp, t * columns_here + i)

                @block.tensor
                def _(pe):
                    for g in range(2 * PK_HEADS):
                        mm = pe.matmul(sc[:, g // 4, g % 4, :], q[:, g, t * P:(t + 1) * P], keys[:, g, :], start=True, stop=True)
                        if g % 4 == 3:
                            mm.then_inc(scores_ready, 1)
                    for i in range(columns_here):
                        column = t * columns_here + i
                        pe.wait_ge(ada_in[column % ADA_SLOTS], 16 * (column // ADA_SLOTS + 1))
                        for k in range(DC):
                            mm = pe.matmul(modulation[:, i:i + 1], ada[column % ADA_SLOTS][:, k * P:(k + 1) * P], c_silu[:, k:k + 1],
                                           start=(k == 0), stop=(k == DC - 1))
                        mm.then_inc(ada_used, 1)
                    pe.wait_ge(picks_ready, 1)
                    for i in range(3):
                        mm = pe.transpose(turn[:, i, :], picks[:, i, :], C["ident"][:, :])
                    mm.then_inc(turned, 1)

                @block.scalar
                def _(act):
                    act.wait_ge(sub_ready, 1)
                    act.activation(picks[:, 2, :], picks[:, 2, :], ACT.Exp).then_inc(exp_ready, 1)
                    act.wait_ge(ada_used, (t + 1) * columns_here)
                    act.activation(mod[:, t * columns_here:(t + 1) * columns_here], modulation[:, :], ACT.Copy)

                @block.vector
                def _(dve):
                    for g in range(4):
                        dve.wait_ge(scores_ready, g + 1)
                        dve.tensor_copy(scores[:, 4 * g:4 * g + 4, :], sc[:, g, :, :])
                    dve.drain()

                    def top16(values, best, where, lists):
                        for r in range(2):
                            for g in range(lists):
                                dve.max(best(g)[:, 8 * r:8 * r + 8], values(g))
                            dve.drain()
                            for g in range(lists):
                                dve.max_index(where(g)[:, 8 * r:8 * r + 8], best(g)[:, 8 * r:8 * r + 8], values(g))
                            if r == 0:
                                dve.drain()
                                for g in range(lists):
                                    dve.match_replace(values(g), best(g)[:, 0:8], values(g), LOW)
                            dve.drain()

                    top16(lambda g: scores[:, g, :], lambda g: best[:, g, :], lambda g: where[:, g, :], 2 * PK_HEADS)
                    dve.tensor_copy(wheref[:, :, :, :].rearrange("p h a k -> p (h a k)"),
                                    where[:, :, :].rearrange("p g k -> p (g k)"))
                    halves_of = best[:, :, :].rearrange("p (h a) k -> p h a k", a=2)
                    dve.tensor_tensor(pair[:, :, :].rearrange("p h (a b) -> p h a b", a=PK_TOP),
                                      halves_of[:, :, 0, :].unsqueeze(3).to_broadcast([P, PK_HEADS, PK_TOP, PK_TOP]),
                                      halves_of[:, :, 1, :].unsqueeze(2).to_broadcast([P, PK_HEADS, PK_TOP, PK_TOP]), ALU.add)
                    dve.drain()
                    top16(lambda h: pair[:, h, :], lambda h: top[:, h, :],
                          lambda h: at[:, h * PK_TOP:(h + 1) * PK_TOP], PK_HEADS)
                    gates = picks[:, 2, :].rearrange("p (h k) -> p h k", h=PK_HEADS)
                    dve.tensor_tensor(gates, top[:, :, :], top[:, :, 0:1].to_broadcast([P, PK_HEADS, PK_TOP]),
                                      ALU.subtract).then_inc(sub_ready, 1)
                    dve.tensor_scalar(half[:, 0, :], at[:, :], 4, None, ALU.logical_shift_right)
                    dve.tensor_scalar(half[:, 1, :], at[:, :], 15, None, ALU.bitwise_and)
                    dve.drain()
                    dve.tensor_copy(halff[:, :, :], half[:, :, :])
                    dve.drain()
                    for i in range(2):
                        dve.tensor_tensor(hot, halff[:, i, :].unsqueeze(2).to_broadcast([P, PICKS, PK_TOP]),
                                          C["iota"][:, 0:PK_TOP].unsqueeze(1).to_broadcast([P, PICKS, PK_TOP]), ALU.is_equal)
                        dve.drain()
                        hot4 = hot.rearrange("p (h k) a -> p h k a", h=PK_HEADS)
                        dve.tensor_tensor(hot4, hot4, wheref[:, :, i, :].unsqueeze(2).to_broadcast(
                            [P, PK_HEADS, PK_TOP, PK_TOP]), ALU.mult)
                        dve.drain()
                        dve.tensor_reduce(picks[:, i, :], hot, AX_X, ALU.add)
                        dve.drain()
                    dve.wait_ge(exp_ready, 1)
                    dve.tensor_reduce(sums[:, :], gates, AX_X, ALU.add)
                    dve.drain()
                    dve.reciprocal(sums[:, :], sums[:, :])
                    dve.drain()
                    dve.tensor_tensor(gates, gates, sums[:, :].unsqueeze(2).to_broadcast([P, PK_HEADS, PK_TOP]), ALU.mult)
                    dve.drain()
                    dve.nop().then_inc(picks_ready, 1)
                    dve.wait_ge(turned, 1)
                    dve.tensor_copy(by_pick[:, :, :], turn[:, :, :])
                    dve.drain()

            with Phase(nc, f"pg{t}") as p2, nc.Block() as block:
                cell = [p2.ps(f"cell{s}", [P, GROUP, NKEYS]) for s in range(2)]
                hot_ready, cells_ready, cells_read = (p2.sem(s) for s in ("hot_ready", "cells_ready", "cells_read"))
                groups = P // GROUP

                @block.vector
                def _(dve):
                    def make(g, s, first):
                        wait_from(dve, cells_ready, g - 1)
                        for i in range(GROUP):
                            token = bass.ds(g * GROUP + i, 1)
                            dve.tensor_scalar(first_hot[s * GROUP + i][:, :], C["iota"][:, :], by_pick[:, 0, token],
                                              None, ALU.is_equal)
                            last = dve.tensor_scalar(second_hot[s * GROUP + i][:, :], C["iota"][:, :], by_pick[:, 1, token],
                                                     by_pick[:, 2, token], ALU.is_equal, ALU.mult)
                        last.then_inc(hot_ready, 1)

                    over_steps(dve, groups, 2, make)

                @block.scalar
                def _(act):
                    def read(g, s, first):
                        act.wait_ge(cells_ready, g + 1)
                        act.wait_ge(cells_ready, 1)
                        act.activation(grid[:, :, bass.ds(g * GROUP, GROUP)].rearrange("p j t -> p t j"), cell[s][:, :, :],
                                       ACT.Copy).then_inc(cells_read, 1)

                    wait_from(act, stored, 16 * t)
                    over_steps(act, groups, 2, read)

                @block.tensor
                def _(pe):
                    def step(g, s, first):
                        pe.wait_ge(hot_ready, g + 1)
                        wait_from(pe, cells_read, g - 1)
                        for i in range(GROUP):
                            mm = pe.matmul(cell[s][:, i, :], first_hot[s * GROUP + i][:, :], second_hot[s * GROUP + i][:, :],
                                           start=True, stop=True)
                        mm.then_inc(cells_ready, 1)

                    over_steps(pe, groups, 2, step)

                @block.sync
                def _(sp):
                    if t + 1 < TILES:
                        for i in range(ADA_SLOTS):
                            load_ada(sp, (t + 1) * columns_here + i)
                    sp.wait_ge(cells_read, groups)
                    sp.dma_start(gates_dram[:, :, t * P:(t + 1) * P].rearrange("j i t -> i j t"), grid[:, :, :]).then_inc(stored, 16)
                    if t == TILES - 1:
                        sp.wait_ge(stored, 16 * TILES)


def experts(nc, W, x, gates_dram, f):
    GROUP = 2
    groups = NKEYS // GROUP
    with Phase(nc, "ex") as ph, nc.Block() as block:
        u_raw, v_raw, g_in_sb = ([ph.sb(f"{k}{s}", [P, w]) for s in range(GROUP)] for k, w in (("u", D), ("v", D), ("g", SEQ)))
        u = [Pair(ph, f"up{s}", [P, D]) for s in range(GROUP)]
        v = [[Pair(ph, f"vp{b}_{s}", [P, D]) for s in range(GROUP)] for b in range(2)]
        hidden = [[Pair(ph, f"a{b}_{s}", [P, SEQ]) for s in range(GROUP)] for b in range(2)]
        act_raw = [ph.sb(f"act_raw{s}", [P, SEQ]) for s in range(GROUP)]
        up = [ph.ps(f"upp{s}", [P, BANK]) for s in range(GROUP)]
        down = [ph.ps(f"down{s}", [P, BANK]) for s in range(4)]
        u_in, g_in, v_in = ([ph.sem(f"{k}_in{s}") for s in range(GROUP)] for k in "ugv")
        u_high, u_low, v_high, v_low, a_high, a_low = (ph.sem(s) for s in ("u_high", "u_low", "v_high", "v_low", "a_high", "a_low"))
        up_done, gelu_done, gated, down_done, added = (ph.sem(s) for s in ("up_done", "gelu_done", "gated", "down_done", "added"))

        def over_groups(eng, stage):
            stage(0, 0, False)
            stage(1, 1, False)
            with eng.Fori(1, groups // 2 - 1) as i:
                stage(2 * i, 0, False)
                stage(2 * i + 1, 1, False)
            stage(groups - 2, 0, False)
            stage(groups - 1, 1, True)

        @block.sync
        def _(sp):
            def load_u(j, s):
                wait_from(sp, u_low, j - 1)
                sp.dma_start(u_raw[s][:, :], W["peer_u"][j]).then_inc(u_in[s], 16)

            def stage(g, b, last):
                for s in range(GROUP):
                    j = g * GROUP + s
                    if not last:
                        load_u(j + GROUP, s)
                    wait_from(sp, gated, j - 1)
                    sp.dma_start(g_in_sb[s][:, :], gates_dram[j]).then_inc(g_in[s], 16)
                    wait_from(sp, v_low, j - 1)
                    sp.dma_start(v_raw[s][:, :], W["peer_v"][j]).then_inc(v_in[s], 16)

            for s in range(GROUP):
                load_u(s, s)
            over_groups(sp, stage)

        @block.tensor
        def _(pe):
            def ups(g):
                for s in range(GROUP):
                    j = g * GROUP + s
                    pe.wait_ge(u_low, j + 1)
                    wait_from(pe, gelu_done, j - 1)
                    for k in range(DC):
                        part = slice(k * P, (k + 1) * P)
                        mm = multiply(pe, up[s][:, :], (u[s].high[:, part], u[s].low[:, part]),
                                      (x.high[:, k, :], x.low[:, k, :]), k == 0, k == DC - 1)
                    mm.then_inc(up_done, 1)

            def downs(g, b):
                pe.wait_ge(v_low, GROUP * g + GROUP)
                pe.wait_ge(a_low, GROUP * g + GROUP)
                for c in range(DC):
                    part = slice(c * P, (c + 1) * P)
                    wait_from(pe, added, g * DC + c - 3)
                    for s in range(GROUP):
                        mm = multiply(pe, down[c % 4][:, :], (v[b][s].high[:, part], v[b][s].low[:, part]),
                                      (hidden[b][s].high[:, :], hidden[b][s].low[:, :]), s == 0, s == GROUP - 1)
                    mm.then_inc(down_done, 1)

            def stage(g, b, last):
                ups(g)
                if not (isinstance(g, int) and g == 0):
                    downs(g - 1, 1 - b)

            over_groups(pe, stage)
            downs(groups - 1, 1)

        @block.scalar
        def _(act):
            def round_u(j, s, count):
                act.wait_ge(u_in[s], count)
                wait_from(act, up_done, j - 1)
                act.activation(u[s].high[:, :], u_raw[s][:, :], ACT.Copy).then_inc(u_high, 1)

            def stage(g, b, last):
                for s in range(GROUP):
                    j = g * GROUP + s
                    act.wait_ge(up_done, j + 1)
                    wait_from(act, a_low, j - 1)
                    act.activation(act_raw[s][:, :], up[s][:, :], ACT.Gelu_apprx_tanh).then_inc(gelu_done, 1)
                    if not last:
                        round_u(j + GROUP, s, 16 * g + 32)
                    act.wait_ge(v_in[s], 16 * g + 16)
                    wait_from(act, down_done, (g - 1) * DC)
                    act.activation(v[b][s].high[:, :], v_raw[s][:, :], ACT.Copy).then_inc(v_high, 1)
                    act.wait_ge(gated, j + 1)
                    act.activation(hidden[b][s].high[:, :], act_raw[s][:, :], ACT.Copy).then_inc(a_high, 1)

            for s in range(GROUP):
                round_u(s, s, 16)
            over_groups(act, stage)

        @block.vector
        def _(dve):
            def low_u(j, s):
                dve.wait_ge(u_high, j + 1)
                dve.tensor_tensor(u[s].low[:, :], u_raw[s][:, :], u[s].high[:, :], ALU.subtract).then_inc(u_low, 1)

            def add(g):
                for c in range(DC):
                    dve.wait_ge(down_done, g * DC + c + 1)
                    if isinstance(g, int) and g == 0:
                        dve.tensor_copy(f[:, c, :], down[c % 4][:, :]).then_inc(added, 1)
                    else:
                        dve.tensor_tensor(f[:, c, :], f[:, c, :], down[c % 4][:, :], ALU.add).then_inc(added, 1)
                dve.drain()

            def stage(g, b, last):
                for s in range(GROUP):
                    j = g * GROUP + s
                    dve.wait_ge(g_in[s], 16 * g + 16)
                    dve.wait_ge(gelu_done, j + 1)
                    dve.tensor_tensor(act_raw[s][:, :], act_raw[s][:, :], g_in_sb[s][:, :], ALU.mult).then_inc(gated, 1)
                    if not last:
                        low_u(j + GROUP, s)
                    dve.wait_ge(v_high, j + 1)
                    dve.tensor_tensor(v[b][s].low[:, :], v_raw[s][:, :], v[b][s].high[:, :], ALU.subtract).then_inc(v_low, 1)
                    dve.wait_ge(a_high, j + 1)
                    dve.tensor_tensor(hidden[b][s].low[:, :], act_raw[s][:, :], hidden[b][s].high[:, :],
                                      ALU.subtract).then_inc(a_low, 1)
                if not (isinstance(g, int) and g == 0):
                    add(g - 1)

            for s in range(GROUP):
                low_u(s, s)
            over_groups(dve, stage)
            add(groups - 1)


def second_block(nc, W, V, C, x, gates_dram, mod):
    with Phase(nc, "b2") as ph:
        C = C | load(nc, ph, "c2", {k: W[k] for k in ("iota", "before", "inv_count")})
        y = ph.sb("y", [P, DC, SEQ])
        c_silu = ph.sb("c_silu", [P, DC])
        with Phase(nc, "b2z") as pz:
            z = pz.sb("z", [P, B2_END, SEQ])
            with Phase(nc, "b2x") as px:
                pair = Pair(px, "x2", [P, DC, SEQ])
                split(nc, "sx2", x, pair)
                project(nc, "p2", SEQ, pair, W["w_in_2"], B2_END, z)
            stick_breaking(nc, V, C, x, z, y)
            pool_weights(nc, V, W, y)
            conf = pz.sb("conf", [P, 2, SEQ])
            layer_norm(nc, "lna", SEQ, C["ones"], y[:, 0:2, :], conf, V["norm_a_g"], V["norm_a_b"], LN_EPS, silu=True)
            with nc.Block() as block:
                @block.vector
                def _(dve):
                    dve.tensor_copy(y[:, 0:2, :], conf[:, :, :])

                @block.scalar
                def _(act):
                    act.activation(c_silu[:, :], V["c"], ACT.Silu)
        with Phase(nc, "b2y") as py:
            pair = Pair(py, "y2", [P, DC, SEQ])
            split(nc, "sy2", y, pair)
            project(nc, "wo2", SEQ, pair, W["w_out_2"], DC, x, residual=True)
        layer_norm(nc, "ln1", SEQ, C["ones"], x, y, V["ln1_g"], V["ln1_b"], LN_EPS)
        with Phase(nc, "pq") as pq:
            q = pq.sb("q", [P, 2 * PK_HEADS, SEQ])
            with Phase(nc, "pqx") as px:
                pair = Pair(px, "q2", [P, DC, SEQ])
                split(nc, "sq2", y, pair)
                project(nc, "pqp", SEQ, pair, W["peer_wq"], 2 * PK_HEADS, q)
            choose_experts(nc, C, W, q, gates_dram, c_silu, mod)
        with Phase(nc, "pf") as pf:
            f = pf.sb("f", [P, DC, SEQ])
            with Phase(nc, "pfx") as px:
                pair = Pair(px, "e2", [P, DC, SEQ])
                split(nc, "se2", y, pair)
                experts(nc, W, pair, gates_dram, f)
            with nc.Block() as block:
                @block.vector
                def _(dve):
                    for c in range(DC):
                        dve.scalar_tensor_tensor(out=f[:, c, :], in0=y[:, c, :], scalar=DEEP_ALPHA, in1=f[:, c, :],
                                                 op0=ALU.mult, op1=ALU.add)
            layer_norm(nc, "ln2", SEQ, C["ones"], f, x, V["ln2_g"], V["ln2_b"], LN_EPS)
U3, V3, DQ, DV_END, DZ, DAB, G3, END3 = 0, 8, 16, 40, 40, 48, 49, 65
DN = 8
DCONV = 4
DCH = 64
NDC = SEQ // DCH
GRP = 4
DN_LEVELS = (1, 2, 4, 8, 16, 32)
ROW_G, ROW_B, ROW_BG, ROW_KD = 0, 32, 64, 96
GONE = -110.0


def spatial_gating(nc, V, C, W, xn, o_a):
    with Phase(nc, "sg") as ph:
        C = C | load(nc, ph, "sgc", {"upto": W["upto"]})
        z = ph.sb("z", [P, 2 * DC, SEQ])
        vn = ph.sb("vn", [P, DC, SEQ])
        project(nc, "sgp", SEQ, xn, W["w_in_3"][U3:DQ], 2 * DC, z, function=ACT.Gelu)
        layer_norm(nc, "sgl", SEQ, C["ones"], z[:, DC:, :], vn, V["gm_ln_g"], V["gm_ln_b"], EPS)
        with nc.Block() as block:
            w = ph.sb("w", [P, DC, P])
            bias = ph.sb("bias", [1, DC * P])
            vt = [ph.sb(f"vt{i}", [P, TILES, P]) for i in range(2)]
            turn = ph.ps("turn", [P, 2, TILES, P])
            mixed = ph.ps("mixed", [P, 2, TILES, P])
            loaded, masked, turned, turn_read, mixed_ready, mixed_read = (
                ph.sem(s) for s in ("loaded", "masked", "turned", "turn_read", "mixed_ready", "mixed_read"))

            @block.sync
            def _(sp):
                sp.dma_start(w[:, :, :], W["gm_w_s"]).then_inc(loaded, 16)
                sp.dma_start(bias[:, :], W["gm_b_s"]).then_inc(loaded, 16)

            @block.vector
            def _(dve):
                dve.wait_ge(loaded, 32)
                dve.tensor_tensor(w[:, :, :], w[:, :, :], C["upto"][:, :].unsqueeze(1).to_broadcast([P, DC, P]),
                                  ALU.mult).then_inc(masked, 1)
                for g in range(DC):
                    dve.wait_ge(mixed_ready, g + 1)
                    dve.tensor_tensor(o_a[:, g, :], z[:, g, :], mixed[:, g % 2, :, :].rearrange("p a b -> p (a b)"),
                                      ALU.mult).then_inc(mixed_read, 1)

            @block.scalar
            def _(act):
                for g in range(DC):
                    act.wait_ge(turned, g + 1)
                    if g >= 2:
                        act.wait_ge(mixed_ready, g - 1)
                    act.activation(vt[g % 2][:, :, :], turn[:, g % 2, :, :], ACT.Copy).then_inc(turn_read, 1)

            @block.tensor
            def _(pe):
                def turns(g):
                    if g >= 2:
                        pe.wait_ge(turn_read, g - 1)
                    for n in range(TILES):
                        mm = pe.transpose(turn[:, g % 2, n, :], vn[:, g, n * P:(n + 1) * P], C["ident"][:, :])
                    mm.then_inc(turned, 1)

                turns(0)
                pe.wait_ge(masked, 1)
                for g in range(DC):
                    if g + 1 < DC:
                        turns(g + 1)
                    pe.wait_ge(turn_read, g + 1)
                    if g >= 2:
                        pe.wait_ge(mixed_read, g - 1)
                    for n in range(TILES):
                        pe.matmul(mixed[:, g % 2, n, :], vt[g % 2][:, n, :], w[:, g, :], start=True, stop=False)
                        mm = pe.matmul(mixed[:, g % 2, n, :], C["ones"][0:1, :], bias[0:1, g * P:(g + 1) * P],
                                       start=False, stop=True)
                    mm.then_inc(mixed_ready, 1)


def delta_rows(nc, V, C, W, ab, rows, cols, ends):
    with Phase(nc, "dr") as ph, nc.Block() as block:
        a, e, beta = ph.sb("a", [DN, SEQ]), ph.sb("e", [DN, SEQ]), ph.sb("beta", [DN, SEQ])
        g = ph.sb("g", [DN, SEQ])
        t1, t2 = ph.sb("t1", [DN, SEQ]), ph.sb("t2", [DN, SEQ])
        keep = ph.sb("keep", [DN, SEQ])
        rate = ph.sb("rate", [DN, 1])
        turn = ph.ps("turn", [P, TILES, P])
        wide = ph.ps("wide", [P, 2, BANK])
        a_ready, log_ready, g_ready, parts_ready = (ph.sem(s) for s in ("a_ready", "log_ready", "g_ready", "parts_ready"))
        rows_ready, turned, wide_ready, wide_read = (ph.sem(s) for s in ("rows_ready", "turned", "wide_ready", "wide_read"))

        def chunked(x):
            return x[:, :].rearrange("p (n c) -> p n c", c=DCH)

        @block.vector
        def _(dve):
            dve.memset(rows[:, :], 0.0)
            dve.memset(keep[:, :], 1.0)
            dve.tensor_scalar(a[:, :], ab[0:DN, :], V["dt_bias"][0:DN, 0:1], None, ALU.add)
            dve.drain()
            dve.memset(chunked(keep)[:, :, 0:1], 0.0)
            dve.nop().then_inc(a_ready, 1)
            dve.wait_ge(log_ready, 1)
            dve.scalar_tensor_tensor(out=e[:, :], in0=a[:, :], scalar=0.0, in1=e[:, :], op0=ALU.max, op1=ALU.add)
            dve.drain()
            dve.tensor_scalar(e[:, :], e[:, :], rate[:, 0:1], -1.0, ALU.mult, ALU.mult)
            dve.drain()
            dve.tensor_scalar(e[:, :], e[:, :], GONE, None, ALU.max)
            dve.drain()
            dve.tensor_tensor_scan(g[:, :], keep[:, :], e[:, :], 0.0, ALU.mult, ALU.add)
            dve.drain()
            dve.tensor_tensor(chunked(t1), chunked(g)[:, :, DCH - 1:DCH].to_broadcast([DN, NDC, DCH]), chunked(g), ALU.subtract)
            dve.drain()
            dve.nop().then_inc(g_ready, 1)
            dve.wait_ge(parts_ready, 1)
            dve.tensor_copy(rows[ROW_G:ROW_G + DN, :], g[:, :])
            dve.tensor_copy(rows[ROW_B:ROW_B + DN, :], beta[:, :])
            dve.tensor_tensor(rows[ROW_BG:ROW_BG + DN, :], beta[:, :], t2[:, :], ALU.mult)
            dve.tensor_copy(rows[ROW_KD:ROW_KD + DN, :], t1[:, :])
            dve.drain()
            dve.nop().then_inc(rows_ready, 1)
            dve.wait_ge(turned, 1)
            dve.tensor_copy(cols[:, :, :], turn[:, :, :])
            dve.drain()

        @block.scalar
        def _(act):
            act.activation(rate[:, :], V["a_log"][0:DN, 0:1], ACT.Exp)
            act.wait_ge(a_ready, 1)
            act.activation(e[:, :], a[:, :], ACT.Abs)
            act.drain()
            act.activation(e[:, :], e[:, :], ACT.Exp, scale=-1.0)
            act.drain()
            act.activation(e[:, :], e[:, :], ACT.Ln, bias=1.0)
            act.drain()
            act.nop().then_inc(log_ready, 1)
            act.wait_ge(g_ready, 1)
            act.activation(t2[:, :], g[:, :], ACT.Exp)
            act.activation(t1[:, :], t1[:, :], ACT.Exp)
            act.activation(beta[:, :], ab[ROW_B:ROW_B + DN, :], ACT.Sigmoid)
            act.drain()
            act.nop().then_inc(parts_ready, 1)
            for h in range(DN):
                act.wait_ge(wide_ready, h + 1)
                act.activation(ends[:, h, :], wide[:, h % 2, DCH - 1:SEQ:DCH], ACT.Exp).then_inc(wide_read, 1)

        @block.tensor
        def _(pe):
            pe.wait_ge(rows_ready, 1)
            for n in range(TILES):
                mm = pe.transpose(turn[:, n, :], rows[:, n * P:(n + 1) * P], C["ident"][:, :])
            mm.then_inc(turned, 1)
            for h in range(DN):
                if h >= 2:
                    pe.wait_ge(wide_read, h - 1)
                pe.matmul(wide[:, h % 2, :], C["sel"][0:DN, h, :], rows[ROW_G:ROW_G + DN, :],
                          start=True, stop=True).then_inc(wide_ready, 1)


def delta_inputs(nc, V, C, W, xn, parts):
    with Phase(nc, "di") as ph:
        z = ph.sb("z", [P, DN, DCONV + SEQ])
        with nc.Block() as block:
            @block.gpsimd
            def _(pool):
                pool.memset(z[:, :, 0:DCONV], 0.0)
        for part, dst in enumerate(parts):
            first = DQ + part * DN
            project(nc, f"dip{part}", SEQ, xn, W["w_in_3"][first:first + DN], DN, z[:, :, DCONV:])
            with Phase(nc, f"dc{part}") as pc, nc.Block() as block:
                conv_ready = pc.sem("conv_ready")

                @block.vector
                def _(dve):
                    for k in range(DCONV):
                        for m in range(DN):
                            tap = 3 * DN * k + part * DN + m
                            weight = V["conv_w"][:, tap:tap + 1]
                            if k == 0:
                                dve.tensor_scalar(dst[:, m, :], z[:, m, 1:1 + SEQ], weight, None, ALU.mult)
                            else:
                                last = dve.scalar_tensor_tensor(out=dst[:, m, :], in0=z[:, m, k + 1:k + 1 + SEQ], scalar=weight,
                                                                in1=dst[:, m, :], op0=ALU.mult, op1=ALU.add)
                                if k == DCONV - 1:
                                    last.then_inc(conv_ready, 1)
                        dve.drain()

                @block.scalar
                def _(act):
                    for m in range(DN):
                        act.wait_ge(conv_ready, m + 1)
                        act.activation(dst[:, m, :], dst[:, m, :], ACT.Silu)
    head_norms(nc, "dl", SEQ, C, parts[0:2], [lambda h: P ** -0.5, lambda h: 1.0], 1.0)


def delta_factors(nc, C, rows, cols, queries, keys, values, qk, kd):
    with Phase(nc, "df") as ph:
        dt, at, inv, invT, tmp = (ph.sb(s, [P, GRP, SEQ]) for s in ("dt", "at", "inv", "invT", "tmp"))
        pa, pb = ph.ps("pa", [P, GRP, BANK]), ph.ps("pb", [P, GRP, BANK])

        def tiles(x):
            return x.rearrange("p (n t) -> p n t", t=P)

        def mask(i):
            return C["fmasks"][:, i, :].unsqueeze(1).to_broadcast([P, TILES, P])

        def tile(n):
            return slice(n * P, (n + 1) * P)

        for group in range(DN // GRP):
            heads = [(i, group * GRP + i) for i in range(GRP)]
            kq = lambda h: queries[:, h, :]
            kk = lambda h: keys[:, h, :]
            kv = lambda h: values[:, h, :]

            with Phase(nc, f"f1{group}") as p, nc.Block() as block:
                wide, args, exps = p.sem("wide"), p.sem("args"), p.sem("exps")

                @block.tensor
                def _(pe):
                    for i, h in heads:
                        pe.matmul(pa[:, i, :], C["sel"][0:DN, h, :], rows[ROW_G:ROW_G + DN, :], start=True, stop=True)
                        pe.matmul(pb[:, i, :], C["sel"][ROW_B:ROW_B + DN, h, :], rows[ROW_B:ROW_B + DN, :],
                                  start=True, stop=True).then_inc(wide, 1)

                @block.vector
                def _(dve):
                    for i, h in heads:
                        dve.wait_ge(wide, i + 1)
                        dve.tensor_tensor(invT[:, i, :], kk(h), pb[:, i, :], ALU.mult)
                        for n in range(TILES):
                            last = dve.tensor_scalar(dt[:, i, tile(n)], pa[:, i, tile(n)], cols[:, n, ROW_G + h:ROW_G + h + 1],
                                                     0.0, ALU.subtract, ALU.min)
                        last.then_inc(args, 1)

                @block.scalar
                def _(act):
                    for i, h in heads:
                        act.wait_ge(args, i + 1)
                        act.activation(inv[:, i, :], pa[:, i, :], ACT.Exp)
                        act.activation(dt[:, i, :], dt[:, i, :], ACT.Exp)

            with Phase(nc, f"f2{group}") as p, nc.Block() as block:
                products_ready = p.sem("products")

                @block.tensor
                def _(pe):
                    for i, h in heads:
                        for n in range(TILES):
                            pe.matmul(pa[:, i, tile(n)], kk(h)[:, tile(n)], invT[:, i, tile(n)], start=True, stop=True)
                            mm = pe.matmul(pb[:, i, tile(n)], kk(h)[:, tile(n)], kq(h)[:, tile(n)], start=True, stop=True)
                        mm.then_inc(products_ready, 1)

                @block.vector
                def _(dve):
                    for i, h in heads:
                        dve.wait_ge(products_ready, i + 1)
                        dve.tensor_tensor(at[:, i, :], pa[:, i, :], dt[:, i, :], ALU.mult)
                        dve.tensor_tensor(qk[:, h, :], pb[:, i, :], dt[:, i, :], ALU.mult)
                        dve.tensor_tensor(kq(h), kq(h), inv[:, i, :], ALU.mult)
                    dve.drain()
                    for i, h in heads:
                        dve.tensor_tensor(tiles(at[:, i, :]), tiles(at[:, i, :]), mask(1), ALU.mult)
                        dve.tensor_tensor(tiles(qk[:, h, :]), tiles(qk[:, h, :]), mask(0), ALU.mult)
                    dve.drain()
                    for i, h in heads:
                        dve.tensor_tensor(tiles(dt[:, i, :]), tiles(at[:, i, :]), mask(2), ALU.mult)
                    dve.drain()
                    for i, h in heads:
                        dve.tensor_tensor(tiles(invT[:, i, :]), C["ident"][:, :].unsqueeze(1).to_broadcast([P, TILES, P]),
                                          tiles(dt[:, i, :]), ALU.subtract)
                    dve.drain()

            with Phase(nc, f"f3{group}") as p, nc.Block() as block:
                turned = p.sem("turned")

                @block.tensor
                def _(pe):
                    for i, h in heads:
                        for n in range(TILES):
                            pe.transpose(pa[:, i, tile(n)], kk(h)[:, tile(n)], C["ident"][:, :])
                            mm = pe.transpose(pb[:, i, tile(n)], kv(h)[:, tile(n)], C["ident"][:, :])
                        mm.then_inc(turned, 1)

                @block.vector
                def _(dve):
                    for i, h in heads:
                        dve.wait_ge(turned, i + 1)
                        for n in range(TILES):
                            col = lambda r: cols[:, n, r + h:r + h + 1]
                            dve.tensor_scalar(kv(h)[:, tile(n)], pb[:, i, tile(n)], col(ROW_B), None, ALU.mult)
                            dve.tensor_scalar(kk(h)[:, tile(n)], pa[:, i, tile(n)], col(ROW_BG), None, ALU.mult)
                            dve.tensor_scalar(kd[:, h, tile(n)], pa[:, i, tile(n)], col(ROW_KD), None, ALU.mult)
                    dve.drain()

            with Phase(nc, f"f4{group}") as p, nc.Block() as block:
                turned = p.sem("turned")

                @block.tensor
                def _(pe):
                    for i, h in heads:
                        for n in range(TILES):
                            mm = pe.transpose(pa[:, i, tile(n)], invT[:, i, tile(n)], C["ident"][:, :])
                        mm.then_inc(turned, 1)

                @block.scalar
                def _(act):
                    for i, h in heads:
                        act.wait_ge(turned, i + 1)
                        act.activation(inv[:, i, :], pa[:, i, :], ACT.Copy)

            for level in range(1, len(DN_LEVELS)):
                with Phase(nc, f"f5{group}{level}") as p, nc.Block() as block:
                    cut_ready, y_ready, y_copied, both_ready = (p.sem(s) for s in ("cut_ready", "y_ready", "y_copied", "both_ready"))

                    @block.vector
                    def _(dve):
                        for i, h in heads:
                            dve.tensor_tensor(tiles(dt[:, i, :]), tiles(at[:, i, :]), mask(2 + level), ALU.mult).then_inc(cut_ready, 1)
                        for i, h in heads:
                            dve.wait_ge(both_ready, i + 1)
                            dve.tensor_tensor(inv[:, i, :], inv[:, i, :], pa[:, i, :], ALU.subtract)
                            dve.tensor_tensor(invT[:, i, :], invT[:, i, :], pb[:, i, :], ALU.subtract)
                        dve.drain()

                    @block.tensor
                    def _(pe):
                        for i, h in heads:
                            pe.wait_ge(cut_ready, i + 1)
                            for n in range(TILES):
                                mm = pe.matmul(pb[:, i, tile(n)], dt[:, i, tile(n)], inv[:, i, tile(n)], start=True, stop=True)
                            mm.then_inc(y_ready, 1)
                        for i, h in heads:
                            pe.wait_ge(y_copied, i + 1)
                            for n in range(TILES):
                                pe.matmul(pa[:, i, tile(n)], invT[:, i, tile(n)], tmp[:, i, tile(n)], start=True, stop=True)
                                mm = pe.matmul(pb[:, i, tile(n)], tmp[:, i, tile(n)], invT[:, i, tile(n)], start=True, stop=True)
                            mm.then_inc(both_ready, 1)

                    @block.scalar
                    def _(act):
                        for i, h in heads:
                            act.wait_ge(y_ready, i + 1)
                            act.activation(tmp[:, i, :], pb[:, i, :], ACT.Copy).then_inc(y_copied, 1)

            with Phase(nc, f"f6{group}") as p, nc.Block() as block:
                done = p.sem("done")

                @block.tensor
                def _(pe):
                    for i, h in heads:
                        for n in range(TILES):
                            pe.matmul(pa[:, i, tile(n)], invT[:, i, tile(n)], kv(h)[:, tile(n)], start=True, stop=True)
                            mm = pe.matmul(pb[:, i, tile(n)], kk(h)[:, tile(n)], invT[:, i, tile(n)], start=True, stop=True)
                        mm.then_inc(done, 1)

                @block.scalar
                def _(act):
                    for i, h in heads:
                        act.wait_ge(done, i + 1)
                        act.activation(kv(h), pa[:, i, :], ACT.Copy)

                @block.vector
                def _(dve):
                    for i, h in heads:
                        dve.wait_ge(done, i + 1)
                        dve.tensor_copy(kk(h), pb[:, i, :])
                    dve.drain()


def delta_scan(nc, queries, keys, values, qk, kd, ends):
    with Phase(nc, "ds") as ph, nc.Block() as block:
        states = [ph.sb(f"state{i}", [P, DN, P]) for i in range(2)]
        vnew = ph.sb("vnew", [P, DN, P])
        ws = ph.ps("ws", [P, DN, P])
        su = ph.ps("su", [P, DN, P])
        out = ph.ps("out", [P, 2, DN, DCH])
        ws_ready, v_ready, su_ready, out_ready, state_ready, out_read = (
            ph.sem(s) for s in ("ws_ready", "v_ready", "su_ready", "out_ready", "state_ready", "out_read"))

        @block.tensor
        def _(pe):
            for n in range(NDC):
                t, lo = n // 2, DCH * (n % 2)
                rows, tok = slice(lo, lo + DCH), slice(n * DCH, (n + 1) * DCH)
                state = states[n % 2]
                pe.wait_ge(state_ready, n + 1)
                for h in range(DN):
                    mm = pe.matmul(ws[rows, h, :], keys[:, h, tok], state[:, h, :], start=True, stop=True)
                mm.then_inc(ws_ready, 1)
                pe.wait_ge(v_ready, n + 1)
                for h in range(DN):
                    mm = pe.matmul(su[:, h, :], kd[rows, h, t * P:(t + 1) * P], vnew[rows, h, :], start=True, stop=True)
                mm.then_inc(su_ready, 1)
                if n >= 2:
                    pe.wait_ge(out_read, n - 1)
                for h in range(DN):
                    pe.matmul(out[:, n % 2, h, :], state[:, h, :], queries[:, h, tok], start=True, stop=False)
                    mm = pe.matmul(out[:, n % 2, h, :], vnew[rows, h, :], qk[rows, h, tok], start=False, stop=True)
                mm.then_inc(out_ready, 1)

        @block.vector
        def _(dve):
            dve.memset(states[0][:, :, :], 0.0).then_inc(state_ready, 1)
            for n in range(NDC):
                t, lo = n // 2, DCH * (n % 2)
                rows = slice(lo, lo + DCH)
                dve.wait_ge(ws_ready, n + 1)
                dve.tensor_tensor(vnew[rows, :, :], values[rows, :, t * P:(t + 1) * P], ws[rows, :, :],
                                  ALU.subtract).then_inc(v_ready, 1)
                dve.wait_ge(su_ready, n + 1)
                if n:
                    dve.wait_ge(out_ready, n)
                for h in range(DN):
                    dve.scalar_tensor_tensor(out=states[1 - n % 2][:, h, :], in0=states[n % 2][:, h, :], scalar=ends[:, h, n:n + 1],
                                             in1=su[:, h, :], op0=ALU.mult, op1=ALU.add)
                dve.drain()
                dve.nop().then_inc(state_ready, 1)

        @block.scalar
        def _(act):
            for n in range(NDC):
                act.wait_ge(out_ready, n + 1)
                act.activation(queries[:, :, n * DCH:(n + 1) * DCH], out[:, n % 2, :, :], ACT.Copy).then_inc(out_read, 1)


def delta_out(nc, V, C, W, xn, o):
    with Phase(nc, "do") as ph:
        z = ph.sb("z", [P, DN, SEQ])
        project(nc, "dop", SEQ, xn, W["w_in_3"][DZ:DAB], DN, z, function=ACT.Silu)
        head_norms(nc, "don", SEQ, C, [o], [lambda h: V["dn_norm_g"][:, 0:1]], 1.0 / P, gate=z[:, :, :])


def third_block(nc, W, V, C, x, mod_flat, out):
    with Phase(nc, "b3") as ph:
        mod = mod_flat[:, :].unsqueeze(2)
        gains = ph.sb("gains", [P, 3, DC])
        xn = Pair(ph, "xn", [P, DC, SEQ])
        with nc.Block() as block:
            @block.vector
            def _(dve):
                dve.tensor_tensor(mod[:, :, 0], mod[:, :, 0], V["b_ada"], ALU.add)
                dve.drain()
                for i, g in enumerate(("norm1_g", "norm2_g", "norm3_g")):
                    dve.scalar_tensor_tensor(out=gains[:, i, :], in0=mod[:, (3 * i + 1) * DC:(3 * i + 2) * DC, 0], scalar=1.0,
                                             in1=V[g], op0=ALU.add, op1=ALU.mult)
                    if i != 1:
                        gate = mod[:, (3 * i + 2) * DC:(3 * i + 3) * DC, 0]
                        dve.tensor_scalar(gate, gate, 0.5, None, ALU.mult)
                dve.drain()

        def shift(i):
            return mod[:, 3 * i * DC:(3 * i + 1) * DC, 0]

        def gate(i):
            return mod[:, (3 * i + 2) * DC:(3 * i + 3) * DC, :]

        def swiglu(i, w_in, w_out):
            rms_norm(nc, f"m{i}", SEQ, C["ones"], x, xn, gains[:, i, :], shift=shift(i))
            with Phase(nc, f"s{i}") as pf:
                hidden = Pair(pf, "hidden", [P, FC, SEQ])
                gated_up(nc, f"s{i}u", SEQ, xn, w_in[0:FC], w_in[FC:2 * FC], FC, hidden)
                project(nc, f"s{i}d", SEQ, hidden, w_out, DC, x, residual=True, column=gate(i))

        swiglu(0, W["ffn1_w_in_3"], W["ffn1_w_out_3"])
        rms_norm(nc, "m1", SEQ, C["ones"], x, xn, gains[:, 1, :], shift=shift(1))
        with Phase(nc, "mx3") as pm:
            o_a, o_b = pm.sb("o_a", [P, DC, SEQ]), pm.sb("o_b", [P, DC, SEQ])
            spatial_gating(nc, V, C, W, xn, o_a)
            with Phase(nc, "dn") as pd:
                C = C | load(nc, pd, "dc", {k: W[k] for k in ("fmasks", "sel", "pick")})
                queries = o_b
                keys, values = pd.sb("keys", [P, DN, SEQ]), pd.sb("values", [P, DN, SEQ])
                rows, cols = pd.sb("rows", [P, SEQ]), pd.sb("cols", [P, TILES, P])
                ends = pd.sb("ends", [P, DN, NDC])
                with Phase(nc, "ab") as pa:
                    ab = pa.sb("ab", [P, 1, SEQ])
                    project(nc, "abp", SEQ, xn, W["w_in_3"][DAB:G3], 1, ab)
                    delta_rows(nc, V, C, W, ab[:, 0, :], rows, cols, ends)
                delta_inputs(nc, V, C, W, xn, [queries, keys, values])
                with Phase(nc, "dk") as pk:
                    qk, kd = pk.sb("qk", [P, DN, SEQ]), pk.sb("kd", [P, DN, SEQ])
                    delta_factors(nc, C, rows, cols, queries, keys, values, qk, kd)
                    delta_scan(nc, queries, keys, values, qk, kd, ends)
                delta_out(nc, V, C, W, xn, o_b)
            gates = pm.sb("gates", [P, 2 * DC, SEQ])
            project(nc, "g3p", SEQ, xn, W["w_in_3"][G3:END3], 2 * DC, gates, function=ACT.Sigmoid)
            with Phase(nc, "gt") as pg:
                pairs = [Pair(pg, f"{k}_pair", [P, DC, SEQ]) for k in ("oa", "ob")]
                split(nc, "soa", o_a, pairs[0])
                split(nc, "sob", o_b, pairs[1])
                merge(nc, "mg3", SEQ, pairs[0], W["w_branch"][0], gates[:, 0:DC, :], pairs[1], W["w_branch"][1],
                      gates[:, DC:2 * DC, :], DC, xn)
            project(nc, "wo3", SEQ, xn, W["w_out_3"], DC, x, residual=True, column=gate(1))
        swiglu(2, W["ffn2_w_in_3"], W["ffn2_w_out_3"])
        final = ph.sb("final", [P, DC, SEQ])
        rms_norm(nc, "fin", SEQ, C["ones"], x, None, V["final_g"], plain=final)
        with nc.Block() as block:
            stored = ph.sem("stored")

            @block.sync
            def _(sp):
                sp.dma_start(out, final[:, :, :]).then_inc(stored, 16)
                sp.wait_ge(stored, 16)
def tiles_of(w):
    k, n = w.shape
    return w.reshape(k // P, P, n // P, P).transpose(2, 1, 0, 3).reshape(n // P, P, k)


def columns(v):
    return v.reshape(-1, P).T


def first_constants():
    c = {}
    i = np.arange(P)
    c["ident"] = np.eye(P, dtype=np.float32)
    c["ones"] = np.ones((P, P), np.float32)
    c["ones64"] = (i[:, None] // HD == i[None, :] // HD).astype(np.float32)
    swap = np.zeros((P, P), np.float32)
    swap[i[1::2], i[0::2]] = -1.0
    swap[i[0::2], i[1::2]] = 1.0
    c["swap"] = swap
    width, theta, axis = 64, 10000.0, HD // 2
    rows = SEQ // width
    row = np.concatenate([np.zeros(META), np.repeat(np.arange(rows), width)]).astype(np.float32)
    col = np.concatenate([np.zeros(META), np.tile(np.arange(width), rows)]).astype(np.float32)
    inv = (np.float32(theta) ** (-np.arange(0, axis, 2, dtype=np.float32) / np.float32(axis))).astype(np.float32)
    angle = np.concatenate([row[:, None] * inv, col[:, None] * inv], axis=-1)
    pair = (i % HD) // 2
    c["cos"] = np.cos(angle).astype(np.float32)[:, pair].T
    c["sin"] = np.sin(angle).astype(np.float32)[:, pair].T
    s, t = i[:, None], i[None, :]
    masks = np.zeros((16, P, P), np.uint32)
    masks[0] = s == t
    for n, w in enumerate((64, 32, 16, 8, 4, 2, 1)):
        late = (s // (2 * w) == t // (2 * w)) & (s // w % 2 == 0) & (t // w % 2 == 1)
        masks[1 + n], masks[9 + n] = late, late.T
    c["masks"] = masks.transpose(1, 0, 2)
    return {k: np.ascontiguousarray(v) for k, v in c.items()}


def first_weights(a):
    w = a["w_in"][0]
    cut_at = np.cumsum([512] * 6 + [128, 128])
    k0, k1 = w[:, cut_at[5]:cut_at[5] + HD], w[:, cut_at[5] + HD:cut_at[6]]
    w_in = np.concatenate([w[:, :cut_at[5]], k0, k0, k1, k1, w[:, cut_at[6]:]], axis=1)
    weights = {"w_in": tiles_of(w_in)}
    for n in ("ffn1_w_gate", "ffn1_w_up", "ffn1_w_down", "ffn2_w_gate", "ffn2_w_up", "ffn2_w_down", "w_up_a", "w_up_b", "w_out"):
        weights[n] = tiles_of(a[n][0])
    weights["meta"] = np.ascontiguousarray(a["meta_tokens"].T.reshape(DC, P, META).transpose(1, 0, 2))
    vectors = {n: columns(a[n]) for n in ("ffn1_norm", "mix_norm", "ffn2_norm", "hg_out_norm")}
    vectors["lb"] = np.concatenate([columns(a["hg_lb_fwd"]), columns(a["hg_lb_bwd"])], axis=1)
    for n in ("q_norm", "k_norm"):
        vectors[n] = np.concatenate([a[n], a[n]], axis=1).T
    return weights, vectors


def second_constants():
    c = {}
    i = np.arange(P)
    c["iota"] = np.broadcast_to(i.astype(np.float32), (P, P))
    c["before"] = (i[None, :] < i[:, None]).astype(np.float32)
    t = np.arange(SEQ)
    count = np.stack([np.minimum(t + 1, w) for w in WINDOWS]).astype(np.float32)
    c["inv_count"] = np.repeat((np.float32(1.0) / count).reshape(2, 2, SEQ), 64, axis=1).transpose(1, 0, 2)
    return {k: np.ascontiguousarray(v) for k, v in c.items()}


def second_weights(a):
    weights = {n: tiles_of(a[n][0]) for n in ("w_in_2", "w_out_2")}
    weights["peer_wq"] = tiles_of(a["peer_wq_2"][0])
    u = a["peer_u_2"][0].reshape(P, NKEYS, DC, P)
    weights["peer_u"] = u.transpose(1, 3, 2, 0).reshape(NKEYS, P, D)
    weights["peer_v"] = a["peer_v_2"][0].reshape(P, NKEYS, D).transpose(1, 0, 2)
    weights["peer_keys"] = a["peer_keys_2"][0].reshape(2 * PK_HEADS, NKEYS, P).transpose(2, 0, 1)
    pool = np.zeros((P, 2, P), np.float32)
    for g in range(len(WINDOWS)):
        lo = 64 * (g % 2)
        pool[lo:lo + 64, g // 2, lo:lo + 64] = a["pool_w_2"][0, g]
    weights["pool_w"] = pool
    vectors = {n: columns(a[n + "_2"]) for n in ("conv_a_b", "norm_a_g", "norm_a_b", "pool_scale", "ln1_g", "ln1_b",
                                                 "ln2_g", "ln2_b", "conv_a_w", "conv_c_w")}
    return weights, vectors


def third_constants():
    c = {}
    i = np.arange(P)
    e, t = i[:, None], i[None, :]
    same = e // DCH == t // DCH
    masks = [same & (e <= t), same & (e < t)]
    for w in DN_LEVELS:
        masks.append((e // (2 * w) == t // (2 * w)) & (e // w % 2 == 0) & (t // w % 2 == 1))
    c["fmasks"] = np.stack(masks, axis=1).astype(np.float32)
    c["upto"] = (e <= t).astype(np.float32)
    sel = np.zeros((P, DN, P), np.float32)
    for h in range(DN):
        sel[h, h, :] = 1.0
        sel[ROW_B + h, h, :] = 1.0
    c["sel"] = sel
    c["pick"] = np.broadcast_to(np.eye(DN, dtype=np.float32), (P, DN, DN))
    return {k: np.ascontiguousarray(v) for k, v in c.items()}


def third_weights(a):
    weights = {n: tiles_of(a[n][0]) for n in ("ffn1_w_in_3", "ffn1_w_out_3", "ffn2_w_in_3", "ffn2_w_out_3", "w_out_3")}
    weights["w_ada"] = tiles_of(a["w_ada_3"][0])
    weights["w_branch"] = np.stack([tiles_of(a["w_branch_3"][0, i]) for i in range(2)])
    w = a["w_in_3"][0]
    small = 6 * D
    ab = np.zeros((D, P), w.dtype)
    ab[:, 0:DN], ab[:, ROW_B:ROW_B + DN] = w[:, small:small + DN], w[:, small + DN:small + 2 * DN]
    weights["w_in_3"] = tiles_of(np.concatenate([w[:, :small], ab, w[:, small + 2 * DN:]], axis=1))
    weights["gm_w_s"] = a["gm_w_s_3"][0].transpose(2, 0, 1)
    weights["gm_b_s"] = a["gm_b_s_3"].reshape(1, DC * P)
    vectors = {n: columns(a[n + "_3"]) for n in ("norm1_g", "norm2_g", "norm3_g", "final_g", "gm_ln_g", "gm_ln_b", "dn_norm_g",
                                                 "b_ada", "c", "conv_w")}
    for n in ("a_log", "dt_bias"):
        vectors[n] = np.zeros((P, 1), np.float32)
        vectors[n][0:DN, 0] = a[n + "_3"][0]
    return weights, vectors


def whole_program(nc, tensors, vector_columns, out):
    gates = nc.dram_tensor("expert_gates", [NKEYS, P, SEQ], F32).ap()
    with Phase(nc, "all") as ph:
        there = load(nc, ph, "first_load", {k: tensors[k] for k in ("vectors", "ident", "ones")})
        vectors = {k: there["vectors"][:, a:b] for k, (a, b) in vector_columns.items()}
        hidden = ph.sb("hidden", [P, DC, L])
        mod = ph.sb("mod", [P, MODS * DC])
        first_block(nc, tensors, vectors, there, tensors["x"], hidden)
        x = hidden[:, :, META:]
        second_block(nc, tensors, vectors, there, x, gates, mod)
        third_block(nc, tensors, vectors, there, x, mod, out)


def kernel(**inputs):
    import concourse.bacc as _bacc
    from concourse.bass_utils import run_bass_kernel_spmd as _run

    a = {k: np.asarray(v) for k, v in inputs.items()}
    tensors, vectors = {}, {}
    for weights, small in (first_weights(a), second_weights(a), third_weights(a)):
        tensors.update(weights)
        vectors.update(small)
    for constants in (first_constants(), second_constants(), third_constants()):
        tensors.update(constants)
    tensors["x"] = a["x"][0].T.reshape(DC, P, SEQ).transpose(1, 0, 2)
    ends = np.cumsum([v.shape[1] for v in vectors.values()])
    vector_columns = {k: (int(e) - v.shape[1], int(e)) for (k, v), e in zip(vectors.items(), ends)}
    tensors["vectors"] = np.concatenate(list(vectors.values()), axis=1)

    nc = _bacc.Bacc("TRN2", target_bir_lowering=False, num_devices=1)
    arrays, drams = {}, {}
    for name, t in tensors.items():
        arrays[f"in_{name}"] = np.ascontiguousarray(t)
        drams[name] = nc.dram_tensor(f"in_{name}", t.shape, mybir.dt.from_np(t.dtype), kind="ExternalInput").ap()
    out = nc.dram_tensor("out", [P, DC, SEQ], F32, kind="ExternalOutput").ap()
    whole_program(nc, drams, vector_columns, out)
    r = _run(nc, [arrays], core_ids=[0])
    got = r.results[0]["out"]
    return np.ascontiguousarray(got.transpose(1, 0, 2).reshape(D, SEQ).T)[None]
```
